# Optimizing a Trainium2 kernel written in Bass

```python
import jax, jax.numpy as jnp
from jax import lax
import numpy as np

D_MODEL = 2048
BATCH = 1
SEQ = 256
DEPTH = 1

MIX_WIDTH = D_MODEL
RWKV_WIDTH = MIX_WIDTH // 2
CONV_WIDTH = MIX_WIDTH - RWKV_WIDTH
HEAD_DIM = 64
RWKV_HEADS = RWKV_WIDTH // HEAD_DIM
CONV_GROUPS = CONV_WIDTH // HEAD_DIM
CONV_K = 3
DECAY_LORA = max(32, int(round(1.8 * RWKV_WIDTH ** 0.5 / 32)) * 32)
AAA_LORA = max(32, int(round(1.8 * RWKV_WIDTH ** 0.5 / 32)) * 32)
GATE_LORA = max(32, int(round(0.6 * RWKV_WIDTH ** 0.8 / 32)) * 32)
RWKV_COLS = 3 * RWKV_WIDTH + DECAY_LORA + AAA_LORA + GATE_LORA
CONV_COLS = 3 * CONV_WIDTH
IN_COLS = RWKV_COLS + CONV_COLS
NORM_EPS = 1e-6
GN_EPS = 64e-5
PEER_HEADS = 8
N_KEYS = 128
N_EXPERTS = N_KEYS * N_KEYS
PEER_QUERY_DIM = 256
PEER_HALF = PEER_QUERY_DIM // 2
PEER_TOPK = 16
PEER_TOKEN_BLOCK = 128

kernel_name = 'hybrid_rwkv7_shortconv_peer_layer'

def rms_norm(x, w):
    xf = x.astype(jnp.float32)
    y = xf * lax.rsqrt(jnp.mean(xf * xf, axis=-1, keepdims=True) + NORM_EPS)
    return (y * w.astype(jnp.float32)).astype(x.dtype)

def wkv7_scan(r, decay, k, v, a_vec, b_vec):
    B, S, H, N = r.shape

    def step(state, inp):
        r_t, w_t, k_t, v_t, a_t, b_t = inp
        sa = jnp.einsum('bhij,bhj->bhi', state, a_t)
        state = (state * w_t[:, :, None, :] + sa[..., None] * b_t[:, :, None, :]
                 + v_t[..., None] * k_t[:, :, None, :])
        y_t = jnp.einsum('bhij,bhj->bhi', state, r_t)
        return state, y_t

    xs = tuple(jnp.swapaxes(t, 0, 1) for t in (r, decay, k, v, a_vec, b_vec))
    init = jnp.zeros((B, H, N, N), jnp.float32)
    _, ys = lax.scan(step, init, xs)
    return jnp.swapaxes(ys, 0, 1)

def rwkv7_group(z_r, z_k, z_v, z_w, z_a, z_g, w0, w_up, a0, a_up, g_up, k_k, k_a, r_k, ln_x_w, ln_x_b):
    B, S, C = z_r.shape
    f32 = jnp.float32
    heads = lambda t: t.reshape(B, S, RWKV_HEADS, HEAD_DIM)
    w = -jax.nn.softplus(-(w0 + jnp.tanh(z_w) @ w_up)) - 0.5
    decay = jnp.exp(-jnp.exp(w.astype(f32)))
    a = jax.nn.sigmoid(a0 + z_a @ a_up)
    g = jax.nn.sigmoid(z_g) @ g_up
    kk = heads(z_k * k_k).astype(f32)
    kk = kk * lax.rsqrt(jnp.sum(kk * kk, axis=-1, keepdims=True) + 1e-12)
    k = z_k * (1.0 + (a - 1.0) * k_a)
    r_h = heads(z_r).astype(f32)
    k_h = heads(k).astype(f32)
    v_h = heads(z_v).astype(f32)
    a_h = heads(a).astype(f32)
    y = wkv7_scan(r_h, heads(decay), k_h, v_h, -kk, kk * a_h)
    mean = jnp.mean(y, axis=-1, keepdims=True)
    var = jnp.mean(jnp.square(y - mean), axis=-1, keepdims=True)
    gn_w = ln_x_w.reshape(RWKV_HEADS, HEAD_DIM).astype(f32)
    gn_b = ln_x_b.reshape(RWKV_HEADS, HEAD_DIM).astype(f32)
    y = (y - mean) * lax.rsqrt(var + GN_EPS) * gn_w + gn_b
    bonus = jnp.sum(r_h * k_h * r_k.astype(f32), axis=-1, keepdims=True) * v_h
    return (y + bonus).reshape(B, S, C).astype(z_r.dtype) * g

def short_conv_group(z_b, z_c, z_x, conv_w, conv_norm_w):
    B, S, C = z_x.shape
    u = z_c * z_x
    u_pad = jnp.pad(u, ((0, 0), (CONV_K - 1, 0), (0, 0)))
    y = conv_w[0] * u_pad[:, 0:S]
    for j in range(1, CONV_K):
        y = y + conv_w[j] * u_pad[:, j:j + S]
    y = (z_b * y).reshape(B, S, CONV_GROUPS, HEAD_DIM)
    y = rms_norm(y, conv_norm_w.reshape(CONV_GROUPS, HEAD_DIM))
    return y.reshape(B, S, C)

def peer_ffn(h, w_q, sub_keys_1, sub_keys_2, expert_u, expert_v):
    B, S, D = h.shape
    f32 = jnp.float32
    q = (h @ w_q).reshape(B, S, PEER_HEADS, 2, PEER_HALF).astype(f32)
    s1 = jnp.einsum('bshd,hnd->bshn', q[..., 0, :], sub_keys_1.astype(f32))
    s2 = jnp.einsum('bshd,hnd->bshn', q[..., 1, :], sub_keys_2.astype(f32))
    v1, i1 = lax.top_k(s1, PEER_TOPK)
    v2, i2 = lax.top_k(s2, PEER_TOPK)
    cand = (v1[..., :, None] + v2[..., None, :]).reshape(B, S, PEER_HEADS, PEER_TOPK * PEER_TOPK)
    cidx = (i1[..., :, None] * N_KEYS + i2[..., None, :]).reshape(B, S, PEER_HEADS, PEER_TOPK * PEER_TOPK)
    top, pos = lax.top_k(cand, PEER_TOPK)
    eidx = jnp.take_along_axis(cidx, pos, axis=-1)
    gate = jax.nn.softmax(top, axis=-1)
    n_blk = (B * S) // PEER_TOKEN_BLOCK
    KT = PEER_HEADS * PEER_TOPK
    hb = h.reshape(n_blk, PEER_TOKEN_BLOCK, D)
    ib = eidx.reshape(n_blk, PEER_TOKEN_BLOCK, KT)
    gb = gate.reshape(n_blk, PEER_TOKEN_BLOCK, KT).astype(h.dtype)

    def block(args):
        h_t, idx, g = args
        u = jnp.take(expert_u, idx, axis=0)
        act = jax.nn.gelu(jnp.einsum('td,tkd->tk', h_t, u), approximate=False)
        vv = jnp.take(expert_v, idx, axis=0)
        return jnp.einsum('tk,tkd->td', g * act, vv)

    out = lax.map(block, (hb, ib, gb))
    return out.reshape(B, S, D)

def hybrid_layer(x, c, ada_w, ada_b, pre_mix_w, post_mix_w, w_in, rwkv_mix, w0, w_up, a0, a_up, g_up,
                 k_k, k_a, r_k, ln_x_w, ln_x_b, conv_w, conv_norm_w, w_out, pre_ffn_w, post_ffn_w,
                 w_q, sub_keys_1, sub_keys_2, expert_u, expert_v):
    mod = jax.nn.silu(c) @ ada_w + ada_b
    shift1, scale1, gate1, shift2, scale2, gate2 = [m[:, None, :] for m in jnp.split(mod, 6, axis=-1)]
    h = rms_norm(x, pre_mix_w) * (1.0 + scale1) + shift1
    z = h @ w_in
    z_rw, z_cv = z[..., :RWKV_COLS], z[..., RWKV_COLS:]
    prev = jnp.pad(z_rw, ((0, 0), (1, 0), (0, 0)))[:, :-1]
    z_rw = z_rw + (prev - z_rw) * rwkv_mix
    C = RWKV_WIDTH
    cuts = [C, 2 * C, 3 * C, 3 * C + DECAY_LORA, 3 * C + DECAY_LORA + AAA_LORA]
    z_r, z_k, z_v, z_w, z_a, z_g = jnp.split(z_rw, cuts, axis=-1)
    z_b, z_c, z_x = jnp.split(z_cv, 3, axis=-1)
    y_rwkv = rwkv7_group(z_r, z_k, z_v, z_w, z_a, z_g, w0, w_up, a0, a_up, g_up, k_k, k_a, r_k, ln_x_w, ln_x_b)
    y_conv = short_conv_group(z_b, z_c, z_x, conv_w, conv_norm_w)
    mix = jnp.concatenate([y_rwkv, y_conv], axis=-1) @ w_out
    x = x + gate1 * rms_norm(mix, post_mix_w)
    h = rms_norm(x, pre_ffn_w) * (1.0 + scale2) + shift2
    ff = peer_ffn(h, w_q, sub_keys_1, sub_keys_2, expert_u, expert_v)
    return x + gate2 * rms_norm(ff, post_ffn_w)

def setup_inputs(seed: int = 0) -> dict:
    key = jax.random.key(seed)
    ks = jax.random.split(key, 32)
    L, D = DEPTH, D_MODEL
    nrm = lambda k, shape, std: jax.random.normal(k, shape, jnp.float32) * std
    return {
        'x': nrm(ks[0], (BATCH, SEQ, D), 1.0),
        'c': nrm(ks[1], (BATCH, D), 1.0),
        'ada_w': nrm(ks[2], (L, D, 6 * D), 0.5 * D ** -0.5),
        'ada_b': nrm(ks[3], (L, 6 * D), 0.01),
        'pre_mix_w': 1.0 + nrm(ks[4], (L, D), 0.02),
        'post_mix_w': 1.0 + nrm(ks[5], (L, D), 0.02),
        'w_in': nrm(ks[6], (L, D, IN_COLS), D ** -0.5),
        'rwkv_mix': jax.random.uniform(ks[7], (L, RWKV_COLS), jnp.float32),
        'w0': -1.0 + nrm(ks[8], (L, RWKV_WIDTH), 0.5),
        'w_up': nrm(ks[9], (L, DECAY_LORA, RWKV_WIDTH), 0.1),
        'a0': nrm(ks[10], (L, RWKV_WIDTH), 0.1),
        'a_up': nrm(ks[11], (L, AAA_LORA, RWKV_WIDTH), 0.5 * AAA_LORA ** -0.5),
        'g_up': nrm(ks[12], (L, GATE_LORA, RWKV_WIDTH), GATE_LORA ** -0.5),
        'k_k': 0.85 + nrm(ks[13], (L, RWKV_WIDTH), 0.05),
        'k_a': 1.0 + nrm(ks[14], (L, RWKV_WIDTH), 0.05),
        'r_k': nrm(ks[15], (L, RWKV_HEADS, HEAD_DIM), 0.1),
        'ln_x_w': 1.0 + nrm(ks[16], (L, RWKV_WIDTH), 0.02),
        'ln_x_b': nrm(ks[17], (L, RWKV_WIDTH), 0.01),
        'conv_w': nrm(ks[18], (L, CONV_K, CONV_WIDTH), CONV_K ** -0.5),
        'conv_norm_w': 1.0 + nrm(ks[19], (L, CONV_WIDTH), 0.02),
        'w_out': nrm(ks[20], (L, MIX_WIDTH, D), MIX_WIDTH ** -0.5),
        'pre_ffn_w': 1.0 + nrm(ks[21], (L, D), 0.02),
        'post_ffn_w': 1.0 + nrm(ks[22], (L, D), 0.02),
        'w_q': nrm(ks[23], (L, D, PEER_HEADS * PEER_QUERY_DIM), D ** -0.5),
        'sub_keys_1': nrm(ks[24], (L, PEER_HEADS, N_KEYS, PEER_HALF), PEER_HALF ** -0.5),
        'sub_keys_2': nrm(ks[25], (L, PEER_HEADS, N_KEYS, PEER_HALF), PEER_HALF ** -0.5),
        'expert_u': nrm(ks[26], (L, N_EXPERTS, D), D ** -0.5),
        'expert_v': nrm(ks[27], (L, N_EXPERTS, D), (PEER_HEADS * PEER_TOPK) ** -0.5),
    }

def reference(x, c, ada_w, ada_b, pre_mix_w, post_mix_w, w_in, rwkv_mix, w0, w_up, a0, a_up, g_up,
              k_k, k_a, r_k, ln_x_w, ln_x_b, conv_w, conv_norm_w, w_out, pre_ffn_w, post_ffn_w,
              w_q, sub_keys_1, sub_keys_2, expert_u, expert_v):
    layer_params = (ada_w, ada_b, pre_mix_w, post_mix_w, w_in, rwkv_mix, w0, w_up, a0, a_up, g_up,
                    k_k, k_a, r_k, ln_x_w, ln_x_b, conv_w, conv_norm_w, w_out, pre_ffn_w, post_ffn_w,
                    w_q, sub_keys_1, sub_keys_2, expert_u, expert_v)
    for layer in range(DEPTH):
        x = hybrid_layer(x, c, *[p[layer] for p in layer_params])
    return x


_drawn_inputs = setup_inputs


def setup_inputs(seed=0):
    import zlib

    import numpy as np

    out = dict(_drawn_inputs(seed))
    spreads = {}
    factors = {'k_k': 2.943, 'ln_x_w': 3.373, 'ln_x_b': 5.758, 'post_ffn_w': 8.0}
    for name, (base, spread) in spreads.items():
        noise = np.random.default_rng([zlib.crc32(name.encode()), seed]).standard_normal(out[name].shape)
        drawn = base * np.exp(spread * noise) if base else spread * noise
        out[name] = __import__('jax').numpy.asarray(drawn.astype(out[name].dtype))
    for name, factor in factors.items():
        out[name] = (out[name] * factor).astype(out[name].dtype)
    return out
```

```python
from contextlib import ExitStack
import math

import numpy as np
import concourse.bass as bass
from concourse import mybir

ALU = mybir.AluOpType
ACT = mybir.ActivationFunctionType
AX = mybir.AxisListType
F32 = mybir.dt.float32
I32 = mybir.dt.int32
U32 = mybir.dt.uint32

P = 128
D = 2048
T = 256
TB = T // P
KC = D // P
VECS = 6
VEC_ORDER = (1, 0, 2, 3, 4, 5)
SL = 2048
RING = 8
GROUP = 512
KT = 4
TILES = KC // KT
ZS = T + 1
Z_R, Z_K, Z_V, Z_B, Z_C, Z_X, Z_L = 0, 8, 16, 24, 32, 40, 48
NZ = 51
PAIRS = 8
PC = 16
MIX_R, MIX_K, MIX_V, W0, A0, K_K, K_A, R_K, LN_W, LN_B, CW0, CW1, CW2, CN = range(14)
CH = 64
NCH = T // CH
LEVELS = 6
DECAY = math.exp(-0.5)
HEADS, TOPK, NKEYS = 8, 16, 128
KTOP = HEADS * TOPK
C_PMW, C_PFW, C_AB, C_C, C_ML, C_PP = 0, 16, 32, 96, 112, 116
NCOL = C_PP + PAIRS * PC


ACT_K = [k for k in range(KC) if k // 2 % 2 == 0]
VEC_K = [k for k in range(KC) if k // 2 % 2 == 1]
ACT_H = " ".join(f"h{k}" for k in ACT_K)
VEC_H = " ".join(f"h{k}" for k in VEC_K)


class Steps:

    def __init__(self, sem, names, lead=False):
        self.sem, self.names, self.per = sem, names.split(), len(names.split())
        assert len(set(self.names)) == self.per
        self.lead = self.per if lead else 0
        self.next = 0

    def at(self, name, i=0):
        return i * self.per + (self.lead + self.names.index(name) + 1)

    def done(self, ins, name):
        assert self.names[self.next % self.per] == name, (self.names[self.next % self.per], name)
        self.next += 1
        return ins.then_inc(self.sem, 1)


def build_layer(nc, x, cols, ada, ada_b, post_mix_w, post_ffn_w, w_lora, w_in, w_tail, lora_up, keys,
                expert_u, expert_v, out):
    with ExitStack() as ctx:
        arena_size = 53200
        arena = ctx.enter_context(nc.sbuf_tensor("arena", [P, arena_size], F32))
        ps = ctx.enter_context(nc.psum_tensor("ps", [P, 4096], F32))
        top = [0]

        def take(n):
            a = top[0]
            top[0] += n
            assert top[0] <= arena_size, top[0]
            return a

        def view(a, *shape):
            n = int(np.prod(shape))
            v = arena[:, a:a + n]
            if len(shape) == 2:
                v = v.rearrange("p (a b) -> p a b", a=shape[0])
            if len(shape) == 3:
                v = v.rearrange("p (a b c) -> p a b c", a=shape[0], b=shape[1])
            return v

        def new(*shape):
            return view(take(int(np.prod(shape))), *shape)

        def sem(name):
            return ctx.enter_context(nc.semaphore(name))

        def bank(b, lo=0, hi=512):
            return ps[:, b * 512 + lo:b * 512 + hi]

        def bank3(b, n):
            return bank(b).rearrange("p (a b) -> p a b", a=n)

        ring = new(RING, SL)
        z_at = take(NZ * ZS)
        zT = view(z_at, NZ, ZS)
        xn = view(z_at, TB, D)
        mixrow = view(z_at + Z_K * ZS, TB, D)
        qT = view(z_at + Z_B * ZS, KC, T)
        scores = [view(z_at, KC, NKEYS), view(z_at + Z_K * ZS, KC, NKEYS)]
        xs = new(TB, D)
        gw1 = new(D)
        colp = new(NCOL)
        ident, ones, bones, bmean = new(P), new(P), new(P), new(P)
        lmask = new(LEVELS, P)
        m0T, strict, incl = new(P), new(P), new(CH)
        cst = new(4)
        silu_c, tmp16 = new(KC), new(KC)
        modc = new(4, KC)
        ss, lns, rstd = new(8), new(8), new(8)
        g_at = take(0)
        hT = new(KC, T)
        acc = new(5, D)
        top[0] = 4 * SL
        tz, sgz = new(T), new(2, T)
        lw = new(4, P)
        pp, npp = new(PC), new(PC)
        dz = new(3, T)
        dr, dk, dv = (dz[:, n, :] for n in range(3))
        zr, zk, zv = (new(T) for _ in range(3))
        ewa = new(2, T)
        reset = new(T)
        cs, cse, Wt, Wi, We = (new(T) for _ in range(5))
        kkr, kk2, rn, kk, kka, t1, kf, rt, rk, gT = (new(T) for _ in range(10))
        Gt, y = new(T), new(T)
        assert top[0] <= RING * SL
        top[0] = g_at
        yc, bon, rsy = new(T), new(T), new(T)
        u = new(T + 2)
        cy, csq, crs = new(T), new(T), new(T)
        ab, bb, kb, vb = (new(NCH, P) for _ in range(4))
        LT = new(NCH, P)
        LTm = [new(NCH, P) for _ in range(2)]
        X, XT, T1 = new(NCH, P), new(NCH, P), new(NCH, P)
        AKT = new(NCH, P)
        RBK = new(NCH, 2, CH)
        vtok, btok, ktok = new(NCH, P), new(NCH, P), new(NCH, P)
        UA = new(NCH, 2, P)
        QPb = new(NCH, 2, P)
        ET, Fw, St = new(2, P), new(3, P), new(2, P)
        mix_top = top[0]
        top[0] = g_at
        h2T = new(KC, T)
        gw2 = new(D)
        acc5 = new(D)
        v16, i16 = new(KC, TOPK), new(KC, TOPK)
        iu = new(KC, TOPK)
        repl = acc5
        cand = new(HEADS, TOPK * TOPK)
        eq = acc5.rearrange("p (a b c) -> p a b c", a=HEADS, b=TOPK)
        topv, pos, hi_u, lo_u, hi_f, lo_f, ei, ej = (new(HEADS, TOPK) for _ in range(8))
        iota16 = new(TOPK)
        gate = new(TB, KTOP)
        gsum, grec = new(HEADS), new(HEADS)
        idx = new(4 * KTOP + 2)
        stage = new(8, 2)
        actv, wv = new(TB, KTOP), new(TB, KTOP)
        ff = cand.rearrange("p a b -> p (a b)")
        junk = acc5
        i32 = lambda v: v.bitcast(I32)
        u32 = lambda v: v.bitcast(U32)

        land = [sem(f"slot_landed{s}") for s in range(RING)]
        w_used, ada_used = sem("weight_tile_used"), sem("ada_tile_used")
        x_in, cols_in, gw1_in, gw2_in = sem("x_in"), sem("cols_in"), sem("gw1_in"), sem("gw2_in")
        keys_in, lw_in, abb_in = sem("keys_in"), sem("lora_up_in"), sem("ada_b_rows_in")
        consts = sem("constants_ready")
        z_out = sem("z_evacuated")
        stored = sem("out_stored")
        v0 = Steps(sem("vec_prologue"), "den rec silu s1a s1b s1 b1 xn0 xn1 " + VEC_H)
        a0 = Steps(sem("act_prologue"), "expc sq0 sq1 ln exp " + ACT_H)
        p0 = Steps(sem("pe_prologue"), "scale1 shift1 " + " ".join(f"tr{k}" for k in range(0, KC, 2)))
        p1 = Steps(sem("pe_modulation"), "shift2 scale2 gate1")
        v1 = Steps(sem("vec_modulation"), "b2 s2a s2b s2 g1 gw1 dl0 dl1 dl2 ml0 ml1 ml2 eg1 sg reset")
        a1 = Steps(sem("act_modulation"), "tanh za eg")
        pv = Steps(sem("vec_mixing"), "pp npp zr zk zv kkr den sig cs cse kk kka t1 kf "
                   "ab0 ab1 bb0 bb1 rk X0a X0 akt rbk "
                   + " ".join(f"X{m} XT{m}" for m in range(1, LEVELS - 1)) + " XT5 "
                   "qp2 et g s2 s3 c0 c1 c2 yc bon yn aff addb yg cout", lead=True)
        pa = Steps(sem("act_mixing"), "ew ea gT vb0 vb1 Wt Wi We lnk rn lt vtok atok btok ktok "
                   + " ".join(f"T1_{m}" for m in range(1, LEVELS)) + " u1 qp1 f0 f1 f2 y lny rsy lnc rsc", lead=True)
        pp_ = Steps(sem("pe_mixing"), "wa g kks lt l akt rbk vtr atr btr ktr u1 bon "
                    + " ".join(f"T1_{m} X{m}" for m in range(1, LEVELS)) +
                    " qp g_ et f s2 s3 y mean var conv", lead=True)
        pg = Steps(sem("pool_mixing"), "dr dk dv kk2 kb0 kb1 rt XT0a XT0 "
                   + " ".join(f"m{m}" for m in range(1, LEVELS)) + " u cyb csq sqy", lead=True)
        zeroed = sem("blocks_zeroed")
        m_out = sem("mix_evacuated")
        a2 = Steps(sem("act_output"), "sqm0 sqm1 ln exp sqx0 sqx1 ln2 exp2 " + ACT_H)
        v2 = Steps(sem("vec_output"), "mw0 mx0 mw1 mx1 xn0 xn1 " + VEC_H + " g2 gw2")
        p2 = Steps(sem("pe_output"), " ".join(f"tr{k}" for k in range(0, KC, 2)) + " gate2")
        q_out = sem("queries_evacuated")
        sc_ps, sc_out = sem("scores_ready"), sem("scores_evacuated")
        vr = sem("vec_routing")
        ar = sem("act_routing")
        h_ps, h_used = sem("h_rows_ready"), sem("h_rows_used")
        staged, used = sem("indices_staged"), sem("expert_row_used")
        accz = sem("expert_sum_cleared")
        gland = [sem(f"row_landed{s}") for s in range(RING)]
        fin_v, fin_a, gelu_done, wv_done = sem("vec_final"), sem("act_final"), sem("gelu_done"), sem("weights_ready")

        block = ctx.enter_context(nc.Block())
        NADA = VECS * KC

        @block.sync
        def _(sp):
            for s in range(RING):
                sp.dma_start(ring[:, s, :], ada[s]).then_inc(land[s], 16)
            with sp.Fori(1, 2 * KC // RING) as t:
                for s in range(RING):
                    sp.wait_ge(ada_used, t * RING + (s + 1 - RING))
                    sp.dma_start(ring[:, s, :], ada[bass.ds(t * RING + s, 1)].rearrange("a p n -> p (a n)")).then_inc(land[s], 16)
            for j in range(TILES):
                sp.wait_ge(ada_used, 2 * KC - RING + j + 1)
                sp.dma_start(ring[:, j, 0:KT * 384], w_lora[j]).then_inc(land[j], 16)
            with sp.Fori(0, 3) as it:
                for g in range(4):
                    for j in range(TILES):
                        sp.wait_ge(w_used, it * 16 + (4 * g + j + 1))
                        sp.dma_start(ring[:, j, :], w_in[bass.ds(it * 16 + (4 * g + j), 1)].rearrange("a p n -> p (a n)")).then_inc(land[j], 16)
                        sp.wait_ge(ada_used, it * 16 + (2 * KC + 4 * g + j - 3))
                        sp.dma_start(ring[:, 4 + j, :], ada[bass.ds(it * 16 + (2 * KC + 4 * g + j), 1)].rearrange("a p n -> p (a n)")).then_inc(land[4 + j], 16)
            sp.wait_ge(ada_used, 5 * KC)
            sp.dma_start(ring[:, 6, :], ada_b[2 * D:3 * D].rearrange("(a n) -> a n", a=1).broadcast_to([P, D])).then_inc(abb_in, 16)
            sp.wait_ge(v1.sem, v1.at("gw1"))
            for j in range(TILES):
                sp.wait_ge(w_used, 4 * 13 - 3 + j)
                sp.dma_start(ring[:, j, :], w_tail[j]).then_inc(land[j], 16)
            with sp.Fori(0, PAIRS) as i:
                sp.wait_ge(pp_.sem, i * pp_.per + (pp_.names.index("g") + 1))
                sp.dma_start(lw.rearrange("p a b -> p (a b)"), lora_up[bass.ds(i, 1)].rearrange("a p n -> p (a n)")).then_inc(lw_in, 16)
            for e in (pv, pa, pp_, pg):
                sp.wait_ge(e.sem, (PAIRS + 1) * e.per)
            for t in range(4):
                for j in range(TILES):
                    if t:
                        sp.wait_ge(w_used, 4 * (13 + t - 1) + j + 1)
                        sp.dma_start(ring[:, j, :], w_tail[4 * t + j]).then_inc(land[j], 16)
                        sp.wait_ge(ada_used, 5 * KC + 4 * (t - 1) + j + 1)
                    sp.dma_start(ring[:, 4 + j, :], ada[5 * KC + 4 * t + j]).then_inc(land[4 + j], 16)
            sp.wait_ge(ada_used, NADA)
            sp.dma_start(ring[:, 6, :], ada_b[5 * D:6 * D].rearrange("(a n) -> a n", a=1).broadcast_to([P, D])).then_inc(abb_in, 16)
            sp.dma_start(gw2[:, :], post_ffn_w.rearrange("(a n) -> a n", a=1).broadcast_to([P, D])).then_inc(gw2_in, 16)
            sp.dma_start(ring[:, 4, :], keys).then_inc(keys_in, 16)
            for t in range(4, 8):
                for j in range(TILES):
                    sp.wait_ge(w_used, 4 * (13 + t - 1) + j + 1)
                    sp.dma_start(ring[:, j, :], w_tail[4 * t + j]).then_inc(land[j], 16)
            for tb in range(TB):
                sp.wait_ge(fin_v, 2 * (tb + 1))
                sp.dma_start(out[tb * P:(tb + 1) * P, :], xs[:, tb, :]).then_inc(stored, 16)
            sp.wait_ge(stored, 16 * TB)

        @block.gpsimd
        def _(pool):
            nconst = [0]

            def const(ins):
                nconst[0] += 1
                ins.then_inc(consts, 1)

            def after():
                pool.wait_ge(consts, nconst[0])

            for t in (ident, lmask[:, :, :], m0T, bones):
                const(nc.gpsimd.memset(t, 0.0))
            for t in (ones, strict, incl):
                const(nc.gpsimd.memset(t, 1.0))
            const(nc.gpsimd.memset(bmean, 0.0))
            after()
            for v, n in ((1e-6, 0), (64e-5, 1), (1e-12, 2), (0.0, 3)):
                const(nc.gpsimd.memset(cst[:, n:n + 1], v))
            for h in range(2):
                after()
                const(nc.gpsimd.memset(bones[h * 64:h * 64 + 64, h * 64:h * 64 + 64], 1.0))
                const(nc.gpsimd.memset(bmean[h * 64:h * 64 + 64, h * 64:h * 64 + 64], 1.0 / 64))
            after()
            const(nc.gpsimd.affine_select(out=ident, in_=ident, compare_op=ALU.not_equal, fill=1.0, base=0,
                                          pattern=[[-1, P]], channel_multiplier=1))
            for m in range(LEVELS):
                B = 1 << m
                v = lmask[:, m, :].rearrange("p (q r) -> p q r", r=2 * B)[:, :, B:]
                const(nc.gpsimd.memset(v, 1.0))
                after()
                const(nc.gpsimd.affine_select(out=v, in_=v, compare_op=ALU.is_ge, fill=0.0, base=0,
                                              pattern=[[-2 * B, P // (2 * B)], [0, B]], channel_multiplier=1))
                after()
                const(nc.gpsimd.affine_select(out=v, in_=v, compare_op=ALU.is_ge, fill=0.0, base=B - 1,
                                              pattern=[[2 * B, P // (2 * B)], [0, B]], channel_multiplier=-1))
            v = m0T.rearrange("p (q r) -> p q r", r=2)[:, :, 0:1]
            const(nc.gpsimd.affine_select(out=v, in_=v, compare_op=ALU.not_equal, fill=1.0, base=-1,
                                          pattern=[[-2, P // 2], [0, 1]], channel_multiplier=1))
            v = strict.rearrange("p (h r) -> p h r", h=2)
            const(nc.gpsimd.affine_select(out=v, in_=v, compare_op=ALU.is_gt, fill=0.0, base=0,
                                          pattern=[[CH, 2], [1, CH]], channel_multiplier=-1))
            after()
            const(nc.gpsimd.affine_select(out=v, in_=v, compare_op=ALU.is_ge, fill=0.0, base=0,
                                          pattern=[[-CH, 2], [0, CH]], channel_multiplier=1))
            for h in range(2):
                v = incl[h * 64:h * 64 + 64, :]
                after()
                const(nc.gpsimd.affine_select(out=v, in_=v, compare_op=ALU.is_ge, fill=0.0, base=0,
                                              pattern=[[1, CH]], channel_multiplier=-1))
            assert nconst[0] == NCONST, nconst[0]
            after()
            pool.wait_ge(v1.sem, v1.at("reset"))
            for n, t in enumerate((ab, bb, kb, vb)):
                nc.gpsimd.memset(t[:, :, :], 0.0).then_inc(zeroed, 1)
            nc.gpsimd.memset(u[:, 0:2], 0.0).then_inc(zeroed, 1)
            pool.wait_ge(zeroed, 6)
            pool.sem_inc(pg.sem, pg.lead)
            with pool.Fori(0, PAIRS) as i:
                for name, z, d in (("dr", Z_R, dr), ("dk", Z_K, dk), ("dv", Z_V, dv)):
                    zc = zT[:, bass.ds(i + z, 1), :]
                    if name == "dr":
                        pool.wait_ge(pv.sem, i * pv.per + pv.per)
                    pg.done(nc.gpsimd.tensor_tensor(d.rearrange("p (a b) -> p a b", a=1), zc[:, :, 0:T], zc[:, :, 1:ZS], ALU.subtract), name)
                pool.wait_ge(pv.sem, pv.at("kkr", i))
                pg.done(nc.gpsimd.tensor_tensor(kk2, kkr, kkr, ALU.mult), "kk2")
                pool.wait_ge(pp_.sem, i * pp_.per + pp_.per)
                pool.wait_ge(pa.sem, pa.at("Wi", i))
                pool.wait_ge(pv.sem, pv.at("kf", i))
                for h in range(2):
                    r = slice(h * 64, h * 64 + 64)
                    pool.wait_ge(pg.sem, pg.at(("kk2", "kb0")[h], i))
                    pg.done(nc.gpsimd.tensor_tensor(kb[r, :, r], kf[r, :].rearrange("p (c t) -> p c t", c=NCH),
                                                    Wi[r, :].rearrange("p (c t) -> p c t", c=NCH), ALU.mult), f"kb{h}")
                pool.wait_ge(pg.sem, pg.at("kb1", i))
                pg.done(nc.gpsimd.tensor_tensor(rt, zr, Wt, ALU.mult), "rt")
                pool.wait_ge(pa.sem, pa.at("lt", i))
                pg.done(nc.gpsimd.tensor_tensor(XT[:, :, :], LT[:, :, :], lmask[:, 0:1, :].broadcast_to([P, NCH, P]), ALU.mult), "XT0a")
                pool.wait_ge(pg.sem, pg.at("XT0a", i))
                pg.done(nc.gpsimd.tensor_tensor(XT[:, :, :], XT[:, :, :], ident.rearrange("p (a b) -> p a b", a=1).broadcast_to([P, NCH, P]), ALU.add), "XT0")
                for m in range(1, LEVELS):
                    if m > 2:
                        pool.wait_ge(pp_.sem, pp_.at(f"T1_{m - 2}", i))
                    pg.done(nc.gpsimd.tensor_tensor(LTm[m % 2][:, :, :], LT[:, :, :], lmask[:, m:m + 1, :].broadcast_to([P, NCH, P]), ALU.mult), f"m{m}")
                pg.done(nc.gpsimd.tensor_tensor(u[:, 2:].rearrange("p (a b) -> p a b", a=1), zT[:, bass.ds(i + Z_C, 1), 1:ZS],
                                                zT[:, bass.ds(i + Z_X, 1), 1:ZS], ALU.mult), "u")
                pool.wait_ge(pv.sem, pv.at("c2", i))
                pg.done(nc.gpsimd.tensor_tensor(cy.rearrange("p (a b) -> p a b", a=1), cy.rearrange("p (a b) -> p a b", a=1),
                                                zT[:, bass.ds(i + Z_B, 1), 1:ZS], ALU.mult), "cyb")
                pool.wait_ge(pg.sem, pg.at("cyb", i))
                pg.done(nc.gpsimd.tensor_tensor(csq, cy, cy, ALU.mult), "csq")
                pool.wait_ge(pv.sem, pv.at("yc", i))
                pg.done(nc.gpsimd.tensor_tensor(y, yc, yc, ALU.mult), "sqy")
            pool.wait_ge(vr, NR)
            nc.gpsimd.tensor_copy(i32(stage[:, 0, :]), i32(idx[:, 0:2])).then_inc(staged, 1)
            pool.sem_inc(used, RING)
            for ph in range(2 * TB):
                table = (expert_u, expert_v)[ph % 2]
                with pool.Fori(0, KTOP // 16) as t:
                    for g in range(8):
                        n = ph * KTOP + 2 * g
                        pool.wait_ge(staged, t * 8 + (ph * KTOP // 2 + g + 1))
                        pool.wait_ge(used, t * 16 + (n + 2))
                        nc.gpsimd.tensor_copy(i32(stage[:, (g + 1) % 8, :]), i32(idx)[:, bass.ds(t * 16 + (n + 2), 2)]).then_inc(staged, 1)
                        for j in range(2):
                            s = (2 * g + j) % RING
                            nc.gpsimd.indirect_dma_start(
                                out=ring[:, s, :], out_offset=None, in_=table[:, :],
                                in_offset=bass.IndirectOffsetOnAxis(ap=i32(stage[:, g, :])[:, j:j + 1], axis=0)).then_inc(gland[s], 16)

        @block.scalar
        def _(act):
            act.dma_start(colp, cols).then_inc(cols_in, 16)
            act.dma_start(xs[:, :, :], x.rearrange("(b p) n -> p b n", p=P)).then_inc(x_in, 16)
            act.dma_start(gw1, post_mix_w.rearrange("(a n) -> a n", a=1).broadcast_to([P, D])).then_inc(gw1_in, 16)
            act.wait_ge(cols_in, 16)
            a0.done(nc.scalar.activation(tmp16, colp[:, C_C:C_C + KC], ACT.Exp, scale=-1.0), "expc")
            act.wait_ge(x_in, 16)
            for b in range(TB):
                a0.done(nc.scalar.activation(xn[:, b, :], xs[:, b, :], ACT.Square, accum_out=ss[:, b:b + 1]), f"sq{b}")
            act.wait_ge(consts, NCONST)
            act.wait_ge(a0.sem, a0.at("sq1"))
            a0.done(nc.scalar.activation(lns[:, 0:2], ss[:, 0:2], ACT.Ln, bias=cst[:, 0:1], scale=1.0 / D), "ln")
            act.wait_ge(a0.sem, a0.at("ln"))
            a0.done(nc.scalar.activation(rstd[:, 0:2], lns[:, 0:2], ACT.Exp, scale=-0.5), "exp")
            act.wait_ge(v0.sem, v0.at("b1"))
            for k in ACT_K:
                act.wait_ge(p0.sem, p0.at(f"tr{k - k % 2}"))
                a0.done(nc.scalar.activation(hT[:, k, :], bank((k // 2) % 4, k % 2 * T, k % 2 * T + T), ACT.Identity,
                                             bias=modc[:, 1, k:k + 1], scale=modc[:, 0, k:k + 1]), f"h{k}")
            act.wait_ge(w_used, TILES)
            act.wait_ge(v0.sem, v0.at("h15"))
            nc.scalar.activation(zT[:, Z_L:Z_L + 2, 1:ZS], bank3(4, 2), ACT.Copy).then_inc(z_out, 1)
            nc.scalar.activation(zT[:, Z_L + 2, 1:ZS], bank(5, 0, T), ACT.Copy).then_inc(z_out, 1)
            with act.Fori(0, 3) as it:
                for g in range(4):
                    act.wait_ge(w_used, it * 16 + 4 * (g + 2))
                    for h in range(2):
                        nc.scalar.activation(zT[:, bass.ds(it * 16 + (4 * g + 2 * h), 2), 1:ZS], bank3(2 * (g % 2) + h, 2), ACT.Copy).then_inc(z_out, 1)
            act.wait_ge(v1.sem, v1.at("ml2"))
            a1.done(nc.scalar.activation(tz[0:64, :], dr[0:64, :], ACT.Tanh), "tanh")
            a1.done(nc.scalar.activation(tz[64:P, :], dr[64:P, :], ACT.Copy), "za")
            a1.done(nc.scalar.activation(sgz[:, :, :], dz[:, 1:3, :], ACT.Exp, scale=-1.0), "eg")
            act.sem_inc(pa.sem, pa.lead)
            with act.Fori(0, PAIRS) as i:
                act.wait_ge(pp_.sem, pp_.at("wa", i))
                act.wait_ge(pv.sem, pv.at("npp", i))
                pa.done(nc.scalar.activation(ewa[:, 0, :], bank(0, 0, T), ACT.Exp, bias=npp[:, W0:W0 + 1], scale=-1.0), "ew")
                pa.done(nc.scalar.activation(ewa[:, 1, :], bank(0, T), ACT.Exp, bias=npp[:, A0:A0 + 1], scale=-1.0), "ea")
                act.wait_ge(pp_.sem, pp_.at("g", i))
                pa.done(nc.scalar.activation(gT, bank(1, 0, T), ACT.Copy), "gT")
                act.wait_ge(pv.sem, pv.at("zv", i))
                for h in range(2):
                    r = slice(h * 64, h * 64 + 64)
                    pa.done(nc.scalar.activation(vb[r, :, r], zv[r, :].rearrange("p (c t) -> p c t", c=NCH), ACT.Copy), f"vb{h}")
                act.wait_ge(pv.sem, pv.at("cs", i))
                pa.done(nc.scalar.activation(Wt, cs, ACT.Exp, scale=-DECAY), "Wt")
                pa.done(nc.scalar.activation(Wi, cs, ACT.Exp, scale=DECAY), "Wi")
                act.wait_ge(pv.sem, pv.at("cse", i))
                pa.done(nc.scalar.activation(We, cse, ACT.Exp, scale=-DECAY), "We")
                act.wait_ge(pp_.sem, pp_.at("kks", i))
                pa.done(nc.scalar.activation(rn, bank(7, 0, T), ACT.Ln, bias=cst[:, 2:3]), "lnk")
                act.wait_ge(pa.sem, pa.at("lnk", i))
                pa.done(nc.scalar.activation(rn, rn, ACT.Exp, scale=-0.5), "rn")
                act.wait_ge(pp_.sem, pp_.at("lt", i))
                pa.done(nc.scalar.activation(LT.rearrange("p a b -> p (a b)"), bank(2), ACT.Copy), "lt")
                act.wait_ge(pp_.sem, pp_.at("vtr", i))
                pa.done(nc.scalar.activation(vtok.rearrange("p a b -> p (a b)"), bank(6), ACT.Copy), "vtok")
                act.wait_ge(pp_.sem, pp_.at("atr", i))
                pa.done(nc.scalar.activation(UA[:, :, 1, :], bank3(7, NCH), ACT.Copy), "atok")
                act.wait_ge(pp_.sem, pp_.at("btr", i))
                pa.done(nc.scalar.activation(btok.rearrange("p a b -> p (a b)"), bank(0), ACT.Copy), "btok")
                act.wait_ge(pp_.sem, pp_.at("ktr", i))
                pa.done(nc.scalar.activation(ktok.rearrange("p a b -> p (a b)"), bank(1), ACT.Copy), "ktok")
                for m in range(1, LEVELS):
                    act.wait_ge(pp_.sem, pp_.at(f"T1_{m}", i))
                    pa.done(nc.scalar.activation(T1.rearrange("p a b -> p (a b)"), bank(2), ACT.Copy), f"T1_{m}")
                act.wait_ge(pp_.sem, pp_.at("u1", i))
                pa.done(nc.scalar.activation(UA[:, :, 0, :], bank3(5, NCH), ACT.Copy), "u1")
                act.wait_ge(pp_.sem, pp_.at("qp", i))
                pa.done(nc.scalar.activation(QPb[:, 0:2, :, :].rearrange("p a b c -> p (a b c)"), bank(6), ACT.Copy), "qp1")
                act.wait_ge(pp_.sem, pp_.at("f", i))
                for c in range(3):
                    w = (c + 1) * CH - 1
                    pa.done(nc.scalar.activation(Fw[:, c, :], bank(4, c * P, c * P + P), ACT.Copy, scale=Wt[:, w:w + 1]), f"f{c}")
                act.wait_ge(pp_.sem, pp_.at("y", i))
                pa.done(nc.scalar.activation(y, bank(5, 0, T), ACT.Copy), "y")
                act.wait_ge(pp_.sem, pp_.at("var", i))
                act.wait_ge(pg.sem, pg.at("sqy", i))
                pa.done(nc.scalar.activation(rsy, bank(6, T), ACT.Ln, bias=cst[:, 1:2]), "lny")
                act.wait_ge(pa.sem, pa.at("lny", i))
                pa.done(nc.scalar.activation(rsy, rsy, ACT.Exp, scale=-0.5), "rsy")
                act.wait_ge(pp_.sem, pp_.at("conv", i))
                pa.done(nc.scalar.activation(crs, bank(7, 0, T), ACT.Ln, bias=cst[:, 0:1]), "lnc")
                act.wait_ge(pa.sem, pa.at("lnc", i))
                pa.done(nc.scalar.activation(crs, crs, ACT.Exp, scale=-0.5), "rsc")
            for g in range(4):
                act.wait_ge(w_used, 4 * (14 + g))
                for b in range(TB):
                    nc.scalar.activation(mixrow[:, b, g * GROUP:(g + 1) * GROUP], bank(2 * (g % 2) + b), ACT.Copy).then_inc(m_out, 1)
            act.wait_ge(m_out, 8)
            for b in range(TB):
                if b:
                    act.wait_ge(a2.sem, a2.at("sqm0"))
                a2.done(nc.scalar.activation(ff, mixrow[:, b, :], ACT.Square, accum_out=ss[:, 2 + b:3 + b]), f"sqm{b}")
            act.wait_ge(a2.sem, a2.at("sqm1"))
            a2.done(nc.scalar.activation(lns[:, 2:4], ss[:, 2:4], ACT.Ln, bias=cst[:, 0:1], scale=1.0 / D), "ln")
            act.wait_ge(a2.sem, a2.at("ln"))
            a2.done(nc.scalar.activation(rstd[:, 2:4], lns[:, 2:4], ACT.Exp, scale=-0.5), "exp")
            for b in range(TB):
                act.wait_ge(v2.sem, v2.at(f"mx{b}"))
                act.wait_ge(a2.sem, a2.at("exp" if b == 0 else "sqx0"))
                a2.done(nc.scalar.activation(ff, xs[:, b, :], ACT.Square, accum_out=ss[:, 4 + b:5 + b]), f"sqx{b}")
            act.wait_ge(a2.sem, a2.at("sqx1"))
            a2.done(nc.scalar.activation(lns[:, 4:6], ss[:, 4:6], ACT.Ln, bias=cst[:, 0:1], scale=1.0 / D), "ln2")
            act.wait_ge(a2.sem, a2.at("ln2"))
            a2.done(nc.scalar.activation(rstd[:, 4:6], lns[:, 4:6], ACT.Exp, scale=-0.5), "exp2")
            for k in ACT_K:
                act.wait_ge(p2.sem, p2.at(f"tr{k - k % 2}"))
                a2.done(nc.scalar.activation(h2T[:, k, :], bank((k // 2) % 4, k % 2 * T, k % 2 * T + T), ACT.Identity,
                                             bias=modc[:, 2, k:k + 1], scale=modc[:, 3, k:k + 1]), f"h{k}")
            for g in range(4):
                act.wait_ge(w_used, 4 * (18 + g))
                for h in range(2):
                    nc.scalar.activation(qT[:, 4 * g + 2 * h:4 * g + 2 * h + 2, :], bank3(2 * (g % 2) + h, 2), ACT.Copy).then_inc(q_out, 1)
            for b in range(TB):
                for q in range(4):
                    act.wait_ge(sc_ps, 4 * b + q + 1)
                    nc.scalar.activation(scores[b][:, 4 * q:4 * q + 4, :], bank3(4 + q, 4), ACT.Copy).then_inc(sc_out, 1)
            for b in range(TB):
                act.wait_ge(vr, GATE_AT[b])
                gv = gate[:, b, :]
                nc.scalar.activation(gv, gv, ACT.Exp).then_inc(ar, 1)
            for b in range(TB):
                act.wait_ge(used, RING + (2 * b + 1) * KTOP)
                nc.scalar.activation(wv[:, b, :], actv[:, b, :], ACT.Gelu).then_inc(gelu_done, 1)
                act.wait_ge(used, RING + (2 * b + 2) * KTOP)
                nc.scalar.activation(junk, ps[:, 2048:4096], ACT.Square, accum_out=ss[:, 6 + b:7 + b]).then_inc(fin_a, 1)
                act.wait_ge(fin_a, 3 * b + 1)
                nc.scalar.activation(lns[:, 6 + b:7 + b], ss[:, 6 + b:7 + b], ACT.Ln, bias=cst[:, 0:1], scale=1.0 / D).then_inc(fin_a, 1)
                act.wait_ge(fin_a, 3 * b + 2)
                nc.scalar.activation(rstd[:, 6 + b:7 + b], lns[:, 6 + b:7 + b], ACT.Exp, scale=-0.5).then_inc(fin_a, 1)

        @block.tensor
        def _(pe):
            mm = nc.tensor.matmul

            def columns(v, out_bank, at):
                for k in range(KC):
                    last = mm(bank(out_bank, at + k, at + k + 1), acc[:, v, k * P:(k + 1) * P], ones[:, 0:1], start=True, stop=True)
                return last

            pe.wait_ge(consts, NCONST)
            for v, name in enumerate(("scale1", "shift1")):
                pe.wait_ge(ada_used, KC * (v + 1))
                p0.done(columns(v, 7, v * KC), name)

            def turn(src, st, v, a):
                for k in range(0, KC, 2):
                    if k >= 8:
                        e = a if k // 2 % 2 == 0 else v
                        pe.wait_ge(e.sem, e.at(f"h{k - 7}"))
                    for kk in range(2):
                        for b in range(TB):
                            last = nc.tensor.transpose(bank((k // 2) % 4, kk * T + b * P, kk * T + b * P + P),
                                                       src[:, b, (k + kk) * P:(k + kk + 1) * P], ident)
                    st.done(last, f"tr{k}")

            pe.wait_ge(v0.sem, v0.at("xn1"))
            turn(xn, p0, v0, a0)

            def channels(g, b0, h, nsub, width):
                for j in range(TILES):
                    w = ring[:, j, 0:KT * width].rearrange("p (a b) -> p a b", a=KT)
                    for kk in range(KT):
                        k = j * KT + kk
                        for s in range(nsub):
                            last = mm(bank(b0 + s // 2, (s % 2) * T, (s % 2) * T + T), w[:, kk, s * P:(s + 1) * P], h[:, k, :],
                                      start=(k == 0 and s % 2 == 0), stop=(k == KC - 1), skip_group_check=True)
                    yield j, last

            pe.wait_ge(a0.sem, a0.at("h13"))
            pe.wait_ge(v0.sem, v0.at("h15"))
            steps = channels(0, 4, hT, 3, 384)
            for j in range(TILES):
                pe.wait_ge(land[j], 16 * 5)
                next(steps)[1].then_inc(w_used, 1)
            pe.sem_inc(z_out, 2)
            with pe.Fori(0, 3) as it:
                for g in range(4):
                    pe.wait_ge(z_out, it * 8 + (2 * g + 2))
                    steps = channels(g, 2 * (g % 2), hT, 4, GROUP)
                    for j in range(TILES):
                        pe.wait_ge(land[j], it * 64 + 16 * (6 + g))
                        next(steps)[1].then_inc(w_used, 1)
            pe.wait_ge(ada_used, 5 * KC)
            pe.wait_ge(z_out, 28)
            p1.done(columns(3, 7, 0), "shift2")
            p1.done(columns(4, 7, KC), "scale2")

            def rows(a, v, a_col):
                for q in range(4):
                    last = mm(bank(q), ones, a[:, q * 512:(q + 1) * 512], start=True, stop=True)
                return last

            p1.done(rows(acc[:, 2, :], 0, 0), "gate1")
            pe.wait_ge(v1.sem, v1.at("gw1"))
            pe.wait_ge(v1.sem, v1.at("reset"))
            pe.wait_ge(a1.sem, a1.at("za"))
            pe.sem_inc(pp_.sem, pp_.lead)
            with pe.Fori(0, PAIRS) as i:
                S = pp_
                pe.wait_ge(lw_in, i * 16 + 16)
                pe.wait_ge(pa.sem, i * pa.per + pa.per)
                pe.wait_ge(pv.sem, i * pv.per + pv.per)
                mm(bank(0, 0, T), lw[:, 0, :], tz, start=True, stop=True)
                S.done(mm(bank(0, T), lw[:, 1, :], tz, start=True, stop=True), "wa")
                mm(bank(1, 0, T), lw[:, 2, :], sgz[:, 0, :], start=True, stop=False)
                S.done(mm(bank(1, 0, T), lw[:, 3, :], sgz[:, 1, :], start=False, stop=True), "g")
                pe.wait_ge(pg.sem, pg.at("kk2", i))
                S.done(mm(bank(7, 0, T), bones, kk2, start=True, stop=True), "kks")
                pe.wait_ge(pv.sem, pv.at("bb1", i))
                for c in range(NCH):
                    last = mm(bank(2, c * P, c * P + P), bb[:, c, :], ab[:, c, :], start=True, stop=True)
                S.done(last, "lt")
                for c in range(NCH):
                    last = mm(bank(3, c * P, c * P + P), ab[:, c, :], bb[:, c, :], start=True, stop=True)
                S.done(last, "l")
                pe.wait_ge(pg.sem, pg.at("rt", i))
                for c in range(NCH):
                    last = mm(bank(4, c * P, c * P + P), kb[:, c, :], ab[:, c, :], start=True, stop=True)
                S.done(last, "akt")
                for c in range(NCH):
                    mm(bank(5, c * P, c * P + CH), bb[:, c, :], rt[:, c * CH:(c + 1) * CH], start=True, stop=True)
                    last = mm(bank(5, c * P + CH, c * P + P), kb[:, c, :], rt[:, c * CH:(c + 1) * CH], start=True, stop=True)
                S.done(last, "rbk")

                def turned(b, t, name):
                    for c in range(NCH):
                        last = nc.tensor.transpose(bank(b, c * P, c * P + P), t[:, c, :], ident)
                    S.done(last, name)

                pe.wait_ge(pa.sem, pa.at("vb1", i))
                turned(6, vb, "vtr")
                pe.wait_ge(pa.sem, pa.at("lnk", i))
                turned(7, ab, "atr")
                pe.wait_ge(pa.sem, pa.at("ea", i))
                turned(0, bb, "btr")
                pe.wait_ge(pa.sem, pa.at("rn", i))
                turned(1, kb, "ktr")
                pe.wait_ge(pv.sem, pv.at("rbk", i))
                pe.wait_ge(pa.sem, pa.at("vtok", i))
                for c in range(NCH):
                    last = mm(bank(5, c * P, c * P + P), AKT[:, c, :], vtok[:, c, :], start=True, stop=True)
                S.done(last, "u1")
                pe.wait_ge(pa.sem, pa.at("btok", i))
                S.done(mm(bank(0, 0, T), bones, rk, start=True, stop=True), "bon")
                for m in range(1, LEVELS):
                    pe.wait_ge(pg.sem, pg.at(f"m{m}", i))
                    if m == 1:
                        pe.wait_ge(pv.sem, pv.at("X0", i))
                        pe.wait_ge(pa.sem, pa.at("lt", i))
                    else:
                        pe.wait_ge(pv.sem, pv.at(f"XT{m - 1}", i))
                    for c in range(NCH):
                        last = mm(bank(2, c * P, c * P + P), LTm[m % 2][:, c, :], X[:, c, :], start=True, stop=True)
                    S.done(last, f"T1_{m}")
                    pe.wait_ge(pa.sem, pa.at(f"T1_{m}", i))
                    if m < LEVELS - 1:
                        for c in range(NCH):
                            mm(bank(3, c * P, c * P + P), XT[:, c, :], T1[:, c, :], start=True, stop=True)
                    for c in range(NCH):
                        last = mm(bank(4, c * P, c * P + P), T1[:, c, :], XT[:, c, :], start=True, stop=True)
                    S.done(last, f"X{m}")
                pe.wait_ge(pv.sem, pv.at("XT5", i))
                pe.wait_ge(pa.sem, pa.at("u1", i))
                for c in range(NCH):
                    last = mm(bank(6 + c // 2, (c % 2) * T, (c % 2) * T + T), XT[:, c, :], UA[:, c, :, :].rearrange("p a b -> p (a b)"), start=True, stop=True)
                S.done(last, "qp")
                pe.wait_ge(pv.sem, pv.at("qp2", i))
                pe.wait_ge(pa.sem, pa.at("qp1", i))
                for c in range(1, NCH):
                    last = mm(bank(2, c * CH, c * CH + CH), QPb[:, c, 1, :], RBK[:, c, 0, :], start=True, stop=True)
                S.done(last, "g_")
                pe.wait_ge(pa.sem, pa.at("ktok", i))
                for c in (1, 2):
                    last = mm(bank(1, (c - 1) * P, c * P), QPb[:, c, 1, :], btok[:, c, :], start=True, stop=True)
                S.done(last, "et")
                for c in range(3):
                    mm(bank(4, c * P, c * P + P), btok[:, c, :], QPb[:, c, 0, :], start=True, stop=False)
                    last = mm(bank(4, c * P, c * P + P), ktok[:, c, :], vtok[:, c, :], start=False, stop=True)
                S.done(last, "f")
                pe.wait_ge(pa.sem, pa.at("f2", i))
                pe.wait_ge(pv.sem, pv.at("et", i))
                S.done(mm(bank(3, 0, P), ET[:, 0, :], Fw[:, 0, :], start=True, stop=True), "s2")
                pe.wait_ge(pv.sem, pv.at("s2", i))
                S.done(mm(bank(3, P, 2 * P), ET[:, 1, :], St[:, 0, :], start=True, stop=True), "s3")
                pe.wait_ge(pv.sem, pv.at("s3", i))
                for c in range(NCH):
                    o = bank(5, c * CH, c * CH + CH)
                    if c:
                        mm(o, Fw[:, 0, :] if c == 1 else St[:, c - 2, :], Gt[:, c * CH:(c + 1) * CH], start=True, stop=False)
                    mm(o, QPb[:, c, 0, :], RBK[:, c, 0, :], start=(c == 0), stop=False)
                    last = mm(o, vtok[:, c, :], RBK[:, c, 1, :], start=False, stop=True)
                S.done(last, "y")
                pe.wait_ge(pa.sem, pa.at("y", i))
                S.done(mm(bank(6, 0, T), bmean, y, start=True, stop=True), "mean")
                pe.wait_ge(pg.sem, pg.at("sqy", i))
                S.done(mm(bank(6, T), bmean, y, start=True, stop=True), "var")
                S.done(mm(bank(7, 0, T), bmean, csq, start=True, stop=True), "conv")
            pe.wait_ge(pv.sem, PAIRS * pv.per + pv.per)
            for g in range(4):
                if g >= 2:
                    pe.wait_ge(m_out, 2 * (g - 1))
                for j in range(TILES):
                    pe.wait_ge(land[j], 16 * (18 + g))
                    w = ring[:, j, :].rearrange("p (a b) -> p a b", a=KT)
                    for kk in range(KT):
                        k = j * KT + kk
                        for b in range(TB):
                            zc = (k if k < 8 else Z_B + k - 8)
                            last = mm(bank(2 * (g % 2) + b), zT[:, zc, 1 + b * P:1 + b * P + P], w[:, kk, :], start=(k == 0), stop=(k == KC - 1))
                    last.then_inc(w_used, 1)
            pe.wait_ge(m_out, 8)
            pe.wait_ge(v2.sem, v2.at("xn1"))
            turn(mixrow, p2, v2, a2)
            pe.wait_ge(ada_used, NADA)
            for q in range(4):
                last = mm(bank(4 + q), ones, acc5[:, q * 512:(q + 1) * 512], start=True, stop=True)
            p2.done(last, "gate2")
            pe.wait_ge(a2.sem, a2.at("h13"))
            pe.wait_ge(v2.sem, v2.at("h15"))
            for g in range(4):
                if g >= 2:
                    pe.wait_ge(q_out, 2 * (g - 1))
                steps = channels(g, 2 * (g % 2), h2T, 4, GROUP)
                for j in range(TILES):
                    pe.wait_ge(land[j], 16 * (22 + g))
                    next(steps)[1].then_inc(w_used, 1)
            pe.wait_ge(q_out, 8)
            pe.wait_ge(keys_in, 16)
            pe.wait_ge(v2.sem, v2.at("gw2"))
            kv = ring[:, 4, :].rearrange("p (a b) -> p a b", a=KC)
            for b in range(TB):
                for q in range(4):
                    if b:
                        pe.wait_ge(sc_out, q + 1)
                    for c in range(4 * q, 4 * q + 4):
                        last = mm(bank(4 + q, (c % 4) * P, (c % 4) * P + P), qT[:, c, b * P:(b + 1) * P], kv[:, c, :], start=True, stop=True)
                    last.then_inc(sc_ps, 1)
            for b in range(TB):
                if b:
                    pe.wait_ge(used, RING + KTOP)
                for k in range(KC):
                    last = nc.tensor.transpose(ps[:, k * P:(k + 1) * P], h2T[:, k, b * P:(b + 1) * P], ident)
                last.then_inc(h_ps, 1)

        @block.vector
        def _(dve):
            V = nc.vector
            tt, ts, stt = V.tensor_tensor, V.tensor_scalar, V.scalar_tensor_tensor
            dve.wait_ge(a0.sem, a0.at("expc"))
            v0.done(ts(tmp16, tmp16, 1.0, None, ALU.add), "den")
            dve.wait_ge(v0.sem, v0.at("den"))
            v0.done(V.reciprocal(tmp16, tmp16), "rec")
            dve.wait_ge(v0.sem, v0.at("rec"))
            v0.done(tt(silu_c, tmp16, colp[:, C_C:C_C + KC], ALU.mult), "silu")
            dve.wait_ge(v0.sem, v0.at("silu"))

            def ada_tile(dst, slot, k):
                if k == 0:
                    ins = ts(dst, ring[:, slot, :], silu_c[:, 0:1], None, ALU.mult)
                else:
                    ins = stt(dst, ring[:, slot, :], silu_c[:, k:k + 1], dst, ALU.mult, ALU.add)
                ins.then_inc(ada_used, 1)

            with dve.Fori(0, 2) as v:
                for k in range(KC):
                    dve.wait_ge(land[k % RING], v * 32 + 16 * (k // RING + 1))
                    if k:
                        dve.wait_ge(ada_used, v * KC + k)
                    ada_tile(acc[:, bass.ds(v, 1), :].rearrange("p a b -> p (a b)"), k % RING, k)
            dve.wait_ge(p0.sem, p0.at("shift1"))
            v0.done(stt(modc[:, 0, :], bank(7, 0, KC), 1.0, colp[:, C_AB:C_AB + KC], ALU.add, ALU.add), "s1a")
            v0.done(tt(modc[:, 1, :], bank(7, KC, 2 * KC), colp[:, C_AB + KC:C_AB + 2 * KC], ALU.add), "s1b")
            dve.wait_ge(v0.sem, v0.at("s1b"))
            v0.done(tt(modc[:, 0, :], modc[:, 0, :], colp[:, C_PMW:C_PMW + KC], ALU.mult), "s1")
            dve.wait_ge(v0.sem, v0.at("s1"))
            v0.done(V.tensor_copy(tmp16, modc[:, 0, :]), "b1")
            dve.wait_ge(a0.sem, a0.at("exp"))
            for b in range(TB):
                v0.done(ts(xn[:, b, :], xs[:, b, :], rstd[:, b:b + 1], None, ALU.mult), f"xn{b}")
            for k in VEC_K:
                dve.wait_ge(p0.sem, p0.at(f"tr{k - k % 2}"))
                v0.done(ts(hT[:, k, :], bank((k // 2) % 4, k % 2 * T, k % 2 * T + T), modc[:, 0, k:k + 1], modc[:, 1, k:k + 1], ALU.mult, ALU.add), f"h{k}")
            with dve.Fori(0, 3) as it:
                for k in range(KC):
                    dve.wait_ge(land[4 + k % 4], it * 64 + 16 * (5 + k // 4))
                    if k:
                        dve.wait_ge(ada_used, it * KC + (2 * KC + k))
                    ada_tile(acc[:, bass.ds(it + 2, 1), :].rearrange("p a b -> p (a b)"), 4 + k % 4, k)
            dve.wait_ge(p1.sem, p1.at("scale2"))
            v1.done(tt(modc[:, 2, :], bank(7, 0, KC), colp[:, C_AB + 2 * KC:C_AB + 3 * KC], ALU.add), "b2")
            v1.done(stt(modc[:, 3, :], bank(7, KC, 2 * KC), 1.0, colp[:, C_AB + 3 * KC:C_AB + 4 * KC], ALU.add, ALU.add), "s2a")
            dve.wait_ge(v1.sem, v1.at("s2a"))
            v1.done(tt(modc[:, 3, :], modc[:, 3, :], colp[:, C_PFW:C_PFW + KC], ALU.mult), "s2b")
            v1.done(V.memset(zT[:, :, 0:1], 0.0), "s2")
            dve.wait_ge(p1.sem, p1.at("gate1"))
            dve.wait_ge(abb_in, 16)
            v1.done(tt(ring[:, 6, :], ps[:, 0:D], ring[:, 6, :], ALU.add), "g1")
            dve.wait_ge(v1.sem, v1.at("g1"))
            dve.wait_ge(gw1_in, 16)
            v1.done(tt(gw1, gw1, ring[:, 6, :], ALU.mult), "gw1")
            dve.wait_ge(v1.sem, v1.at("gw1"))
            dve.wait_ge(z_out, 28)
            for n, d in enumerate((zr, zk, zv)):
                v1.done(tt(d, zT[:, Z_L + n, 0:T], zT[:, Z_L + n, 1:ZS], ALU.subtract), f"dl{n}")
            for n, (d, o) in enumerate(((zr, dr), (zk, dk), (zv, dv))):
                dve.wait_ge(v1.sem, v1.at(f"dl{n}"))
                v1.done(stt(o, d, colp[:, C_ML + n:C_ML + n + 1], zT[:, Z_L + n, 1:ZS], ALU.mult, ALU.add), f"ml{n}")
            dve.wait_ge(a1.sem, a1.at("eg"))
            v1.done(ts(sgz[:, :, :], sgz[:, :, :], 1.0, None, ALU.add), "eg1")
            dve.wait_ge(v1.sem, v1.at("eg1"))
            v1.done(V.reciprocal(sgz[:, :, :], sgz[:, :, :]), "sg")
            V.memset(reset, 1.0).then_inc(zeroed, 1)
            dve.wait_ge(zeroed, 1)
            v1.done(V.memset(reset.rearrange("p (c t) -> p c t", c=NCH)[:, :, 0:1], 0.0), "reset")
            dve.wait_ge(zeroed, 6)
            dve.sem_inc(pv.sem, pv.lead)
            chunked = lambda v: v.rearrange("p (c t) -> p c t", c=NCH)
            flat = lambda v: v.rearrange("p a b -> p (a b)")
            over = lambda v: v.rearrange("p (a b) -> p a b", a=1).broadcast_to([P, NCH, P])
            with dve.Fori(0, PAIRS) as i:
                S = pv
                here = lambda n: S.at(n, i)
                dve.wait_ge(pv.sem, i * pv.per + pv.per)
                S.done(V.tensor_copy(pp, colp[:, bass.ds(i * PC + C_PP, PC)]), "pp")
                dve.wait_ge(pv.sem, here("pp"))
                S.done(ts(npp, pp, -1.0, None, ALU.mult), "npp")
                for name, src, d, z, mx, o in (("zr", "dr", dr, Z_R, MIX_R, zr), ("zk", "dk", dk, Z_K, MIX_K, zk), ("zv", "dv", dv, Z_V, MIX_V, zv)):
                    dve.wait_ge(pg.sem, pg.at(src, i))
                    S.done(stt(o, d, pp[:, mx:mx + 1], zT[:, bass.ds(i + z, 1), 1:ZS].rearrange("p a b -> p (a b)"), ALU.mult, ALU.add), name)
                dve.wait_ge(pv.sem, here("zk"))
                S.done(ts(kkr, zk, pp[:, K_K:K_K + 1], None, ALU.mult), "kkr")
                dve.wait_ge(pa.sem, pa.at("ea", i))
                S.done(ts(flat(ewa), flat(ewa), 1.0, None, ALU.add), "den")
                dve.wait_ge(pv.sem, here("den"))
                S.done(V.reciprocal(flat(ewa), flat(ewa)), "sig")
                dve.wait_ge(pv.sem, here("sig"))
                S.done(V.tensor_tensor_scan(cs, reset, ewa[:, 0, :], 0.0, ALU.mult, ALU.add), "cs")
                dve.wait_ge(pv.sem, here("cs"))
                S.done(tt(cse, cs, ewa[:, 0, :], ALU.subtract), "cse")
                dve.wait_ge(pa.sem, pa.at("rn", i))
                S.done(tt(kk, kkr, rn, ALU.mult), "kk")
                dve.wait_ge(pv.sem, here("kk"))
                S.done(tt(kka, kk, ewa[:, 1, :], ALU.mult), "kka")
                S.done(ts(t1, ewa[:, 1, :], -1.0, pp[:, K_A:K_A + 1], ALU.add, ALU.mult), "t1")
                dve.wait_ge(pv.sem, here("t1"))
                S.done(stt(kf, t1, 1.0, zk, ALU.add, ALU.mult), "kf")
                dve.wait_ge(pp_.sem, i * pp_.per + pp_.per)
                for h in range(2):
                    r = slice(h * 64, h * 64 + 64)
                    S.done(stt(ab[r, :, r], chunked(kk)[r], -1.0, chunked(We)[r], ALU.mult, ALU.mult), f"ab{h}")
                for h in range(2):
                    r = slice(h * 64, h * 64 + 64)
                    S.done(tt(bb[r, :, r], chunked(kka)[r], chunked(Wi)[r], ALU.mult), f"bb{h}")
                dve.wait_ge(pv.sem, here("kf"))
                S.done(stt(rk, zr, pp[:, R_K:R_K + 1], kf, ALU.mult, ALU.mult), "rk")
                dve.wait_ge(pp_.sem, pp_.at("l", i))
                S.done(tt(X[:, :, :], bank3(3, NCH), over(m0T), ALU.mult), "X0a")
                dve.wait_ge(pv.sem, here("X0a"))
                S.done(tt(X[:, :, :], X[:, :, :], over(ident), ALU.add), "X0")
                dve.wait_ge(pp_.sem, pp_.at("akt", i))
                S.done(tt(AKT[:, :, :], bank3(4, NCH), over(strict), ALU.mult), "akt")
                dve.wait_ge(pp_.sem, pp_.at("rbk", i))
                S.done(tt(RBK.rearrange("p a b c -> p (a b) c"), bank3(5, 2 * NCH),
                          incl.rearrange("p (a b) -> p a b", a=1).broadcast_to([P, 2 * NCH, CH]), ALU.mult), "rbk")
                for m in range(1, LEVELS):
                    dve.wait_ge(pp_.sem, pp_.at(f"X{m}", i))
                    if m < LEVELS - 1:
                        S.done(tt(flat(X), bank(3), flat(X), ALU.add), f"X{m}")
                    if m == 1:
                        dve.wait_ge(pg.sem, pg.at("XT0", i))
                    S.done(tt(flat(XT), bank(4), flat(XT), ALU.add), f"XT{m}")
                dve.wait_ge(pp_.sem, pp_.at("qp", i))
                S.done(V.tensor_copy(QPb[:, 2:4, :, :].rearrange("p a b c -> p (a b c)"), bank(7)), "qp2")
                dve.wait_ge(pp_.sem, pp_.at("et", i))
                S.done(tt(ET[:, :, :], bank(1, 0, 2 * P).rearrange("p (a b) -> p a b", a=2),
                          ident.rearrange("p (a b) -> p a b", a=1).broadcast_to([P, 2, P]), ALU.add), "et")
                S.done(tt(Gt[:, CH:], bank(2, CH, T), rt[:, CH:], ALU.add), "g")
                for c, name in ((1, "s2"), (2, "s3")):
                    dve.wait_ge(pp_.sem, pp_.at(name, i))
                    dve.wait_ge(pa.sem, pa.at("f2", i))
                    w = (c + 1) * CH - 1
                    S.done(stt(St[:, c - 1, :], bank(3, (c - 1) * P, c * P), Wt[:, w:w + 1], Fw[:, c, :], ALU.mult, ALU.add), name)
                dve.wait_ge(pg.sem, pg.at("u", i))
                S.done(ts(cy, u[:, 0:T], pp[:, CW0:CW0 + 1], None, ALU.mult), "c0")
                dve.wait_ge(pv.sem, here("c0"))
                S.done(stt(cy, u[:, 1:T + 1], pp[:, CW1:CW1 + 1], cy, ALU.mult, ALU.add), "c1")
                dve.wait_ge(pv.sem, here("c1"))
                S.done(stt(cy, u[:, 2:T + 2], pp[:, CW2:CW2 + 1], cy, ALU.mult, ALU.add), "c2")
                dve.wait_ge(pp_.sem, pp_.at("mean", i))
                S.done(tt(yc, y, bank(6, 0, T), ALU.subtract), "yc")
                S.done(tt(bon, bank(0, 0, T), zv, ALU.mult), "bon")
                dve.wait_ge(pa.sem, pa.at("rsy", i))
                S.done(tt(yc, yc, rsy, ALU.mult), "yn")
                dve.wait_ge(pv.sem, here("yn"))
                S.done(ts(yc, yc, pp[:, LN_W:LN_W + 1], pp[:, LN_B:LN_B + 1], ALU.mult, ALU.add), "aff")
                dve.wait_ge(pv.sem, here("aff"))
                S.done(tt(yc, yc, bon, ALU.add), "addb")
                dve.wait_ge(pv.sem, here("addb"))
                S.done(tt(zT[:, bass.ds(i + Z_R, 1), 1:ZS].rearrange("p a b -> p (a b)"), yc, gT, ALU.mult), "yg")
                dve.wait_ge(pa.sem, pa.at("rsc", i))
                S.done(stt(zT[:, bass.ds(i + Z_B, 1), 1:ZS].rearrange("p a b -> p (a b)"), cy, pp[:, CN:CN + 1], crs, ALU.mult, ALU.mult), "cout")
            dve.wait_ge(pp_.sem, PAIRS * pp_.per + pp_.per)
            dve.wait_ge(pa.sem, PAIRS * pa.per + pa.per)
            dve.wait_ge(pg.sem, PAIRS * pg.per + pg.per)
            for k in range(KC):
                dve.wait_ge(land[4 + k % 4], 16 * (17 + k // 4))
                if k:
                    dve.wait_ge(ada_used, 5 * KC + k)
                ada_tile(acc5, 4 + k % 4, k)
            dve.wait_ge(a2.sem, a2.at("exp"))
            for b in range(TB):
                v2.done(stt(mixrow[:, b, :], mixrow[:, b, :], rstd[:, 2 + b:3 + b], gw1, ALU.mult, ALU.mult), f"mw{b}")
                dve.wait_ge(v2.sem, v2.at(f"mw{b}"))
                v2.done(tt(xs[:, b, :], xs[:, b, :], mixrow[:, b, :], ALU.add), f"mx{b}")
            dve.wait_ge(a2.sem, a2.at("exp2"))
            for b in range(TB):
                v2.done(ts(mixrow[:, b, :], xs[:, b, :], rstd[:, 4 + b:5 + b], None, ALU.mult), f"xn{b}")
            for k in VEC_K:
                dve.wait_ge(p2.sem, p2.at(f"tr{k - k % 2}"))
                v2.done(ts(h2T[:, k, :], bank((k // 2) % 4, k % 2 * T, k % 2 * T + T), modc[:, 3, k:k + 1], modc[:, 2, k:k + 1], ALU.mult, ALU.add), f"h{k}")
            dve.wait_ge(p2.sem, p2.at("gate2"))
            dve.wait_ge(abb_in, 32)
            v2.done(tt(ring[:, 6, :], ps[:, 2048:4096], ring[:, 6, :], ALU.add), "g2")
            dve.wait_ge(v2.sem, v2.at("g2"))
            dve.wait_ge(gw2_in, 16)
            v2.done(tt(gw2, gw2, ring[:, 6, :], ALU.mult), "gw2")
            nr = [0]

            def r(ins):
                nr[0] += 1
                return ins.then_inc(vr, 1)

            def settle():
                dve.wait_ge(vr, nr[0])

            for n in range(TOPK):
                r(V.memset(iota16[:, n:n + 1], float(n)))
            NEG = -3.0e38

            def top16(src, vals, where, rep):
                r(V.max(vals[:, 0:8], src))
                settle()
                r(V.max_index(where[:, 0:8], vals[:, 0:8], src))
                r(V.match_replace(rep, vals[:, 0:8], src, NEG))
                settle()
                r(V.max(vals[:, 8:16], rep))
                settle()
                r(V.max_index(where[:, 8:16], vals[:, 8:16], rep))

            for b in range(TB):
                dve.wait_ge(sc_out, 4 * (b + 1))
                for c in range(KC):
                    top16(scores[b][:, c, :], v16[:, c, :], u32(iu[:, c, :]), repl[:, c * NKEYS:(c + 1) * NKEYS])
                settle()
                r(V.tensor_copy(i16[:, :, :], u32(iu[:, :, :])))
                vp = v16.rearrange("p (h s) k -> p h s k", s=2)
                ip = i16.rearrange("p (h s) k -> p h s k", s=2)
                full = [P, HEADS, TOPK, TOPK]
                for h in range(HEADS):
                    r(tt(cand[:, h, :].rearrange("p (a b) -> p a b", a=TOPK),
                         v16[:, 2 * h, :].rearrange("p (a b) -> p a b", b=1).broadcast_to([P, TOPK, TOPK]),
                         v16[:, 2 * h + 1, :].rearrange("p (a b) -> p a b", a=1).broadcast_to([P, TOPK, TOPK]), ALU.add))
                settle()
                for h in range(HEADS):
                    top16(cand[:, h, :], topv[:, h, :], u32(pos[:, h, :]), repl[:, h * 256:(h + 1) * 256])
                settle()
                r(ts(u32(hi_u[:, :, :]), u32(pos[:, :, :]), 4, None, ALU.logical_shift_right))
                r(ts(u32(lo_u[:, :, :]), u32(pos[:, :, :]), 15, None, ALU.bitwise_and))
                settle()
                r(V.tensor_copy(hi_f[:, :, :], u32(hi_u[:, :, :])))
                r(V.tensor_copy(lo_f[:, :, :], u32(lo_u[:, :, :])))
                settle()
                for half, sel, dst in ((0, hi_f, ei), (1, lo_f, ej)):
                    for h in range(HEADS):
                        r(tt(eq[:, h, :, :], sel[:, h, :].rearrange("p (a b) -> p a b", b=1).broadcast_to([P, TOPK, TOPK]),
                             iota16.rearrange("p (a b) -> p a b", a=1).broadcast_to([P, TOPK, TOPK]), ALU.is_equal))
                    settle()
                    for h in range(HEADS):
                        r(tt(eq[:, h, :, :], eq[:, h, :, :], i16[:, 2 * h + half, :].rearrange("p (a b) -> p a b", a=1).broadcast_to([P, TOPK, TOPK]), ALU.mult))
                    settle()
                    r(V.tensor_reduce(dst.rearrange("p a b -> p (a b)"), eq.rearrange("p a b c -> p (a b) c"), AX.X, ALU.add))
                    settle()
                r(stt(ei[:, :, :], ei[:, :, :], float(NKEYS), ej[:, :, :], ALU.mult, ALU.add))
                settle()
                for rep_ in range(2):
                    r(V.tensor_copy(i32(idx[:, (2 * b + rep_) * KTOP:(2 * b + rep_ + 1) * KTOP]), ei.rearrange("p a b -> p (a b)")))
                gb = gate[:, b, :].rearrange("p (h k) -> p h k", h=HEADS)
                r(tt(gb, topv[:, :, :], topv[:, :, 0:1].broadcast_to([P, HEADS, TOPK]), ALU.subtract))
                assert nr[0] == GATE_AT[b], nr[0]
                dve.wait_ge(ar, b + 1)
                r(V.tensor_reduce(gsum, gb, AX.X, ALU.add))
                settle()
                r(V.reciprocal(grec, gsum))
                settle()
                r(tt(gb, gb, grec.rearrange("p (a b) -> p a b", b=1).broadcast_to([P, HEADS, TOPK]), ALU.mult))
            r(V.memset(i32(idx[:, 4 * KTOP:4 * KTOP + 2]), 0))
            settle()
            assert nr[0] == NR, nr[0]
            for b in range(TB):
                dve.wait_ge(h_ps, b + 1)
                with dve.Fori(0, KTOP // 16) as t:
                    for j in range(16):
                        s = j % RING
                        dve.wait_ge(gland[s], t * 32 + 16 * (2 * b * 16 + j // RING + 1))
                        stt(ring[:, s, :], ring[:, s, :], 1.0, ps[:, 0:D], ALU.mult, ALU.mult,
                            accum_out=actv[:, b, bass.ds(t * 16 + j, 1)]).then_inc(used, 1)
                dve.wait_ge(gelu_done, b + 1)
                tt(wv[:, b, :], wv[:, b, :], gate[:, b, :], ALU.mult).then_inc(wv_done, 1)
                V.memset(ps[:, 2048:4096], 0.0).then_inc(wv_done, 1)
                dve.wait_ge(wv_done, 2 * b + 2)
                with dve.Fori(0, KTOP // 16) as t:
                    for j in range(16):
                        s = j % RING
                        dve.wait_ge(gland[s], t * 32 + 16 * ((2 * b + 1) * 16 + j // RING + 1))
                        dve.wait_ge(used, t * 16 + (RING + (2 * b + 1) * KTOP + j))
                        stt(ps[:, 2048:4096], ring[:, s, :], wv[:, b, bass.ds(t * 16 + j, 1)], ps[:, 2048:4096], ALU.mult, ALU.add).then_inc(used, 1)
                dve.wait_ge(fin_a, 3 * b + 3)
                stt(ff, ps[:, 2048:4096], rstd[:, 6 + b:7 + b], gw2, ALU.mult, ALU.mult).then_inc(fin_v, 1)
                dve.wait_ge(fin_v, 2 * b + 1)
                tt(xs[:, b, :], xs[:, b, :], ff, ALU.add).then_inc(fin_v, 1)


NCONST = 40
GATE_AT = (187, 361)
NR = 365


def kernel(x, c, ada_w, ada_b, pre_mix_w, post_mix_w, w_in, rwkv_mix, w0, w_up, a0, a_up, g_up, k_k, k_a, r_k,
           ln_x_w, ln_x_b, conv_w, conv_norm_w, w_out, pre_ffn_w, post_ffn_w, w_q, sub_keys_1, sub_keys_2,
           expert_u, expert_v):
    import concourse.bacc as bacc
    from concourse.bass_utils import run_bass_kernel_spmd as run

    f = lambda a: np.asarray(a)
    as_cols = lambda v: v.reshape(-1, P).T
    RW = 1024
    lora0 = 3 * RW
    wi = f(w_in)[0]
    ab = f(ada_b)[0].reshape(VECS, D)
    mix = f(rwkv_mix)[0]
    lmix = np.zeros(384, np.float32)
    lmix[:288] = mix[lora0:lora0 + 288]
    per = [mix[0:RW], mix[RW:2 * RW], mix[2 * RW:3 * RW], f(w0)[0], f(a0)[0], f(k_k)[0], f(k_a)[0], f(r_k)[0].reshape(-1),
           f(ln_x_w)[0], f(ln_x_b)[0], f(conv_w)[0, 0], f(conv_w)[0, 1], f(conv_w)[0, 2], f(conv_norm_w)[0],
           np.zeros(RW, np.float32), np.zeros(RW, np.float32)]
    pp = np.stack([as_cols(v) for v in per], 2).reshape(P, PAIRS * PC)
    cols = np.concatenate([as_cols(f(pre_mix_w)[0]), as_cols(f(pre_ffn_w)[0]), as_cols(ab[1]), as_cols(ab[0]), as_cols(ab[3]),
                           as_cols(ab[4]), as_cols(f(c)[0]), as_cols(lmix), np.zeros((P, 1), np.float32), pp], 1)
    ada = f(ada_w)[0].reshape(KC, P, VECS, D).transpose(2, 0, 1, 3)[list(VEC_ORDER)].reshape(VECS * KC, P, D)

    def tiles(w, width):
        n = w.shape[1] // width
        return w.reshape(TILES, KT, P, n, width).transpose(3, 0, 2, 1, 4).reshape(n * TILES, P, KT * width)

    lw = np.zeros((D, 384), np.float32)
    lw[:, :288] = wi[:, lora0:lora0 + 288]
    w_main = np.concatenate([wi[:, :lora0], wi[:, lora0 + 288:]], 1)
    up = np.zeros((4, P, RW), np.float32)
    up[0, 0:64] = f(w_up)[0]
    up[1, 64:P] = f(a_up)[0]
    up[2] = f(g_up)[0, 0:P]
    up[3, 0:32] = f(g_up)[0, P:]
    lora_up = up.reshape(4, P, PAIRS, P).transpose(2, 1, 0, 3).reshape(PAIRS, P, 4 * P)
    keys = np.stack([f(sub_keys_1)[0], f(sub_keys_2)[0]], 1).reshape(KC, NKEYS, P).transpose(2, 0, 1).reshape(P, KC * NKEYS)
    arrays = {
        "x": f(x)[0], "cols": cols, "ada": ada, "ada_b": f(ada_b)[0], "post_mix_w": f(post_mix_w)[0],
        "post_ffn_w": f(post_ffn_w)[0], "w_lora": tiles(lw, 384), "w_in": tiles(w_main, GROUP),
        "w_tail": np.concatenate([tiles(f(w_out)[0], GROUP), tiles(f(w_q)[0], GROUP)]),
        "lora_up": lora_up, "keys": keys, "expert_u": f(expert_u)[0], "expert_v": f(expert_v)[0],
    }
    nc = bacc.Bacc("TRN2", target_bir_lowering=False, num_devices=1)
    ins, aps = {}, []
    for name, a in arrays.items():
        ins["in_" + name] = np.ascontiguousarray(a)
        aps.append(nc.dram_tensor("in_" + name, a.shape, F32, kind="ExternalInput").ap())
    out = nc.dram_tensor("out_0", (T, D), F32, kind="ExternalOutput").ap()
    build_layer(nc, *aps, out)
    r = run(nc, [ins], core_ids=[0])
    return r.results[0]["out_0"].reshape(1, T, D)
```

```python
from contextlib import ExitStack
import math

import numpy as np
import concourse.bass as bass
from concourse import mybir

ALU = mybir.AluOpType
ACT = mybir.ActivationFunctionType
AX = mybir.AxisListType
F32 = mybir.dt.float32
I32 = mybir.dt.int32
U32 = mybir.dt.uint32

P = 128
D = 2048
T = 256
TB = T // P
KC = D // P
VECS = 6
VEC_ORDER = (1, 0, 2, 3, 4, 5)
SL = 2048
RING = 8
GROUP = 512
KT = 4
TILES = KC // KT
ZS = T + 1
R, K, V, B, C, X_ = range(6)
WSLOTS = 6
LORA = 3
PAIRS = 8
PC = 16
MIX_R, MIX_K, MIX_V, W0, A0, K_K, K_A, R_K, LN_W, LN_B, CW0, CW1, CW2, CN = range(14)
CH = 64
NCH = T // CH
LEVELS = 6
DECAY = math.exp(-0.5)
HEADS, TOPK, NKEYS = 8, 16, 128
KTOP = HEADS * TOPK
C_PMW, C_PFW, C_PG1, C_PG2, C_AB, C_C, C_ML, C_PP = 0, 16, 32, 48, 64, 160, 176, 180
NCOL = C_PP + PAIRS * PC


ACT_K = [k for k in range(KC) if k // 2 % 2 == 0]
VEC_K = [k for k in range(KC) if k // 2 % 2 == 1]
ACT_H = " ".join(f"h{k}" for k in ACT_K)
VEC_H = " ".join(f"h{k}" for k in VEC_K)


class Steps:

    def __init__(self, sem, names, lead=False):
        self.sem, self.names, self.per = sem, names.split(), len(names.split())
        assert len(set(self.names)) == self.per
        self.lead = self.per if lead else 0
        self.next = 0

    def at(self, name, i=0):
        return i * self.per + (self.lead + self.names.index(name) + 1)

    def done(self, ins, name):
        assert self.names[self.next % self.per] == name, (self.names[self.next % self.per], name)
        self.next += 1
        return ins.then_inc(self.sem, 1)


def build_layer(nc, x, cols, ada, w_in, w_tail, lora_up, keys,
                expert_u, expert_v, out):
    with ExitStack() as ctx:
        arena_size = 53200
        arena = ctx.enter_context(nc.sbuf_tensor("arena", [P, arena_size], F32))
        ps = ctx.enter_context(nc.psum_tensor("ps", [P, 4096], F32))
        top = [0]

        def take(n):
            a = top[0]
            top[0] += n
            assert top[0] <= arena_size, top[0]
            return a

        def view(a, *shape):
            n = int(np.prod(shape))
            v = arena[:, a:a + n]
            if len(shape) == 2:
                v = v.rearrange("p (a b) -> p a b", a=shape[0])
            if len(shape) == 3:
                v = v.rearrange("p (a b c) -> p a b c", a=shape[0], b=shape[1])
            return v

        def new(*shape):
            return view(take(int(np.prod(shape))), *shape)

        def sem(name):
            return ctx.enter_context(nc.semaphore(name))

        def bank(b, lo=0, hi=512):
            return ps[:, b * 512 + lo:b * 512 + hi]

        def bank3(b, n):
            return bank(b).rearrange("p (a b) -> p a b", a=n)

        ring = new(RING, SL)
        yT = new(KC, T)
        z = new(6, ZS)
        hT = new(KC, T)
        h2T = hT
        colp = new(NCOL)
        ident, ones, bones, bmean = new(P), new(P), new(P), new(P)
        lmask = new(LEVELS, P)
        m0T, strict, incl = new(P), new(P), new(CH)
        cst = new(4)
        silu_c, tmp16 = new(KC), new(KC)
        modc = new(VECS, KC)
        s1c, s2c = new(KC), new(KC)
        gcol = new(2, KC)
        ss, lns, rstd = new(16), new(16), new(16)
        tz, sgz = new(T), new(2, T)
        acc = new(D)
        g_at = take(0)
        xn = new(TB, D)
        acc1 = new(D)
        zl = new(3, ZS)
        dl, ml = new(3, T), new(3, T)
        top[0] = g_at
        lw = new(4, P)
        pp, npp = [new(PC), new(PC)], new(PC)
        dz = new(3, T)
        dr, dk, dv = (dz[:, n, :] for n in range(3))
        zr, zk, zv = (new(T) for _ in range(3))
        ewa = new(2, T)
        reset = new(T)
        cs, cse, Wt, Wi, We = (new(T) for _ in range(5))
        kkr, kk2, rn, kk, kka, t1, kf, rt, rk = (new(T) for _ in range(9))
        gT = [new(T), new(T)]
        Gt, y, yc, bon, rsy = (new(T) for _ in range(5))
        u = new(T + 2)
        cy, csq, crs = new(T), new(T), new(T)
        ab, bb, kb, vb = (new(NCH, P) for _ in range(4))
        LT = new(NCH, P)
        LTm = [new(NCH, P) for _ in range(2)]
        X, XT, T1 = new(NCH, P), new(NCH, P), new(NCH, P)
        AKT = new(NCH, P)
        RBK = new(NCH, 2, CH)
        vtok, btok, ktok = new(NCH, P), new(NCH, P), new(NCH, P)
        UA = new(NCH, 2, P)
        QPb = new(NCH, 2, P)
        ET, Fw, St = new(2, P), new(3, P), new(2, P)
        top[0] = g_at
        xs = new(TB, D)
        mix_at = take(TB * D)
        mixrow = view(mix_at, TB, D)
        scores = [view(mix_at, KC, NKEYS), view(mix_at + D, KC, NKEYS)]
        qT = new(KC, T)
        gw2 = new(D)
        junk = new(D)
        ff = new(D)
        v16, i16 = new(2 * 2, TOPK), new(2 * 2, TOPK)
        iu = new(2 * 2, TOPK)
        repl = new(D // 4)
        cand = new(2, TOPK * TOPK)
        eq = new(2 * TOPK, TOPK)
        topv, pos, hi_u, lo_u, hi_f, lo_f, ei, ej = (new(2, TOPK) for _ in range(8))
        iota16 = new(TOPK)
        gate = new(TB, KTOP)
        gsum, grec = new(HEADS), new(HEADS)
        idx = new(4 * KTOP + 2)
        stage = new(8, 2)
        actv, wv = new(TB, KTOP), new(TB, KTOP)
        i32 = lambda v: v.bitcast(I32)
        u32 = lambda v: v.bitcast(U32)

        land = [sem(f"slot_landed{s}") for s in range(RING)]
        w_used, ada_used = sem("weight_tile_used"), sem("ada_tile_used")
        x_in, cols_in, keys_in, lw_in = sem("x_in"), sem("cols_in"), sem("keys_in"), sem("lora_up_in")
        consts = sem("constants_ready")
        z_out = sem("z_evacuated")
        stored = sem("out_stored")
        v0 = Steps(sem("vec_prologue"), "den rec silu m0 m1 s1 s1b xn0 xn1 " + VEC_H +
                   " zero dl0 dl1 dl2 ml0 ml1 ml2 eg1 sg res1 reset")
        a0 = Steps(sem("act_prologue"), "expc sq0 sq1 ln exp " + ACT_H + " tanh za eg")
        p0 = Steps(sem("pe_prologue"), "scale1 shift1 " + " ".join(f"tr{k}" for k in range(0, KC, 2)))
        vm = Steps(sem("vec_mixing"), "X0a X0 akt rbk bon " + " ".join(f"X{m} XT{m} c{m - 1}" for m in (1, 2, 3)) +
                   " X4 XT4 XT5 qp2 et g s2 s3 yc yn aff addb yg cout")
        am = Steps(sem("act_mixing"), "lt vtok atok btok ktok T1_1 u1 T1_2 T1_3 T1_4 T1_5 qp1 f0 f1 f2 lnc rsc y lny rsy")
        pm = Steps(sem("pe_mixing"), "lt l akt rbk vtr atr btr ktr u1 bon " + " ".join(f"T1_{m} X{m}" for m in range(1, LEVELS)) +
                   " qp g_ et conv f s2 s3 y mean var")
        gm = Steps(sem("pool_mixing"), "XT0a XT0 m1 u m2 m3 m4 m5 cyb csq sqy")
        vn = Steps(sem("vec_next"), "pp npp zr zk zv kkr den sig cs cse kk kka t1 kf ab0 ab1 bb0 bb1 rk")
        an = Steps(sem("act_next"), "ew ea gT vb0 vb1 Wt Wi We lnk rn")
        pn = Steps(sem("pe_next"), "wa g kks", lead=True)
        gn = Steps(sem("pool_next"), "dr dk dv kk2 kb0 kb1 rt")
        mod_sum, mod_out = sem("modulation_summed"), sem("modulation_columns")
        zeroed = sem("blocks_zeroed")
        m_out = sem("mix_evacuated")
        a2 = Steps(sem("act_output"), "ln exp sqx0 sqx1 ln2 exp2 " + ACT_H + " gw2")
        v2 = Steps(sem("vec_output"), "s2a s2 ga1 ga2 gc1 gc2 sq0 sq1 mw0 mx0 mw1 mx1 xn0 xn1 " + VEC_H)
        p2 = Steps(sem("pe_output"), "gate1 " + " ".join(f"tr{k}" for k in range(0, KC, 2)) + " gate2")
        q_out = sem("queries_evacuated")
        zl_zero = sem("lora_zero_column")
        sc_ps, sc_out = sem("scores_ready"), sem("scores_evacuated")
        vr = sem("vec_routing")
        ar = sem("act_routing")
        h_ps, h_used = sem("h_rows_ready"), sem("h_rows_used")
        staged, used = sem("indices_staged"), sem("expert_row_used")
        accz = sem("expert_sum_cleared")
        gland = [sem(f"row_landed{s}") for s in range(RING)]
        fin_v, fin_a, gelu_done, wv_done = sem("vec_final"), sem("act_final"), sem("gelu_done"), sem("weights_ready")

        block = ctx.enter_context(nc.Block())
        NADA = VECS * KC

        def tile_of(a, n):
            return a[n] if isinstance(n, int) else a[bass.ds(n, 1)].rearrange("a p n -> p (a n)")

        @block.sync
        def _(sp):
            for s in range(RING):
                sp.dma_start(ring[:, s, :], ada[s]).then_inc(land[s], 16)
            with sp.Fori(1, 2 * KC // RING) as t:
                for s in range(RING):
                    sp.wait_ge(ada_used, t * RING + (s + 1 - RING))
                    sp.dma_start(ring[:, s, :], ada[bass.ds(t * RING + s, 1)].rearrange("a p n -> p (a n)")).then_inc(land[s], 16)
            for m in range(WSLOTS):
                sp.wait_ge(ada_used, 2 * KC - RING + m + 1)
                sp.dma_start(ring[:, m, :], w_in[m]).then_inc(land[m], 16)
            for q in range(2):
                sp.wait_ge(ada_used, 2 * KC - 1 + q)
                sp.dma_start(ring[:, WSLOTS + q, :], ada[2 * KC + q]).then_inc(land[WSLOTS + q], 16)
            for t in range(3):
                m = WSLOTS + t
                sp.wait_ge(w_used, m - WSLOTS + 1)
                sp.dma_start(ring[:, m % WSLOTS, :], w_in[m]).then_inc(land[m % WSLOTS], 16)
            sp.wait_ge(v0.sem, v0.at("sg"))
            sp.wait_ge(p0.sem, p0.at("tr14"))
            sp.dma_start(lw.rearrange("p a b -> p (a b)"), lora_up[0]).then_inc(lw_in, 16)

            def round_loads(i, last):
                for t in range(8):
                    if t < 6 and not last:
                        sp.wait_ge(w_used, i * 6 + (LORA + 6 + t - WSLOTS + 1))
                        s = (LORA + t) % WSLOTS
                        sp.dma_start(ring[:, s, :], tile_of(w_in, i * 6 + (LORA + 6 + t))).then_inc(land[s], 16)
                    if last and t < 6:
                        sp.wait_ge(w_used, LORA + 6 * PAIRS - WSLOTS + t + 1)
                        s = (LORA + t) % WSLOTS
                        sp.dma_start(ring[:, s, :], w_tail[t]).then_inc(land[s], 16)
                    if t < 6 or not last:
                        sp.wait_ge(ada_used, i * 8 + (2 * KC + 2 + t - 1))
                        s = WSLOTS + t % 2
                        sp.dma_start(ring[:, s, :], tile_of(ada, i * 8 + (2 * KC + 2 + t))).then_inc(land[s], 16)
                if not last:
                    sp.wait_ge(pn.sem, (i + 1) * pn.per + pn.at("g") - pn.per)
                    sp.dma_start(lw.rearrange("p a b -> p (a b)"), tile_of(lora_up, i + 1)).then_inc(lw_in, 16)

            with sp.Fori(0, 3) as it:
                for half in range(2):
                    round_loads(it * 2 + half, False)
            round_loads(6, False)
            round_loads(7, True)
            for e in (vm, am, pm, gm):
                sp.wait_ge(e.sem, PAIRS * e.per)
            sp.dma_start(xs[:, :, :], x.rearrange("(b p) n -> p b n", p=P)).then_inc(x_in, 16)
            sp.wait_ge(ada_used, NADA)
            sp.dma_start(ring[:, 6, :], keys).then_inc(keys_in, 16)
            for n in range(6, 32):
                m = LORA + 6 * PAIRS + n
                sp.wait_ge(w_used, m - WSLOTS + 1)
                sp.dma_start(ring[:, m % WSLOTS, :], w_tail[n]).then_inc(land[m % WSLOTS], 16)
            for tb in range(TB):
                sp.wait_ge(fin_v, 2 * (tb + 1))
                sp.dma_start(out[tb * P:(tb + 1) * P, :], xs[:, tb, :]).then_inc(stored, 16)
            sp.wait_ge(stored, 16 * TB)

        @block.gpsimd
        def _(pool):
            nconst = [0]

            def const(ins):
                nconst[0] += 1
                ins.then_inc(consts, 1)

            def after():
                pool.wait_ge(consts, nconst[0])

            for t in (ident, lmask[:, :, :], m0T, bones):
                const(nc.gpsimd.memset(t, 0.0))
            for t in (ones, strict, incl):
                const(nc.gpsimd.memset(t, 1.0))
            const(nc.gpsimd.memset(bmean, 0.0))
            after()
            for v, n in ((1e-6, 0), (64e-5, 1), (1e-12, 2), (0.0, 3)):
                const(nc.gpsimd.memset(cst[:, n:n + 1], v))
            for h in range(2):
                after()
                const(nc.gpsimd.memset(bones[h * 64:h * 64 + 64, h * 64:h * 64 + 64], 1.0))
                const(nc.gpsimd.memset(bmean[h * 64:h * 64 + 64, h * 64:h * 64 + 64], 1.0 / 64))
            after()
            const(nc.gpsimd.affine_select(out=ident, in_=ident, compare_op=ALU.not_equal, fill=1.0, base=0,
                                          pattern=[[-1, P]], channel_multiplier=1))
            for m in range(LEVELS):
                size = 1 << m
                v = lmask[:, m, :].rearrange("p (q r) -> p q r", r=2 * size)[:, :, size:]
                const(nc.gpsimd.memset(v, 1.0))
                after()
                const(nc.gpsimd.affine_select(out=v, in_=v, compare_op=ALU.is_ge, fill=0.0, base=0,
                                              pattern=[[-2 * size, P // (2 * size)], [0, size]], channel_multiplier=1))
                after()
                const(nc.gpsimd.affine_select(out=v, in_=v, compare_op=ALU.is_ge, fill=0.0, base=size - 1,
                                              pattern=[[2 * size, P // (2 * size)], [0, size]], channel_multiplier=-1))
            v = m0T.rearrange("p (q r) -> p q r", r=2)[:, :, 0:1]
            const(nc.gpsimd.affine_select(out=v, in_=v, compare_op=ALU.not_equal, fill=1.0, base=-1,
                                          pattern=[[-2, P // 2], [0, 1]], channel_multiplier=1))
            v = strict.rearrange("p (h r) -> p h r", h=2)
            const(nc.gpsimd.affine_select(out=v, in_=v, compare_op=ALU.is_gt, fill=0.0, base=0,
                                          pattern=[[CH, 2], [1, CH]], channel_multiplier=-1))
            after()
            const(nc.gpsimd.affine_select(out=v, in_=v, compare_op=ALU.is_ge, fill=0.0, base=0,
                                          pattern=[[-CH, 2], [0, CH]], channel_multiplier=1))
            for h in range(2):
                v = incl[h * 64:h * 64 + 64, :]
                after()
                const(nc.gpsimd.affine_select(out=v, in_=v, compare_op=ALU.is_ge, fill=0.0, base=0,
                                              pattern=[[1, CH]], channel_multiplier=-1))
            assert nconst[0] == NCONST, nconst[0]
            after()
            pool.wait_ge(v0.sem, v0.at("reset"))
            for t in (ab, bb, kb, vb):
                nc.gpsimd.memset(t[:, :, :], 0.0).then_inc(zeroed, 1)
            nc.gpsimd.memset(u[:, 0:2], 0.0).then_inc(zeroed, 1)
            pool.wait_ge(zeroed, 5)
            tt = nc.gpsimd.tensor_tensor

            def next_a(j):
                for n, (name, d) in enumerate((("dr", dr), ("dk", dk), ("dv", dv))):
                    pool.wait_ge(z_out, j * 6 + (LORA + n + 1))
                    gn.done(tt(d, z[:, n, 0:T], z[:, n, 1:ZS], ALU.subtract), name)
                pool.wait_ge(vn.sem, vn.at("kkr", j))
                gn.done(tt(kk2, kkr, kkr, ALU.mult), "kk2")

            def next_b(j):
                pool.wait_ge(an.sem, an.at("Wi", j))
                pool.wait_ge(vn.sem, vn.at("kf", j))
                for h in range(2):
                    r = slice(h * 64, h * 64 + 64)
                    pool.wait_ge(gn.sem, gn.at(("kk2", "kb0")[h], j))
                    gn.done(tt(kb[r, :, r], kf[r, :].rearrange("p (c t) -> p c t", c=NCH),
                               Wi[r, :].rearrange("p (c t) -> p c t", c=NCH), ALU.mult), f"kb{h}")
                pool.wait_ge(gn.sem, gn.at("kb1", j))
                gn.done(tt(rt, zr, Wt, ALU.mult), "rt")

            def pool_round(i, last):
                pool.wait_ge(am.sem, am.at("lt", i))
                gm.done(tt(XT[:, :, :], LT[:, :, :], lmask[:, 0:1, :].broadcast_to([P, NCH, P]), ALU.mult), "XT0a")
                pool.wait_ge(gm.sem, gm.at("XT0a", i))
                gm.done(tt(XT[:, :, :], XT[:, :, :], ident.rearrange("p (a b) -> p a b", a=1).broadcast_to([P, NCH, P]), ALU.add), "XT0")
                for m in range(1, LEVELS):
                    if m > 2:
                        pool.wait_ge(pm.sem, pm.at(f"T1_{m - 2}", i))
                    gm.done(tt(LTm[m % 2][:, :, :], LT[:, :, :], lmask[:, m:m + 1, :].broadcast_to([P, NCH, P]), ALU.mult), f"m{m}")
                    if m == 1:
                        pool.wait_ge(z_out, i * 6 + (LORA + 6))
                        gm.done(tt(u[:, 2:], z[:, C, 1:ZS], z[:, X_, 1:ZS], ALU.mult), "u")
                    if m == 5:
                        pool.wait_ge(vm.sem, vm.at("c2", i))
                        gm.done(tt(cy, cy, z[:, B, 1:ZS], ALU.mult), "cyb")
                        pool.wait_ge(gm.sem, gm.at("cyb", i))
                        gm.done(tt(csq, cy, cy, ALU.mult), "csq")
                if not last:
                    next_a(i + 1)
                pool.wait_ge(vm.sem, vm.at("yc", i))
                gm.done(tt(y, yc, yc, ALU.mult), "sqy")
                if not last:
                    next_b(i + 1)

            next_a(0)
            next_b(0)
            with pool.Fori(0, 3) as it:
                for half in range(2):
                    pool_round(it * 2 + half, False)
            pool_round(6, False)
            pool_round(7, True)
            pool.wait_ge(vr, IDX_AT[0])
            pool.wait_ge(sc_ps, 2 * 4)
            nc.gpsimd.tensor_copy(i32(stage[:, 0, :]), i32(idx[:, 0:2])).then_inc(staged, 1)
            pool.sem_inc(used, RING)
            for ph in range(2 * TB):
                if ph == 1:
                    pool.wait_ge(vr, NR)
                table = (expert_u, expert_v)[ph % 2]
                with pool.Fori(0, KTOP // 16) as t:
                    for g in range(8):
                        n = ph * KTOP + 2 * g
                        pool.wait_ge(staged, t * 8 + (ph * KTOP // 2 + g + 1))
                        pool.wait_ge(used, t * 16 + (n + 2))
                        nc.gpsimd.tensor_copy(i32(stage[:, (g + 1) % 8, :]), i32(idx)[:, bass.ds(t * 16 + (n + 2), 2)]).then_inc(staged, 1)
                        for j in range(2):
                            s = (2 * g + j) % RING
                            nc.gpsimd.indirect_dma_start(
                                out=ring[:, s, :], out_offset=None, in_=table[:, :],
                                in_offset=bass.IndirectOffsetOnAxis(ap=i32(stage[:, g, :])[:, j:j + 1], axis=0)).then_inc(gland[s], 16)

        def ring_junk(b):
            return yT.rearrange("p a b -> p (a b)")[:, b * D:(b + 1) * D]

        @block.scalar
        def _(act):
            act.dma_start(colp, cols).then_inc(cols_in, 16)
            act.dma_start(xn[:, :, :], x.rearrange("(b p) n -> p b n", p=P)).then_inc(x_in, 16)
            act.wait_ge(cols_in, 16)
            a0.done(nc.scalar.activation(tmp16, colp[:, C_C:C_C + KC], ACT.Exp, scale=-1.0), "expc")
            act.wait_ge(x_in, 16)
            for b in range(TB):
                a0.done(nc.scalar.activation(ring_junk(b), xn[:, b, :], ACT.Square, accum_out=ss[:, b:b + 1]), f"sq{b}")
            act.wait_ge(consts, NCONST)
            act.wait_ge(a0.sem, a0.at("sq1"))
            a0.done(nc.scalar.activation(lns[:, 0:2], ss[:, 0:2], ACT.Ln, bias=cst[:, 0:1], scale=1.0 / D), "ln")
            act.wait_ge(a0.sem, a0.at("ln"))
            a0.done(nc.scalar.activation(rstd[:, 0:2], lns[:, 0:2], ACT.Exp, scale=-0.5), "exp")
            act.wait_ge(v0.sem, v0.at("s1b"))
            for k in ACT_K:
                act.wait_ge(p0.sem, p0.at(f"tr{k - k % 2}"))
                a0.done(nc.scalar.activation(hT[:, k, :], bank((k // 2) % 4, k % 2 * T, k % 2 * T + T), ACT.Identity,
                                             bias=modc[:, 1, k:k + 1], scale=s1c[:, k:k + 1]), f"h{k}")

            def z_copy(m, dst):
                act.wait_ge(w_used, m + 1)
                nc.scalar.activation(dst, bank(6 + z_bank[0] % 2, 0, T), ACT.Copy).then_inc(z_out, 1)
                z_bank[0] += 1

            z_bank = [0]
            for n in range(LORA):
                z_copy(n, zl[:, n, 1:ZS])
            act.wait_ge(v0.sem, v0.at("zero"))
            for n in range(3):
                z_copy(LORA + n, z[:, n, 1:ZS])
            act.wait_ge(v0.sem, v0.at("ml2"))
            a0.done(nc.scalar.activation(tz[0:64, :], ml[0:64, 0, :], ACT.Tanh), "tanh")
            a0.done(nc.scalar.activation(tz[64:P, :], ml[64:P, 0, :], ACT.Copy), "za")
            a0.done(nc.scalar.activation(sgz[:, :, :], ml[:, 1:3, :], ACT.Exp, scale=-1.0), "eg")
            nc.scalar.preload_act_table_set("natural_log_exp_and_others")
            A = nc.scalar.activation
            flat = lambda v: v.rearrange("p a b -> p (a b)")

            def next_a(j, par):
                act.wait_ge(pn.sem, pn.at("wa", j))
                act.wait_ge(vn.sem, vn.at("npp", j))
                an.done(A(ewa[:, 0, :], bank(0, 0, T), ACT.Exp, bias=npp[:, W0:W0 + 1], scale=-1.0), "ew")
                an.done(A(ewa[:, 1, :], bank(0, T), ACT.Exp, bias=npp[:, A0:A0 + 1], scale=-1.0), "ea")
                act.wait_ge(pn.sem, pn.at("g", j))
                an.done(A(gT[par], bank(1, 0, T), ACT.Copy), "gT")
                act.wait_ge(vn.sem, vn.at("zv", j))
                for h in range(2):
                    r = slice(h * 64, h * 64 + 64)
                    an.done(A(vb[r, :, r], zv[r, :].rearrange("p (c t) -> p c t", c=NCH), ACT.Copy), f"vb{h}")

            def next_b(j):
                act.wait_ge(vn.sem, vn.at("cs", j))
                an.done(A(Wt, cs, ACT.Exp, scale=-DECAY), "Wt")
                an.done(A(Wi, cs, ACT.Exp, scale=DECAY), "Wi")
                act.wait_ge(vn.sem, vn.at("cse", j))
                an.done(A(We, cse, ACT.Exp, scale=-DECAY), "We")
                act.wait_ge(pn.sem, pn.at("kks", j))
                an.done(A(rn, bank(1, 0, T), ACT.Ln, bias=cst[:, 2:3]), "lnk")
                act.wait_ge(an.sem, an.at("lnk", j))
                an.done(A(rn, rn, ACT.Exp, scale=-0.5), "rn")

            def act_round(i, par, last):
                tiles = [0]

                def copies(point):
                    while not last and tiles[0] < TILES_AT[point]:
                        t = tiles[0]
                        if t == 3:
                            act.wait_ge(gm.sem, gm.at("cyb", i))
                        z_copy(i * 6 + (LORA + 6 + t), z[:, t, 1:ZS])
                        tiles[0] += 1

                def step(name, out, in_, func, **kw):
                    am.done(A(out, in_, func, **kw), name)

                act.wait_ge(pm.sem, pm.at("lt", i))
                step("lt", flat(LT), bank(2), ACT.Copy)
                act.wait_ge(pm.sem, pm.at("vtr", i))
                step("vtok", flat(vtok), bank(0), ACT.Copy)
                act.wait_ge(pm.sem, pm.at("atr", i))
                step("atok", UA[:, :, 1, :], bank3(1, NCH), ACT.Copy)
                act.wait_ge(pm.sem, pm.at("btr", i))
                step("btok", flat(btok), bank(0), ACT.Copy)
                act.wait_ge(pm.sem, pm.at("ktr", i))
                step("ktok", flat(ktok), bank(1), ACT.Copy)
                for m in range(1, LEVELS):
                    act.wait_ge(pm.sem, pm.at(f"T1_{m}", i))
                    step(f"T1_{m}", flat(T1), bank(2), ACT.Copy)
                    if m == 1:
                        step("u1", UA[:, :, 0, :], bank3(5, NCH), ACT.Copy)
                    copies(f"T1_{m}")
                act.wait_ge(pm.sem, pm.at("qp", i))
                step("qp1", QPb[:, 0:2, :, :].rearrange("p a b c -> p (a b c)"), bank(0), ACT.Copy)
                copies("qp")
                act.wait_ge(pm.sem, pm.at("f", i))
                for c in range(3):
                    w = (c + 1) * CH - 1
                    step(f"f{c}", Fw[:, c, :], bank(4, c * P, c * P + P), ACT.Copy, scale=Wt[:, w:w + 1])
                step("lnc", crs, bank(1, 0, T), ACT.Ln, bias=cst[:, 0:1])
                act.wait_ge(am.sem, am.at("lnc", i))
                step("rsc", crs, crs, ACT.Exp, scale=-0.5)
                copies("f")
                act.wait_ge(pm.sem, pm.at("y", i))
                step("y", y, bank(5, 0, T), ACT.Copy)
                copies("y")
                if not last:
                    next_a(i + 1, 1 - par)
                copies("wa")
                act.wait_ge(pm.sem, pm.at("var", i))
                step("lny", rsy, bank(5, 0, T), ACT.Ln, bias=cst[:, 1:2])
                act.wait_ge(am.sem, am.at("lny", i))
                step("rsy", rsy, rsy, ACT.Exp, scale=-0.5)
                if not last:
                    next_b(i + 1)
                copies("end")

            next_a(0, 0)
            next_b(0)
            for n in range(3, 6):
                z_copy(LORA + n, z[:, n, 1:ZS])
            with act.Fori(0, 3) as it:
                for half in range(2):
                    act_round(it * 2 + half, half, False)
            act_round(6, 0, False)
            act_round(7, 1, True)
            for g in range(4):
                act.wait_ge(w_used, WOUT + 4 * (g + 1))
                for b in range(TB):
                    nc.scalar.activation(mixrow[:, b, g * GROUP:(g + 1) * GROUP], bank(2 * (g % 2) + b), ACT.Copy).then_inc(m_out, 1)
                    if g or b:
                        act.wait_ge(m_out, 4 * g + 2 * b)
                    nc.scalar.activation(junk[:, 0:GROUP], bank(2 * (g % 2) + b), ACT.Square, accum_out=ss[:, b * 4 + g:b * 4 + g + 1]).then_inc(m_out, 1)
            act.wait_ge(v2.sem, v2.at("sq1"))
            a2.done(nc.scalar.activation(lns[:, 2:4], ss[:, 8:10], ACT.Ln, bias=cst[:, 0:1], scale=1.0 / D), "ln")
            act.wait_ge(a2.sem, a2.at("ln"))
            a2.done(nc.scalar.activation(rstd[:, 2:4], lns[:, 2:4], ACT.Exp, scale=-0.5), "exp")
            for b in range(TB):
                act.wait_ge(v2.sem, v2.at(f"mx{b}"))
                act.wait_ge(a2.sem, a2.at("exp" if b == 0 else "sqx0"))
                a2.done(nc.scalar.activation(ff, xs[:, b, :], ACT.Square, accum_out=ss[:, 10 + b:11 + b]), f"sqx{b}")
            act.wait_ge(a2.sem, a2.at("sqx1"))
            a2.done(nc.scalar.activation(lns[:, 4:6], ss[:, 10:12], ACT.Ln, bias=cst[:, 0:1], scale=1.0 / D), "ln2")
            act.wait_ge(a2.sem, a2.at("ln2"))
            a2.done(nc.scalar.activation(rstd[:, 4:6], lns[:, 4:6], ACT.Exp, scale=-0.5), "exp2")
            for k in ACT_K:
                act.wait_ge(p2.sem, p2.at(f"tr{k - k % 2}"))
                a2.done(nc.scalar.activation(h2T[:, k, :], bank((k // 2) % 4, k % 2 * T, k % 2 * T + T), ACT.Identity,
                                             bias=modc[:, 3, k:k + 1], scale=s2c[:, k:k + 1]), f"h{k}")
            act.wait_ge(p2.sem, p2.at("gate2"))
            a2.done(nc.scalar.activation(gw2, ps[:, 2048:4096], ACT.Copy), "gw2")
            def softmax(g):
                for b in range(TB):
                    act.wait_ge(vr, GATE_AT[2 * g + b])
                    gv = gate[:, b, g * 2 * TOPK:(g + 1) * 2 * TOPK]
                    nc.scalar.activation(gv, gv, ACT.Exp).then_inc(ar, 1)

            for g in range(4):
                act.wait_ge(w_used, WOUT + 16 + 4 * (g + 1))
                for h in range(2):
                    nc.scalar.activation(qT[:, 4 * g + 2 * h:4 * g + 2 * h + 2, :], bank3(2 * (g % 2) + h, 2), ACT.Copy).then_inc(q_out, 1)
                for b in range(TB):
                    act.wait_ge(sc_ps, 2 * g + b + 1)
                    nc.scalar.activation(scores[b][:, 4 * g:4 * g + 4, :], bank3(4 + 2 * (g % 2) + b, 4), ACT.Copy).then_inc(sc_out, 1)
                if g:
                    softmax(g - 1)
            softmax(3)
            for b in range(TB):
                act.wait_ge(used, RING + (2 * b + 1) * KTOP)
                nc.scalar.activation(wv[:, b, :], actv[:, b, :], ACT.Gelu).then_inc(gelu_done, 1)
                act.wait_ge(used, RING + (2 * b + 2) * KTOP)
                nc.scalar.activation(junk, ps[:, 2048:4096], ACT.Square, accum_out=ss[:, 12 + b:13 + b]).then_inc(fin_a, 1)
                act.wait_ge(fin_a, 3 * b + 1)
                nc.scalar.activation(lns[:, 12 + b:13 + b], ss[:, 12 + b:13 + b], ACT.Ln, bias=cst[:, 0:1], scale=1.0 / D).then_inc(fin_a, 1)
                act.wait_ge(fin_a, 3 * b + 2)
                nc.scalar.activation(rstd[:, 12 + b:13 + b], lns[:, 12 + b:13 + b], ACT.Exp, scale=-0.5).then_inc(fin_a, 1)

        @block.tensor
        def _(pe):
            mm = nc.tensor.matmul

            def columns(v, out_bank, at):
                for k in range(KC):
                    last = mm(bank(out_bank, at + k, at + k + 1), v[:, k * P:(k + 1) * P], ones[:, 0:1], start=True, stop=True)
                return last

            pe.wait_ge(consts, NCONST)
            for v, name in ((acc, "scale1"), (acc1, "shift1")):
                pe.wait_ge(ada_used, KC if name == "scale1" else 2 * KC)
                p0.done(columns(v, 7, 0 if name == "scale1" else KC), name)

            def turn(src, st, v, a):
                for k in range(0, KC, 2):
                    if k >= 8:
                        e = a if k // 2 % 2 == 0 else v
                        pe.wait_ge(e.sem, e.at(f"h{k - 7}"))
                    for kk in range(2):
                        for b in range(TB):
                            last = nc.tensor.transpose(bank((k // 2) % 4, kk * T + b * P, kk * T + b * P + P),
                                                       src[:, b, (k + kk) * P:(k + kk + 1) * P], ident)
                    st.done(last, f"tr{k}")

            pe.wait_ge(v0.sem, v0.at("xn1"))
            turn(xn, p0, v0, a0)

            def quarter(slot, b, q):
                w = ring[:, slot, :].rearrange("p (a b) -> p a b", a=KC)
                for k in range(4 * q, 4 * q + 4):
                    last = mm(bank(b, 0, T), w[:, k, :], hT[:, k, :], start=(k == 0), stop=(k == KC - 1))
                return last

            pe.wait_ge(a0.sem, a0.at("h13"))
            pe.wait_ge(v0.sem, v0.at("h15"))

            def whole(m):
                pe.wait_ge(land[m % WSLOTS], 16 * (2 * KC // RING + m // WSLOTS + 1))
                if m >= 2:
                    pe.wait_ge(z_out, m - 1)
                for q in range(4):
                    last = quarter(m % WSLOTS, 6 + m % 2, q)
                last.then_inc(w_used, 1)

            for m in range(LORA + 3):
                whole(m)
            pe.sem_inc(pn.sem, pn.lead)

            def next_a(j):
                pe.wait_ge(lw_in, j * 16 + 16)
                mm(bank(0, 0, T), lw[:, 0, :], tz, start=True, stop=True)
                pn.done(mm(bank(0, T), lw[:, 1, :], tz, start=True, stop=True), "wa")
                mm(bank(1, 0, T), lw[:, 2, :], sgz[:, 0, :], start=True, stop=False)
                pn.done(mm(bank(1, 0, T), lw[:, 3, :], sgz[:, 1, :], start=False, stop=True), "g")

            def next_b(j):
                pe.wait_ge(gn.sem, gn.at("kk2", j))
                pe.wait_ge(an.sem, an.at("gT", j))
                pn.done(mm(bank(1, 0, T), bones, kk2, start=True, stop=True), "kks")

            def pe_round(i, par, last_round):
                S = pm
                state = [0]

                def fill(point):
                    while not last_round and state[0] < FILL_AT[point]:
                        t, q = divmod(state[0], 4)
                        slot, b = (LORA + t) % WSLOTS, 6 + (LORA + t) % 2
                        if q == 0:
                            pe.wait_ge(land[slot], i * 16 + 16 * (2 * KC // RING + (LORA + 6 + t) // WSLOTS + 1))
                            pe.wait_ge(z_out, i * 6 + (LORA + 6 + t - 1))
                        last = quarter(slot, b, q)
                        if q == 3:
                            last.then_inc(w_used, 1)
                        state[0] += 1

                def blocks(b, l, r, name):
                    for c in range(NCH):
                        last = mm(bank(b, c * P, c * P + P), l[:, c, :], r[:, c, :], start=True, stop=True)
                    S.done(last, name)

                def turned(b, t, name):
                    for c in range(NCH):
                        last = nc.tensor.transpose(bank(b, c * P, c * P + P), t[:, c, :], ident)
                    S.done(last, name)

                pe.wait_ge(vn.sem, vn.at("bb1", i))
                blocks(2, bb, ab, "lt")
                blocks(3, ab, bb, "l")
                pe.wait_ge(gn.sem, gn.at("rt", i))
                blocks(4, kb, ab, "akt")
                for c in range(NCH):
                    mm(bank(5, c * P, c * P + CH), bb[:, c, :], rt[:, c * CH:(c + 1) * CH], start=True, stop=True)
                    last = mm(bank(5, c * P + CH, c * P + P), kb[:, c, :], rt[:, c * CH:(c + 1) * CH], start=True, stop=True)
                S.done(last, "rbk")
                pe.wait_ge(an.sem, an.at("rn", i))
                turned(0, vb, "vtr")
                turned(1, ab, "atr")
                fill("atr")
                pe.wait_ge(am.sem, am.at("vtok", i))
                turned(0, bb, "btr")
                pe.wait_ge(am.sem, am.at("atok", i))
                turned(1, kb, "ktr")
                fill("ktr")
                pe.wait_ge(vm.sem, vm.at("rbk", i))
                blocks(5, AKT, vtok, "u1")
                pe.wait_ge(am.sem, am.at("btok", i))
                pe.wait_ge(vn.sem, vn.at("rk", i))
                S.done(mm(bank(0, 0, T), bones, rk, start=True, stop=True), "bon")
                for m in range(1, LEVELS):
                    pe.wait_ge(gm.sem, gm.at(f"m{m}", i))
                    pe.wait_ge(vm.sem, vm.at("X0" if m == 1 else f"XT{m - 1}", i))
                    blocks(2, LTm[m % 2], X, f"T1_{m}")
                    fill(f"T1_{m}")
                    pe.wait_ge(am.sem, am.at(f"T1_{m}", i))
                    if m < LEVELS - 1:
                        for c in range(NCH):
                            mm(bank(3, c * P, c * P + P), XT[:, c, :], T1[:, c, :], start=True, stop=True)
                    blocks(4, T1, XT, f"X{m}")
                    fill(f"X{m}")
                pe.wait_ge(vm.sem, vm.at("XT5", i))
                pe.wait_ge(am.sem, am.at("ktok", i))
                for c in range(NCH):
                    last = mm(bank(c // 2, (c % 2) * T, (c % 2) * T + T), XT[:, c, :], UA[:, c, :, :].rearrange("p a b -> p (a b)"), start=True, stop=True)
                S.done(last, "qp")
                fill("qp")
                pe.wait_ge(vm.sem, vm.at("qp2", i))
                pe.wait_ge(am.sem, am.at("qp1", i))
                for c in range(1, NCH):
                    last = mm(bank(2, c * CH, c * CH + CH), QPb[:, c, 1, :], RBK[:, c, 0, :], start=True, stop=True)
                S.done(last, "g_")
                for c in (1, 2):
                    last = mm(bank(5, (c - 1) * P, c * P), QPb[:, c, 1, :], btok[:, c, :], start=True, stop=True)
                S.done(last, "et")
                pe.wait_ge(gm.sem, gm.at("csq", i))
                S.done(mm(bank(1, 0, T), bmean, csq, start=True, stop=True), "conv")
                for c in range(3):
                    mm(bank(4, c * P, c * P + P), btok[:, c, :], QPb[:, c, 0, :], start=True, stop=False)
                    last = mm(bank(4, c * P, c * P + P), ktok[:, c, :], vtok[:, c, :], start=False, stop=True)
                S.done(last, "f")
                fill("f")
                pe.wait_ge(am.sem, am.at("f2", i))
                pe.wait_ge(vm.sem, vm.at("et", i))
                S.done(mm(bank(3, 0, P), ET[:, 0, :], Fw[:, 0, :], start=True, stop=True), "s2")
                fill("s2")
                pe.wait_ge(vm.sem, vm.at("s2", i))
                S.done(mm(bank(3, P, 2 * P), ET[:, 1, :], St[:, 0, :], start=True, stop=True), "s3")
                fill("s3")
                pe.wait_ge(vm.sem, vm.at("s3", i))
                for c in range(NCH):
                    o = bank(5, c * CH, c * CH + CH)
                    if c:
                        mm(o, Fw[:, 0, :] if c == 1 else St[:, c - 2, :], Gt[:, c * CH:(c + 1) * CH], start=True, stop=False)
                    mm(o, QPb[:, c, 0, :], RBK[:, c, 0, :], start=(c == 0), stop=False)
                    last = mm(o, vtok[:, c, :], RBK[:, c, 1, :], start=False, stop=True)
                S.done(last, "y")
                if par:
                    pe.wait_ge(ada_used, i * 8 + (2 * KC + 8))
                    columns(acc, 3, 0).then_inc(mod_sum, 1)
                fill("y")
                pe.wait_ge(am.sem, am.at("y", i))
                S.done(mm(bank(4, 0, T), bmean, y, start=True, stop=True), "mean")
                if not last_round:
                    pe.wait_ge(am.sem, am.at("lnc", i))
                    next_a(i + 1)
                fill("wa")
                pe.wait_ge(gm.sem, gm.at("sqy", i))
                S.done(mm(bank(5, 0, T), bmean, y, start=True, stop=True), "var")
                if not last_round:
                    next_b(i + 1)
                fill("end")

            next_a(0)
            next_b(0)
            for m in range(LORA + 3, LORA + 6):
                whole(m)
            with pe.Fori(0, 3) as it:
                for half in range(2):
                    pe_round(it * 2 + half, half, False)
            pe_round(6, 0, False)
            pe_round(7, 1, True)

            def groups(g, b0):
                for j in range(TILES):
                    m = WOUT + 16 + 4 * g + j
                    pe.wait_ge(land[m % WSLOTS], 16 * (2 * KC // RING + m // WSLOTS + 1))
                    w = ring[:, m % WSLOTS, :].rearrange("p (a b) -> p a b", a=KT)
                    for kk in range(KT):
                        k = j * KT + kk
                        for s in range(4):
                            last = mm(bank(b0 + s // 2, (s % 2) * T, (s % 2) * T + T), w[:, kk, s * P:(s + 1) * P], h2T[:, k, :],
                                      start=(k == 0 and s % 2 == 0), stop=(k == KC - 1), skip_group_check=True)
                    last.then_inc(w_used, 1)

            def rows(col, b0):
                for k in range(KC):
                    last = mm(bank(b0 + k // 4, k % 4 * P, k % 4 * P + P), col[:, k:k + 1].broadcast_to([P, P]), ident, start=True, stop=True)
                return last
            pe.wait_ge(v2.sem, v2.at("gc2"))
            p2.done(rows(gcol[:, 0, :], 4), "gate1")
            pe.wait_ge(vm.sem, PAIRS * vm.per)
            pe.wait_ge(am.sem, PAIRS * am.per)
            for g in range(4):
                if g >= 2:
                    pe.wait_ge(m_out, 4 * (g - 1))
                for j in range(TILES):
                    m = WOUT + 4 * g + j
                    pe.wait_ge(land[m % WSLOTS], 16 * (2 * KC // RING + m // WSLOTS + 1))
                    w = ring[:, m % WSLOTS, :].rearrange("p (a b) -> p a b", a=KT)
                    for kk in range(KT):
                        k = j * KT + kk
                        for b in range(TB):
                            last = mm(bank(2 * (g % 2) + b), yT[:, k, b * P:(b + 1) * P], w[:, kk, :], start=(k == 0), stop=(k == KC - 1))
                    last.then_inc(w_used, 1)
            pe.wait_ge(m_out, 16)
            pe.wait_ge(v2.sem, v2.at("xn1"))
            turn(mixrow, p2, v2, a2)
            p2.done(rows(gcol[:, 1, :], 4), "gate2")
            pe.wait_ge(a2.sem, a2.at("h13"))
            pe.wait_ge(v2.sem, v2.at("h15"))
            kv = ring[:, 6, :].rearrange("p (a b) -> p a b", a=KC)

            def score(g):
                pe.wait_ge(q_out, 2 * (g + 1))
                if g == 0:
                    pe.wait_ge(keys_in, 16)
                    pe.wait_ge(a2.sem, a2.at("gw2"))
                for b in range(TB):
                    if g >= 2:
                        pe.wait_ge(sc_out, 2 * (g - 2) + b + 1)
                    for c in range(4 * g, 4 * g + 4):
                        last = mm(bank(4 + 2 * (g % 2) + b, (c % 4) * P, (c % 4) * P + P), qT[:, c, b * P:(b + 1) * P], kv[:, c, :], start=True, stop=True)
                    last.then_inc(sc_ps, 1)

            for g in range(4):
                if g >= 2:
                    pe.wait_ge(q_out, 2 * (g - 1))
                groups(g, 2 * (g % 2))
                score(g)
            for b in range(TB):
                if b:
                    pe.wait_ge(used, RING + KTOP)
                for k in range(KC):
                    last = nc.tensor.transpose(ps[:, k * P:(k + 1) * P], h2T[:, k, b * P:(b + 1) * P], ident)
                last.then_inc(h_ps, 1)

        @block.vector
        def _(dve):
            V = nc.vector
            tt, ts, stt = V.tensor_tensor, V.tensor_scalar, V.scalar_tensor_tensor
            dve.wait_ge(a0.sem, a0.at("expc"))
            v0.done(ts(tmp16, tmp16, 1.0, None, ALU.add), "den")
            dve.wait_ge(v0.sem, v0.at("den"))
            v0.done(V.reciprocal(tmp16, tmp16), "rec")
            dve.wait_ge(v0.sem, v0.at("rec"))
            v0.done(tt(silu_c, tmp16, colp[:, C_C:C_C + KC], ALU.mult), "silu")
            dve.wait_ge(v0.sem, v0.at("silu"))

            def ada_tile(dst, slot, k):
                if k == 0:
                    ins = ts(dst, ring[:, slot, :], silu_c[:, 0:1], None, ALU.mult)
                else:
                    ins = stt(dst, ring[:, slot, :], silu_c[:, k:k + 1], dst, ALU.mult, ALU.add)
                ins.then_inc(ada_used, 1)

            for v, dst in enumerate((acc, acc1)):
                for k in range(KC):
                    dve.wait_ge(land[k % RING], v * 32 + 16 * (k // RING + 1))
                    if k:
                        dve.wait_ge(ada_used, v * KC + k)
                    ada_tile(dst, k % RING, k)
            dve.wait_ge(p0.sem, p0.at("shift1"))
            v0.done(tt(modc[:, 0, :], bank(7, 0, KC), colp[:, C_AB:C_AB + KC], ALU.add), "m0")
            v0.done(tt(modc[:, 1, :], bank(7, KC, 2 * KC), colp[:, C_AB + KC:C_AB + 2 * KC], ALU.add), "m1")
            dve.wait_ge(v0.sem, v0.at("m1"))
            v0.done(stt(s1c, modc[:, 0, :], 1.0, colp[:, C_PMW:C_PMW + KC], ALU.add, ALU.mult), "s1")
            dve.wait_ge(v0.sem, v0.at("s1"))
            v0.done(V.tensor_copy(tmp16, s1c), "s1b")
            dve.wait_ge(a0.sem, a0.at("exp"))
            for b in range(TB):
                v0.done(ts(xn[:, b, :], xn[:, b, :], rstd[:, b:b + 1], None, ALU.mult), f"xn{b}")
            for k in VEC_K:
                dve.wait_ge(p0.sem, p0.at(f"tr{k - k % 2}"))
                v0.done(ts(hT[:, k, :], bank((k // 2) % 4, k % 2 * T, k % 2 * T + T), s1c[:, k:k + 1], modc[:, 1, k:k + 1], ALU.mult, ALU.add), f"h{k}")
            v0.done(V.memset(z[:, :, 0:1], 0.0), "zero")
            for n in range(LORA):
                dve.wait_ge(z_out, n + 1)
                if n == 0:
                    V.memset(zl[:, :, 0:1], 0.0).then_inc(zl_zero, 1)
                    dve.wait_ge(zl_zero, 1)
                v0.done(tt(dl[:, n, :], zl[:, n, 0:T], zl[:, n, 1:ZS], ALU.subtract), f"dl{n}")
            for n in range(LORA):
                dve.wait_ge(v0.sem, v0.at(f"dl{n}"))
                v0.done(stt(ml[:, n, :], dl[:, n, :], colp[:, C_ML + n:C_ML + n + 1], zl[:, n, 1:ZS], ALU.mult, ALU.add), f"ml{n}")
            dve.wait_ge(a0.sem, a0.at("eg"))
            v0.done(ts(sgz[:, :, :], sgz[:, :, :], 1.0, None, ALU.add), "eg1")
            dve.wait_ge(v0.sem, v0.at("eg1"))
            v0.done(V.reciprocal(sgz[:, :, :], sgz[:, :, :]), "sg")
            v0.done(V.memset(reset, 1.0), "res1")
            dve.wait_ge(v0.sem, v0.at("res1"))
            v0.done(V.memset(reset.rearrange("p (c t) -> p c t", c=NCH)[:, :, 0:1], 0.0), "reset")
            dve.wait_ge(zeroed, 5)
            chunked = lambda v: v.rearrange("p (c t) -> p c t", c=NCH)
            flat = lambda v: v.rearrange("p a b -> p (a b)")
            over = lambda v: v.rearrange("p (a b) -> p a b", a=1).broadcast_to([P, NCH, P])

            def next_a(j, par):
                p_ = pp[par]
                vn.done(V.tensor_copy(p_, colp[:, bass.ds(j * PC + C_PP, PC)] if not isinstance(j, int)
                                      else colp[:, C_PP + j * PC:C_PP + (j + 1) * PC]), "pp")
                dve.wait_ge(vn.sem, vn.at("pp", j))
                vn.done(ts(npp, p_, -1.0, None, ALU.mult), "npp")
                for n, (name, src, d, mx, o) in enumerate((("zr", "dr", dr, MIX_R, zr), ("zk", "dk", dk, MIX_K, zk), ("zv", "dv", dv, MIX_V, zv))):
                    dve.wait_ge(gn.sem, gn.at(src, j))
                    vn.done(stt(o, d, p_[:, mx:mx + 1], z[:, n, 1:ZS], ALU.mult, ALU.add), name)
                dve.wait_ge(vn.sem, vn.at("zk", j))
                vn.done(ts(kkr, zk, p_[:, K_K:K_K + 1], None, ALU.mult), "kkr")

            def next_b(j):
                dve.wait_ge(an.sem, an.at("ea", j))
                vn.done(ts(flat(ewa), flat(ewa), 1.0, None, ALU.add), "den")
                dve.wait_ge(vn.sem, vn.at("den", j))
                vn.done(V.reciprocal(flat(ewa), flat(ewa)), "sig")
                dve.wait_ge(vn.sem, vn.at("sig", j))
                vn.done(V.tensor_tensor_scan(cs, reset, ewa[:, 0, :], 0.0, ALU.mult, ALU.add), "cs")
                dve.wait_ge(vn.sem, vn.at("cs", j))
                vn.done(tt(cse, cs, ewa[:, 0, :], ALU.subtract), "cse")

            def next_c(j, par):
                p_ = pp[par]
                dve.wait_ge(an.sem, an.at("rn", j))
                vn.done(tt(kk, kkr, rn, ALU.mult), "kk")
                dve.wait_ge(vn.sem, vn.at("kk", j))
                vn.done(tt(kka, kk, ewa[:, 1, :], ALU.mult), "kka")
                vn.done(ts(t1, ewa[:, 1, :], -1.0, p_[:, K_A:K_A + 1], ALU.add, ALU.mult), "t1")
                dve.wait_ge(vn.sem, vn.at("t1", j))
                vn.done(stt(kf, t1, 1.0, zk, ALU.add, ALU.mult), "kf")
                for h in range(2):
                    r = slice(h * 64, h * 64 + 64)
                    vn.done(stt(ab[r, :, r], chunked(kk)[r], -1.0, chunked(We)[r], ALU.mult, ALU.mult), f"ab{h}")
                for h in range(2):
                    r = slice(h * 64, h * 64 + 64)
                    vn.done(tt(bb[r, :, r], chunked(kka)[r], chunked(Wi)[r], ALU.mult), f"bb{h}")
                dve.wait_ge(vn.sem, vn.at("kf", j))
                vn.done(stt(rk, zr, p_[:, R_K:R_K + 1], kf, ALU.mult, ALU.mult), "rk")

            def vec_round(i, par, last):
                S = vm
                p_ = pp[par]
                here = lambda n: S.at(n, i)
                tile = [0]

                def modulation():
                    n = tile[0]
                    k = 8 * par + n
                    dve.wait_ge(land[WSLOTS + n % 2], i * 64 + 16 * (2 * KC // RING + n // 2 + 1))
                    if k:
                        dve.wait_ge(ada_used, i * 8 + (2 * KC + n))
                    ada_tile(acc, WSLOTS + n % 2, k)
                    tile[0] += 1

                dve.wait_ge(pm.sem, pm.at("l", i))
                S.done(tt(X[:, :, :], bank3(3, NCH), over(m0T), ALU.mult), "X0a")
                dve.wait_ge(S.sem, here("X0a"))
                S.done(tt(X[:, :, :], X[:, :, :], over(ident), ALU.add), "X0")
                dve.wait_ge(pm.sem, pm.at("akt", i))
                S.done(tt(AKT[:, :, :], bank3(4, NCH), over(strict), ALU.mult), "akt")
                dve.wait_ge(pm.sem, pm.at("rbk", i))
                S.done(tt(RBK.rearrange("p a b c -> p (a b) c"), bank3(5, 2 * NCH),
                          incl.rearrange("p (a b) -> p a b", a=1).broadcast_to([P, 2 * NCH, CH]), ALU.mult), "rbk")
                modulation()
                dve.wait_ge(pm.sem, pm.at("bon", i))
                S.done(tt(bon, bank(0, 0, T), zv, ALU.mult), "bon")
                for m in range(1, LEVELS):
                    dve.wait_ge(pm.sem, pm.at(f"X{m}", i))
                    if m < LEVELS - 1:
                        S.done(tt(flat(X), bank(3), flat(X), ALU.add), f"X{m}")
                    if m == 1:
                        dve.wait_ge(gm.sem, gm.at("XT0", i))
                    S.done(tt(flat(XT), bank(4), flat(XT), ALU.add), f"XT{m}")
                    if m == 1:
                        dve.wait_ge(gm.sem, gm.at("u", i))
                        S.done(ts(cy, u[:, 0:T], p_[:, CW0:CW0 + 1], None, ALU.mult), "c0")
                    if m in (2, 3):
                        dve.wait_ge(S.sem, here(f"c{m - 2}"))
                        S.done(stt(cy, u[:, m - 1:m - 1 + T], p_[:, CW0 + m - 1:CW0 + m], cy, ALU.mult, ALU.add), f"c{m - 1}")
                    modulation()
                dve.wait_ge(pm.sem, pm.at("qp", i))
                S.done(V.tensor_copy(QPb[:, 2:4, :, :].rearrange("p a b c -> p (a b c)"), bank(1)), "qp2")
                dve.wait_ge(pm.sem, pm.at("et", i))
                S.done(tt(ET[:, :, :], bank(5, 0, 2 * P).rearrange("p (a b) -> p a b", a=2),
                          ident.rearrange("p (a b) -> p a b", a=1).broadcast_to([P, 2, P]), ALU.add), "et")
                S.done(tt(Gt[:, CH:], bank(2, CH, T), rt[:, CH:], ALU.add), "g")
                modulation()
                for c, name in ((1, "s2"), (2, "s3")):
                    dve.wait_ge(pm.sem, pm.at(name, i))
                    w = (c + 1) * CH - 1
                    S.done(stt(St[:, c - 1, :], bank(3, (c - 1) * P, c * P), Wt[:, w:w + 1], Fw[:, c, :], ALU.mult, ALU.add), name)
                modulation()
                assert tile[0] == 8
                if not last:
                    next_a(i + 1, 1 - par)
                dve.wait_ge(pm.sem, pm.at("mean", i))
                S.done(tt(yc, y, bank(4, 0, T), ALU.subtract), "yc")
                if par:
                    dve.wait_ge(mod_sum, mod_count(i))
                    V.tensor_copy(mod_row(i), bank(3, 0, KC)).then_inc(mod_out, 1)
                if not last:
                    next_b(i + 1)
                dve.wait_ge(am.sem, am.at("rsy", i))
                S.done(tt(yc, yc, rsy, ALU.mult), "yn")
                dve.wait_ge(S.sem, here("yn"))
                S.done(ts(yc, yc, p_[:, LN_W:LN_W + 1], p_[:, LN_B:LN_B + 1], ALU.mult, ALU.add), "aff")
                dve.wait_ge(S.sem, here("aff"))
                S.done(tt(yc, yc, bon, ALU.add), "addb")
                dve.wait_ge(S.sem, here("addb"))
                chunk = (lambda n: yT[:, n, :] if isinstance(n, int) else yT[:, bass.ds(n, 1), :].rearrange("p a b -> p (a b)"))
                S.done(tt(chunk(i), yc, gT[par], ALU.mult), "yg")
                S.done(stt(chunk(i + PAIRS), cy, p_[:, CN:CN + 1], crs, ALU.mult, ALU.mult), "cout")
                if not last:
                    next_c(i + 1, 1 - par)

            next_a(0, 0)
            next_b(0)
            next_c(0, 0)
            with dve.Fori(0, 3) as it:
                mod_count = lambda i: it + 1
                mod_row = lambda i: modc[:, bass.ds(it + 2, 1), :].rearrange("p a b -> p (a b)")
                for half in range(2):
                    vec_round(it * 2 + half, half, False)
            mod_count = lambda i: 4
            mod_row = lambda i: modc[:, 5, :]
            vec_round(6, 0, False)
            vec_round(7, 1, True)
            dve.wait_ge(mod_out, 4)
            v2.done(tt(flat(modc[:, 2:6, :]), flat(modc[:, 2:6, :]), colp[:, C_AB + 2 * KC:C_AB + 6 * KC], ALU.add), "s2a")
            dve.wait_ge(v2.sem, v2.at("s2a"))
            v2.done(stt(s2c, modc[:, 4, :], 1.0, colp[:, C_PFW:C_PFW + KC], ALU.add, ALU.mult), "s2")
            v2.done(tt(gcol[:, 0, :], modc[:, 2, :], colp[:, C_PG1:C_PG1 + KC], ALU.mult), "ga1")
            v2.done(tt(gcol[:, 1, :], modc[:, 5, :], colp[:, C_PG2:C_PG2 + KC], ALU.mult), "ga2")
            dve.wait_ge(v2.sem, v2.at("ga2"))
            v2.done(V.tensor_copy(tmp16, gcol[:, 0, :]), "gc1")
            v2.done(V.tensor_copy(silu_c, gcol[:, 1, :]), "gc2")
            dve.wait_ge(m_out, 16)
            for b in range(TB):
                v2.done(V.tensor_reduce(ss[:, 8 + b:9 + b], ss[:, 4 * b:4 * b + 4], AX.X, ALU.add), f"sq{b}")
            dve.wait_ge(a2.sem, a2.at("exp"))
            dve.wait_ge(x_in, 32)
            dve.wait_ge(p2.sem, p2.at("gate1"))
            for b in range(TB):
                v2.done(stt(mixrow[:, b, :], mixrow[:, b, :], rstd[:, 2 + b:3 + b], ps[:, 2048:4096], ALU.mult, ALU.mult), f"mw{b}")
                dve.wait_ge(v2.sem, v2.at(f"mw{b}"))
                v2.done(tt(xs[:, b, :], xs[:, b, :], mixrow[:, b, :], ALU.add), f"mx{b}")
            dve.wait_ge(a2.sem, a2.at("exp2"))
            for b in range(TB):
                v2.done(ts(mixrow[:, b, :], xs[:, b, :], rstd[:, 4 + b:5 + b], None, ALU.mult), f"xn{b}")
            for k in VEC_K:
                dve.wait_ge(p2.sem, p2.at(f"tr{k - k % 2}"))
                v2.done(ts(h2T[:, k, :], bank((k // 2) % 4, k % 2 * T, k % 2 * T + T), s2c[:, k:k + 1], modc[:, 3, k:k + 1], ALU.mult, ALU.add), f"h{k}")
            nr = [0]

            def r(ins):
                nr[0] += 1
                return ins.then_inc(vr, 1)

            def settle():
                dve.wait_ge(vr, nr[0])

            for n in range(TOPK):
                r(V.memset(iota16[:, n:n + 1], float(n)))
            NEG = -3.0e38

            def top16(src, vals, where, rep):
                r(V.max(vals[:, 0:8], src))
                settle()
                r(V.max_index(where[:, 0:8], vals[:, 0:8], src))
                r(V.match_replace(rep, vals[:, 0:8], src, NEG))
                settle()
                r(V.max(vals[:, 8:16], rep))
                settle()
                r(V.max_index(where[:, 8:16], vals[:, 8:16], rep))

            def route(b, g):
                dve.wait_ge(sc_out, 2 * g + b + 1)
                for c in range(4):
                    top16(scores[b][:, 4 * g + c, :], v16[:, c, :], u32(iu[:, c, :]), repl[:, c * NKEYS:(c + 1) * NKEYS])
                settle()
                r(V.tensor_copy(i16[:, :, :], u32(iu[:, :, :])))
                wide = lambda v: v.rearrange("p (a b) -> p a b", b=1).broadcast_to([P, TOPK, TOPK])
                deep = lambda v: v.rearrange("p (a b) -> p a b", a=1).broadcast_to([P, TOPK, TOPK])
                for h in range(2):
                    r(tt(cand[:, h, :].rearrange("p (a b) -> p a b", a=TOPK), wide(v16[:, 2 * h, :]), deep(v16[:, 2 * h + 1, :]), ALU.add))
                settle()
                for h in range(2):
                    top16(cand[:, h, :], topv[:, h, :], u32(pos[:, h, :]), repl[:, h * 256:(h + 1) * 256])
                settle()
                r(ts(u32(hi_u[:, :, :]), u32(pos[:, :, :]), 4, None, ALU.logical_shift_right))
                r(ts(u32(lo_u[:, :, :]), u32(pos[:, :, :]), 15, None, ALU.bitwise_and))
                settle()
                r(V.tensor_copy(hi_f[:, :, :], u32(hi_u[:, :, :])))
                r(V.tensor_copy(lo_f[:, :, :], u32(lo_u[:, :, :])))
                settle()
                gb = gate[:, b, g * 2 * TOPK:(g + 1) * 2 * TOPK].rearrange("p (h k) -> p h k", h=2)
                r(tt(gb, topv[:, :, :], topv[:, :, 0:1].broadcast_to([P, 2, TOPK]), ALU.subtract))
                gates.append(nr[0])
                for half, sel, dst in ((0, hi_f, ei), (1, lo_f, ej)):
                    for h in range(2):
                        r(tt(eq[:, h * TOPK:(h + 1) * TOPK, :], wide(sel[:, h, :]), deep(iota16), ALU.is_equal))
                    settle()
                    for h in range(2):
                        e = eq[:, h * TOPK:(h + 1) * TOPK, :]
                        r(tt(e, e, deep(i16[:, 2 * h + half, :]), ALU.mult))
                    settle()
                    r(V.tensor_reduce(dst.rearrange("p a b -> p (a b)"), eq[:, :, :], AX.X, ALU.add))
                    settle()
                r(stt(ei[:, :, :], ei[:, :, :], float(NKEYS), ej[:, :, :], ALU.mult, ALU.add))
                settle()
                for again in range(2):
                    at = (2 * b + again) * KTOP + g * 2 * TOPK
                    r(V.tensor_copy(i32(idx[:, at:at + 2 * TOPK]), ei.rearrange("p a b -> p (a b)")))
                if g == 3:
                    picked.append(nr[0])

            gates, picked = [], []
            r(V.memset(i32(idx[:, 4 * KTOP:4 * KTOP + 2]), 0))
            for g in range(4):
                for b in range(TB):
                    route(b, g)
            assert tuple(gates) == GATE_AT and tuple(picked) == IDX_AT, (gates, picked)
            dve.wait_ge(ar, 2 * 4)
            for b in range(TB):
                gb = gate[:, b, :].rearrange("p (h k) -> p h k", h=HEADS)
                r(V.tensor_reduce(gsum, gb, AX.X, ALU.add))
                settle()
                r(V.reciprocal(grec, gsum))
                settle()
                r(tt(gb, gb, grec.rearrange("p (a b) -> p a b", b=1).broadcast_to([P, HEADS, TOPK]), ALU.mult))
                settle()
            assert nr[0] == NR, nr[0]
            for b in range(TB):
                dve.wait_ge(h_ps, b + 1)
                with dve.Fori(0, KTOP // 16) as t:
                    for j in range(16):
                        s = j % RING
                        dve.wait_ge(gland[s], t * 32 + 16 * (2 * b * 16 + j // RING + 1))
                        stt(ring[:, s, :], ring[:, s, :], 1.0, ps[:, 0:D], ALU.mult, ALU.mult,
                            accum_out=actv[:, b, bass.ds(t * 16 + j, 1)]).then_inc(used, 1)
                dve.wait_ge(gelu_done, b + 1)
                tt(wv[:, b, :], wv[:, b, :], gate[:, b, :], ALU.mult).then_inc(wv_done, 1)
                V.memset(ps[:, 2048:4096], 0.0).then_inc(wv_done, 1)
                dve.wait_ge(wv_done, 2 * b + 2)
                with dve.Fori(0, KTOP // 16) as t:
                    for j in range(16):
                        s = j % RING
                        dve.wait_ge(gland[s], t * 32 + 16 * ((2 * b + 1) * 16 + j // RING + 1))
                        dve.wait_ge(used, t * 16 + (RING + (2 * b + 1) * KTOP + j))
                        stt(ps[:, 2048:4096], ring[:, s, :], wv[:, b, bass.ds(t * 16 + j, 1)], ps[:, 2048:4096], ALU.mult, ALU.add).then_inc(used, 1)
                dve.wait_ge(fin_a, 3 * b + 3)
                stt(ff, ps[:, 2048:4096], rstd[:, 12 + b:13 + b], gw2, ALU.mult, ALU.mult).then_inc(fin_v, 1)
                dve.wait_ge(fin_v, 2 * b + 1)
                tt(xs[:, b, :], xs[:, b, :], ff, ALU.add).then_inc(fin_v, 1)


NCONST = 40
WOUT = LORA + 6 * PAIRS
FILL_AT = dict(atr=1, ktr=2, T1_1=3, X1=4, T1_2=5, X2=6, T1_3=7, X3=8, T1_4=9, X4=10, T1_5=11, X5=12,
               qp=13, f=14, s2=15, s3=16, y=17, wa=19, end=24)
TILES_AT = {"T1_1": 0, "T1_2": 1, "T1_3": 1, "T1_4": 2, "T1_5": 2, "qp": 3, "f": 3, "y": 4, "wa": 4, "end": 6}
GATE_AT = (55, 106, 157, 208, 259, 310, 361, 412)
IDX_AT = (374, 425)
NR = 431


def kernel(x, c, ada_w, ada_b, pre_mix_w, post_mix_w, w_in, rwkv_mix, w0, w_up, a0, a_up, g_up, k_k, k_a, r_k,
           ln_x_w, ln_x_b, conv_w, conv_norm_w, w_out, pre_ffn_w, post_ffn_w, w_q, sub_keys_1, sub_keys_2,
           expert_u, expert_v):
    import concourse.bacc as bacc
    from concourse.bass_utils import run_bass_kernel_spmd as run

    f = lambda a: np.asarray(a)
    as_cols = lambda v: v.reshape(-1, P).T
    RW = 1024
    lora0 = 3 * RW
    wi = f(w_in)[0]
    ab = f(ada_b)[0].reshape(VECS, D)
    mix = f(rwkv_mix)[0]
    lmix = np.zeros(384, np.float32)
    lmix[:288] = mix[lora0:lora0 + 288]
    per = [mix[0:RW], mix[RW:2 * RW], mix[2 * RW:3 * RW], f(w0)[0], f(a0)[0], f(k_k)[0], f(k_a)[0], f(r_k)[0].reshape(-1),
           f(ln_x_w)[0], f(ln_x_b)[0], f(conv_w)[0, 0], f(conv_w)[0, 1], f(conv_w)[0, 2], f(conv_norm_w)[0],
           np.zeros(RW, np.float32), np.zeros(RW, np.float32)]
    pp = np.stack([as_cols(v) for v in per], 2).reshape(P, PAIRS * PC)
    cols = np.concatenate([as_cols(f(pre_mix_w)[0]), as_cols(f(pre_ffn_w)[0]), as_cols(f(post_mix_w)[0]), as_cols(f(post_ffn_w)[0]),
                           *(as_cols(ab[v]) for v in VEC_ORDER), as_cols(f(c)[0]), as_cols(lmix), np.zeros((P, 1), np.float32), pp], 1)
    ada = f(ada_w)[0].reshape(KC, P, VECS, D).transpose(2, 0, 1, 3)[list(VEC_ORDER)].reshape(VECS * KC, P, D)

    def tiles(w, width):
        n = w.shape[1] // width
        return w.reshape(TILES, KT, P, n, width).transpose(3, 0, 2, 1, 4).reshape(n * TILES, P, KT * width)

    lw = np.zeros((D, 384), np.float32)
    lw[:, :288] = wi[:, lora0:lora0 + 288]
    six = np.concatenate([wi[:, :lora0], wi[:, lora0 + 288:]], 1).reshape(D, 6, PAIRS, P).transpose(0, 2, 1, 3).reshape(D, 6 * PAIRS * P)
    w_main = np.concatenate([lw, six], 1).reshape(KC, P, WOUT, P).transpose(2, 1, 0, 3).reshape(WOUT, P, KC * P)
    up = np.zeros((4, P, RW), np.float32)
    up[0, 0:64] = f(w_up)[0]
    up[1, 64:P] = f(a_up)[0]
    up[2] = f(g_up)[0, 0:P]
    up[3, 0:32] = f(g_up)[0, P:]
    lora_up = up.reshape(4, P, PAIRS, P).transpose(2, 1, 0, 3).reshape(PAIRS, P, 4 * P)
    keys = np.stack([f(sub_keys_1)[0], f(sub_keys_2)[0]], 1).reshape(KC, NKEYS, P).transpose(2, 0, 1).reshape(P, KC * NKEYS)
    arrays = {
        "x": f(x)[0], "cols": cols, "ada": ada, "w_in": w_main,
        "w_tail": np.concatenate([tiles(f(w_out)[0], GROUP), tiles(f(w_q)[0], GROUP)]),
        "lora_up": lora_up, "keys": keys, "expert_u": f(expert_u)[0], "expert_v": f(expert_v)[0],
    }
    nc = bacc.Bacc("TRN2", target_bir_lowering=False, num_devices=1)
    ins, aps = {}, []
    for name, a in arrays.items():
        ins["in_" + name] = np.ascontiguousarray(a)
        aps.append(nc.dram_tensor("in_" + name, a.shape, F32, kind="ExternalInput").ap())
    out = nc.dram_tensor("out_0", (T, D), F32, kind="ExternalOutput").ap()
    build_layer(nc, *aps, out)
    r = run(nc, [ins], core_ids=[0])
    return r.results[0]["out_0"].reshape(1, T, D)
```

```python
from contextlib import ExitStack
import math

import numpy as np
import concourse.bass as bass
from concourse import mybir

ALU = mybir.AluOpType
ACT = mybir.ActivationFunctionType
AX = mybir.AxisListType
F32 = mybir.dt.float32
I32 = mybir.dt.int32
U32 = mybir.dt.uint32

P = 128
D = 2048
T = 256
TB = T // P
KC = D // P
VECS = 6
VEC_ORDER = (1, 0, 2, 3, 4, 5)
SL = 2048
RING = 8
GROUP = 512
KT = 4
TILES = KC // KT
ZS = T + 1
R, K, V, B, C, X_ = range(6)
WSLOTS = 6
LORA = 3
PAIRS = 8
PC = 16
MIX_R, MIX_K, MIX_V, W0, A0, K_K, K_A, R_K, LN_W, LN_B, CW0, CW1, CW2, CN = range(14)
CH = 64
NCH = T // CH
LEVELS = 6
DECAY = math.exp(-0.5)
HEADS, TOPK, NKEYS = 8, 16, 128
KTOP = HEADS * TOPK
ADA_SLOTS = 6
VEC_SHIFT = (3, 7, 11)
A_BASE = 6
C_PMW, C_PFW, C_PG1, C_PG2, C_AB, C_C, C_ML, C_PP = 0, 16, 32, 48, 64, 160, 176, 180
NCOL = C_PP + PAIRS * PC


ACT_K = [k for k in range(KC) if k // 2 % 2 == 0]
VEC_K = [k for k in range(KC) if k // 2 % 2 == 1]
ACT_H = " ".join(f"h{k}" for k in ACT_K)
VEC_H = " ".join(f"h{k}" for k in VEC_K)


OUT_K = tuple(k for k in range(KC) if k % PAIRS != PAIRS - 1) + (PAIRS - 1, KC - 1)
OUT_BANKS = ((6, 7), (0, 1), (2, 3), (0, 1))


def row_place(n):
    if n < 2 * FREE:
        return n % FREE, n // FREE + 1
    turn, s = divmod(n - FREE, ROWS)
    return s, turn + (2 if s < FREE else 1)


class Steps:

    def __init__(self, sem, names, lead=False):
        self.sem, self.names, self.per = sem, names.split(), len(names.split())
        assert len(set(self.names)) == self.per
        self.lead = self.per if lead else 0
        self.next = 0

    def at(self, name, i=0):
        return i * self.per + (self.lead + self.names.index(name) + 1)

    def done(self, ins, name):
        assert self.names[self.next % self.per] == name, (self.names[self.next % self.per], name)
        self.next += 1
        return ins.then_inc(self.sem, 1)


def build_layer(nc, x, cols, ada, w_in, w_tail, lora_up, keys,
                expert_u, expert_v, out):
    with ExitStack() as ctx:
        arena_size = 53200
        arena = ctx.enter_context(nc.sbuf_tensor("arena", [P, arena_size], F32))
        ps = ctx.enter_context(nc.psum_tensor("ps", [P, 4096], F32))
        top = [0]

        def take(n):
            a = top[0]
            top[0] += n
            assert top[0] <= arena_size, top[0]
            return a

        def view(a, *shape):
            n = int(np.prod(shape))
            v = arena[:, a:a + n]
            if len(shape) == 2:
                v = v.rearrange("p (a b) -> p a b", a=shape[0])
            if len(shape) == 3:
                v = v.rearrange("p (a b c) -> p a b c", a=shape[0], b=shape[1])
            return v

        def new(*shape):
            return view(take(int(np.prod(shape))), *shape)

        def sem(name):
            return ctx.enter_context(nc.semaphore(name))

        def bank(b, lo=0, hi=512):
            return ps[:, b * 512 + lo:b * 512 + hi]

        def bank3(b, n):
            return bank(b).rearrange("p (a b) -> p a b", a=n)

        ring = new(RING, SL)
        yT = new(KC, T)
        z_at = take(0)
        z = new(6, ZS)
        tz, sgz = new(T), new(2, T)
        kv = view(z_at, KC, P)
        hT = new(KC, T)
        h2T = hT
        colp = new(NCOL)
        ident, ones, bones, bmean = new(P), new(P), new(P), new(P)
        lmask = new(LEVELS, P)
        m0T, strict, incl = new(P), new(P), new(CH)
        cst = new(4)
        silu_c, tmp16 = new(KC), new(KC)
        modc = new(VECS, KC)
        s1c, s2c = new(KC), new(KC)
        gcol = new(2, KC)
        ss, lns, rstd = new(16), new(16), new(16)
        modt = new(KC)
        acc = new(D)
        g_at = take(0)
        xn = new(TB, D)
        red = new(2, 2, P)
        row = new(2, P)
        early = new(ADA_SLOTS - 2, SL)
        zl = new(3, ZS)
        dl, ml = new(3, T), new(3, T)
        top[0] = g_at
        lw = new(4, P)
        pp, npp = [new(PC), new(PC)], new(PC)
        dz = new(3, T)
        dr, dk, dv = (dz[:, n, :] for n in range(3))
        zr, zk, zv = (new(T) for _ in range(3))
        ewa = new(2, T)
        reset = new(T)
        cs, cse, Wt, Wi, We = (new(T) for _ in range(5))
        kkr, kk2, rn, kk, kka, t1, kf, rt, rk = (new(T) for _ in range(9))
        gT = [new(T), new(T)]
        Gt, y, yc, bon, rsy = (new(T) for _ in range(5))
        u = new(T + 2)
        cy, csq, crs = new(T), new(T), new(T)
        ab, bb, kb, vb = (new(NCH, P) for _ in range(4))
        LT = new(NCH, P)
        LTm = [new(NCH, P) for _ in range(2)]
        X, XT, T1 = new(NCH, P), new(NCH, P), new(NCH, P)
        AKT = new(NCH, P)
        RBK = new(NCH, 2, CH)
        vtok, btok, ktok = new(NCH, P), new(NCH, P), new(NCH, P)
        UA = new(NCH, 2, P)
        QPb = new(NCH, 2, P)
        ET, Fw, St = new(2, P), new(3, P), new(2, P)
        top[0] = g_at
        xs = new(TB, D)
        mix_at = take(TB * D)
        mixrow = view(mix_at, TB, D)
        scores = [view(mix_at, KC, NKEYS), view(mix_at + D, KC, NKEYS)]
        qT = new(KC, T)
        gw1 = new(D)
        gw2 = new(D)
        junk = new(D)
        ff = junk
        v16, i16 = new(2 * 2, TOPK), new(2 * 2, TOPK)
        iu = new(2 * 2, TOPK)
        repl = new(D // 4)
        cand = new(2, TOPK * TOPK)
        eq = new(2 * TOPK, TOPK)
        topv, pos, hi_u, lo_u, hi_f, lo_f, ei, ej = (new(2, TOPK) for _ in range(8))
        iota16 = new(TOPK)
        gate = new(TB, KTOP)
        gsum, grec = new(HEADS), new(HEADS)
        idx = new(4 * KTOP + 2)
        stage = new(ROWS, 2)
        actv, wv = new(TB, KTOP), new(TB, KTOP)
        i32 = lambda v: v.bitcast(I32)
        u32 = lambda v: v.bitcast(U32)

        y_rows = yT.rearrange("p a b -> p (a b)")
        row_slot = [y_rows[:, 0:D], y_rows[:, D:2 * D], acc, gw1, ring[:, WSLOTS + 1, :], ring[:, WSLOTS, :],
                    *(ring[:, (LAST + s) % WSLOTS, :] for s in range(WSLOTS))]
        assert len(row_slot) == ROWS

        land = [sem(f"slot_landed{s}") for s in range(RING)]
        early_land = [sem(f"early_landed{s}") for s in range(ADA_SLOTS - 2)]
        w_used, ada_used = sem("weight_tile_used"), sem("ada_tile_used")
        x_in, cols_in, keys_in, lw_in = sem("x_in"), sem("cols_in"), sem("keys_in"), sem("lora_up_in")
        consts = sem("constants_ready")
        z_out = sem("z_evacuated")
        stored = sem("out_stored")
        v0 = Steps(sem("vec_prologue"), " ".join(
            ["den rec silu"] +
            [(f"a{k} r{k} " if k < KC else "") + (f"b{k} q{k} " if k in VEC_SHIFT else "") +
             ("xn0 xn1" if k == 0 else f"m{k - 1} s{k - 1} n{k - 1}") for k in range(KC + 1)] +
            ["zero dl0 dl1 dl2 ml0 ml1 ml2 eg1 sg res1 reset"]))
        a0 = Steps(sem("act_prologue"), "expc sq0 sq1 ln exp row0 " + " ".join(f"e{k}" for k in range(0, KC, 2)) + " " +
                   " ".join((f"row{k + 1} " if k + 1 < KC and k + 1 not in VEC_SHIFT else "") + f"h{k}" for k in range(KC)) +
                   " tanh za eg")
        p0 = Steps(sem("pe_prologue"), "w0 c0 " + " ".join(f"tr{k}" for k in range(0, KC, 2)) + " " +
                   " ".join(("" if k in VEC_SHIFT else f"w{k} ") + f"c{k}" for k in range(1, KC)))
        vm = Steps(sem("vec_mixing"), "X0a X0 akt rbk bon " + " ".join(f"X{m} XT{m} c{m - 1}" for m in (1, 2, 3)) +
                   " X4 XT4 XT5 qp2 et g s2 s3 yc yn aff addb yg cout")
        am = Steps(sem("act_mixing"), "lt vtok atok btok ktok T1_1 u1 T1_2 T1_3 T1_4 T1_5 qp1 f0 f1 f2 lnc rsc y lny rsy")
        pm = Steps(sem("pe_mixing"), "lt l akt rbk vtr atr btr ktr u1 bon " + " ".join(f"T1_{m} X{m}" for m in range(1, LEVELS)) +
                   " qp g_ et conv f s2 s3 y mean var")
        gm = Steps(sem("pool_mixing"), "XT0a XT0 m1 u m2 m3 m4 m5 cyb csq sqy")
        vn = Steps(sem("vec_next"), "pp npp zr zk zv kkr den sig cs cse kk kka t1 kf ab0 ab1 bb0 bb1 rk")
        an = Steps(sem("act_next"), "ew ea gT vb0 vb1 Wt Wi We lnk rn")
        pn = Steps(sem("pe_next"), "wa g kks", lead=True)
        gn = Steps(sem("pool_next"), "dr dk dv kk2 kb0 kb1 rt")
        mod_sum, mod_out = sem("modulation_turned"), sem("modulation_columns")
        mod_red = sem("modulation_half_reduced")
        zeroed = sem("blocks_zeroed")
        m_out = sem("mix_evacuated")
        a2 = Steps(sem("act_output"), "gw1 ln exp sqx0 ln0 exp0 sqx1 ln1 exp1 " + ACT_H + " rows gw2")
        v2 = Steps(sem("vec_output"), "s2a s2 ga1 sq0 sq1 mx0 mx1 m5 ga2 xn0 xn1 " + VEC_H)
        p2 = Steps(sem("pe_output"), "gate1 " + " ".join(f"tr{k}" for k in range(0, KC, 2)) + " rows gate2")
        m_sq = sem("mix_squares_summed")
        q_out = sem("queries_evacuated")
        zl_zero = sem("lora_zero_column")
        sc_ps, sc_out = sem("scores_ready"), sem("scores_evacuated")
        vr = sem("vec_routing")
        ar = sem("act_routing")
        h_ps, h_used = sem("h_rows_ready"), sem("h_rows_used")
        staged, used = sem("indices_staged"), sem("expert_row_used")
        accz = sem("expert_sum_cleared")
        gland = [sem(f"row_landed{s}") for s in range(ROWS)]
        fin_v, fin_a, gelu_done, wv_done = sem("vec_final"), sem("act_final"), sem("gelu_done"), sem("weights_ready")

        block = ctx.enter_context(nc.Block())
        NADA = (VECS - 2) * KC

        def early_tile(q):
            n = q % ADA_SLOTS
            return (ring[:, WSLOTS + n, :], land[WSLOTS + n]) if n < 2 else (early[:, n - 2, :], early_land[n - 2])

        def early_used(q):
            k = q // 2
            if q % 2 == 0:
                return v0.sem, v0.at(f"r{k}")
            return (v0.sem, v0.at(f"q{k}")) if k in VEC_SHIFT else (p0.sem, p0.at(f"w{k}"))

        def tile_of(a, n):
            return a[n] if isinstance(n, int) else a[bass.ds(n, 1)].rearrange("a p n -> p (a n)")

        @block.sync
        def _(sp):
            for q in range(2 * KC):
                if q >= ADA_SLOTS:
                    sp.wait_ge(*early_used(q - ADA_SLOTS))
                dst, landed = early_tile(q)
                sp.dma_start(dst, ada[q]).then_inc(landed, 16)
                if q in (3, 11):
                    c = slice(q // 11 * SL // 2, (q // 11 + 1) * SL // 2)
                    for m in range(WSLOTS):
                        sp.dma_start(ring[:, m, c], w_in[m][:, c]).then_inc(land[m], 16)
            for q in range(2):
                sp.wait_ge(*early_used(2 * KC - 2 + q))
                sp.dma_start(ring[:, WSLOTS + q, :], ada[2 * KC + q]).then_inc(land[WSLOTS + q], 16)
            sp.wait_ge(p0.sem, p0.at("tr14"))
            sp.dma_start(lw.rearrange("p a b -> p (a b)"), lora_up[0]).then_inc(lw_in, 16)
            for t in range(3):
                m = WSLOTS + t
                sp.wait_ge(w_used, m - WSLOTS + 1)
                sp.dma_start(ring[:, m % WSLOTS, :], w_in[m]).then_inc(land[m % WSLOTS], 16)

            def round_loads(i, last):
                if not last:
                    sp.wait_ge(pn.sem, pn.at("g", i))
                    sp.dma_start(lw.rearrange("p a b -> p (a b)"), tile_of(lora_up, i + 1)).then_inc(lw_in, 16)
                for t in range(8):
                    if t < 6 and not last:
                        sp.wait_ge(w_used, i * 6 + (LORA + 6 + t - WSLOTS + 1))
                        s = (LORA + t) % WSLOTS
                        sp.dma_start(ring[:, s, :], tile_of(w_in, i * 6 + (LORA + 6 + t))).then_inc(land[s], 16)
                    if last and t < 6:
                        sp.wait_ge(w_used, LORA + 6 * PAIRS - WSLOTS + t + 1)
                        s = (LORA + t) % WSLOTS
                        sp.dma_start(ring[:, s, :], w_tail[t]).then_inc(land[s], 16)
                    if t < 6 or not last:
                        sp.wait_ge(ada_used, i * 8 + (2 + t - 1))
                        s = WSLOTS + t % 2
                        sp.dma_start(ring[:, s, :], tile_of(ada, i * 8 + (2 * KC + 2 + t))).then_inc(land[s], 16)

            with sp.Fori(0, 3) as it:
                for half in range(2):
                    round_loads(it * 2 + half, False)
            round_loads(6, False)
            round_loads(7, True)
            for e in (vm, am, pm, gm):
                sp.wait_ge(e.sem, PAIRS * e.per)
            sp.dma_start(xs[:, :, :], x.rearrange("(b p) n -> p b n", p=P)).then_inc(x_in, 16)
            sp.dma_start(kv.rearrange("p a b -> p (a b)"), keys).then_inc(keys_in, 16)
            for n in range(6, 32):
                m = LORA + 6 * PAIRS + n
                sp.wait_ge(w_used, m - WSLOTS + 1)
                sp.dma_start(ring[:, m % WSLOTS, :], w_tail[n]).then_inc(land[m % WSLOTS], 16)
            for tb in range(TB):
                for h in range(2):
                    c = slice(h * D // 2, (h + 1) * D // 2)
                    sp.wait_ge(fin_v, 4 * tb + 2 * (h + 1))
                    sp.dma_start(out[tb * P:(tb + 1) * P, c], xs[:, tb, c]).then_inc(stored, 16)
            sp.wait_ge(stored, 16 * 2 * TB)

        @block.gpsimd
        def _(pool):
            nconst = [0]

            def const(ins):
                nconst[0] += 1
                ins.then_inc(consts, 1)

            def after():
                pool.wait_ge(consts, nconst[0])

            for t in (ident, lmask[:, :, :], m0T, bones):
                const(nc.gpsimd.memset(t, 0.0))
            for t in (ones, strict, incl):
                const(nc.gpsimd.memset(t, 1.0))
            const(nc.gpsimd.memset(bmean, 0.0))
            after()
            for v, n in ((1e-6, 0), (64e-5, 1), (1e-12, 2), (0.0, 3)):
                const(nc.gpsimd.memset(cst[:, n:n + 1], v))
            for h in range(2):
                after()
                const(nc.gpsimd.memset(bones[h * 64:h * 64 + 64, h * 64:h * 64 + 64], 1.0))
                const(nc.gpsimd.memset(bmean[h * 64:h * 64 + 64, h * 64:h * 64 + 64], 1.0 / 64))
            after()
            const(nc.gpsimd.affine_select(out=ident, in_=ident, compare_op=ALU.not_equal, fill=1.0, base=0,
                                          pattern=[[-1, P]], channel_multiplier=1))
            for m in range(LEVELS):
                size = 1 << m
                v = lmask[:, m, :].rearrange("p (q r) -> p q r", r=2 * size)[:, :, size:]
                const(nc.gpsimd.memset(v, 1.0))
                after()
                const(nc.gpsimd.affine_select(out=v, in_=v, compare_op=ALU.is_ge, fill=0.0, base=0,
                                              pattern=[[-2 * size, P // (2 * size)], [0, size]], channel_multiplier=1))
                after()
                const(nc.gpsimd.affine_select(out=v, in_=v, compare_op=ALU.is_ge, fill=0.0, base=size - 1,
                                              pattern=[[2 * size, P // (2 * size)], [0, size]], channel_multiplier=-1))
            v = m0T.rearrange("p (q r) -> p q r", r=2)[:, :, 0:1]
            const(nc.gpsimd.affine_select(out=v, in_=v, compare_op=ALU.not_equal, fill=1.0, base=-1,
                                          pattern=[[-2, P // 2], [0, 1]], channel_multiplier=1))
            v = strict.rearrange("p (h r) -> p h r", h=2)
            const(nc.gpsimd.affine_select(out=v, in_=v, compare_op=ALU.is_gt, fill=0.0, base=0,
                                          pattern=[[CH, 2], [1, CH]], channel_multiplier=-1))
            after()
            const(nc.gpsimd.affine_select(out=v, in_=v, compare_op=ALU.is_ge, fill=0.0, base=0,
                                          pattern=[[-CH, 2], [0, CH]], channel_multiplier=1))
            for h in range(2):
                v = incl[h * 64:h * 64 + 64, :]
                after()
                const(nc.gpsimd.affine_select(out=v, in_=v, compare_op=ALU.is_ge, fill=0.0, base=0,
                                              pattern=[[1, CH]], channel_multiplier=-1))
            assert nconst[0] == NCONST, nconst[0]
            after()
            pool.wait_ge(v0.sem, v0.at("reset"))
            for t in (ab, bb, kb, vb):
                nc.gpsimd.memset(t[:, :, :], 0.0).then_inc(zeroed, 1)
            nc.gpsimd.memset(u[:, 0:2], 0.0).then_inc(zeroed, 1)
            pool.wait_ge(zeroed, 5)
            tt = nc.gpsimd.tensor_tensor

            def next_a(j):
                for n, (name, d) in enumerate((("dr", dr), ("dk", dk), ("dv", dv))):
                    pool.wait_ge(z_out, j * 6 + (LORA + n + 1))
                    gn.done(tt(d, z[:, n, 0:T], z[:, n, 1:ZS], ALU.subtract), name)
                pool.wait_ge(vn.sem, vn.at("kkr", j))
                gn.done(tt(kk2, kkr, kkr, ALU.mult), "kk2")

            def next_b(j):
                pool.wait_ge(an.sem, an.at("Wi", j))
                pool.wait_ge(vn.sem, vn.at("kf", j))
                for h in range(2):
                    r = slice(h * 64, h * 64 + 64)
                    pool.wait_ge(gn.sem, gn.at(("kk2", "kb0")[h], j))
                    gn.done(tt(kb[r, :, r], kf[r, :].rearrange("p (c t) -> p c t", c=NCH),
                               Wi[r, :].rearrange("p (c t) -> p c t", c=NCH), ALU.mult), f"kb{h}")
                pool.wait_ge(gn.sem, gn.at("kb1", j))
                gn.done(tt(rt, zr, Wt, ALU.mult), "rt")

            def pool_round(i, last):
                pool.wait_ge(am.sem, am.at("lt", i))
                gm.done(tt(XT[:, :, :], LT[:, :, :], lmask[:, 0:1, :].broadcast_to([P, NCH, P]), ALU.mult), "XT0a")
                pool.wait_ge(gm.sem, gm.at("XT0a", i))
                gm.done(tt(XT[:, :, :], XT[:, :, :], ident.rearrange("p (a b) -> p a b", a=1).broadcast_to([P, NCH, P]), ALU.add), "XT0")
                for m in range(1, LEVELS):
                    if m > 2:
                        pool.wait_ge(pm.sem, pm.at(f"T1_{m - 2}", i))
                    gm.done(tt(LTm[m % 2][:, :, :], LT[:, :, :], lmask[:, m:m + 1, :].broadcast_to([P, NCH, P]), ALU.mult), f"m{m}")
                    if m == 1:
                        pool.wait_ge(z_out, i * 6 + (LORA + 6))
                        gm.done(tt(u[:, 2:], z[:, C, 1:ZS], z[:, X_, 1:ZS], ALU.mult), "u")
                    if m == 5:
                        pool.wait_ge(vm.sem, vm.at("c2", i))
                        gm.done(tt(cy, cy, z[:, B, 1:ZS], ALU.mult), "cyb")
                        pool.wait_ge(gm.sem, gm.at("cyb", i))
                        gm.done(tt(csq, cy, cy, ALU.mult), "csq")
                if not last:
                    next_a(i + 1)
                pool.wait_ge(vm.sem, vm.at("yc", i))
                gm.done(tt(y, yc, yc, ALU.mult), "sqy")
                if not last:
                    next_b(i + 1)

            next_a(0)
            next_b(0)
            with pool.Fori(0, 3) as it:
                for half in range(2):
                    pool_round(it * 2 + half, False)
            pool_round(6, False)
            pool_round(7, True)
            pool.wait_ge(vr, IDX_AT[0])
            nc.gpsimd.tensor_copy(i32(stage[:, 0, :]), i32(idx[:, 0:2])).then_inc(staged, 1)
            pool.sem_inc(used, ROWS)

            def gathers(ph, lo, hi, first=False):
                table = (expert_u, expert_v)[ph % 2]

                def body(base, count, t):
                    for g in range(count // 2):
                        n = ph * KTOP + base + 2 * g
                        if first and n >= 2 * FREE:
                            pool.wait_ge(w_used, LAST - WSLOTS + n - 2 * FREE + 2)
                        pool.wait_ge(staged, t * (LOOP // 2) + (n // 2 + 1))
                        pool.wait_ge(used, t * LOOP + (n + 2 + (ROWS - FREE if FREE <= n < 2 * FREE else 0)))
                        ahead = i32(idx[:, n + 2:n + 4]) if isinstance(t, int) else i32(idx)[:, bass.ds(t * LOOP + (n + 2), 2)]
                        nc.gpsimd.tensor_copy(i32(stage[:, (n // 2 + 1) % ROWS, :]), ahead).then_inc(staged, 1)
                        for j in range(2):
                            s = row_place(n + j)[0]
                            nc.gpsimd.indirect_dma_start(
                                out=row_slot[s], out_offset=None, in_=table[:, :],
                                in_offset=bass.IndirectOffsetOnAxis(ap=i32(stage[:, n // 2 % ROWS, :])[:, j:j + 1], axis=0)).then_inc(gland[s], 16)

                loops = 0 if first else (hi - lo) // LOOP
                if loops:
                    with pool.Fori(0, loops) as t:
                        body(lo, LOOP, t)
                body(lo + loops * LOOP, hi - lo - loops * LOOP, 0)

            start = FREE + ROWS
            gathers(0, 0, start, first=True)
            pool.wait_ge(vr, IDX_AT[2])
            gathers(0, start, start + 3 * LOOP)
            pool.wait_ge(vr, IDX_AT[3])
            gathers(0, start + 3 * LOOP, KTOP)
            pool.wait_ge(vr, IDX_AT[4])
            gathers(1, 0, KTOP)
            pool.wait_ge(vr, IDX_AT[7])
            for ph in (2, 3):
                gathers(ph, 0, KTOP)

        def ring_junk(b):
            return yT.rearrange("p a b -> p (a b)")[:, b * D:(b + 1) * D]

        @block.scalar
        def _(act):
            act.dma_start(colp, cols).then_inc(cols_in, 16)
            act.dma_start(xn[:, :, :], x.rearrange("(b p) n -> p b n", p=P)).then_inc(x_in, 16)
            act.wait_ge(cols_in, 16)
            a0.done(nc.scalar.activation(tmp16, colp[:, C_C:C_C + KC], ACT.Exp, scale=-1.0), "expc")
            act.wait_ge(x_in, 16)
            for b in range(TB):
                a0.done(nc.scalar.activation(ring_junk(b), xn[:, b, :], ACT.Square, accum_out=ss[:, b:b + 1]), f"sq{b}")
            act.wait_ge(consts, NCONST)
            act.wait_ge(a0.sem, a0.at("sq1"))
            a0.done(nc.scalar.activation(lns[:, 0:2], ss[:, 0:2], ACT.Ln, bias=cst[:, 0:1], scale=1.0 / D), "ln")
            act.wait_ge(a0.sem, a0.at("ln"))
            a0.done(nc.scalar.activation(rstd[:, 0:2], lns[:, 0:2], ACT.Exp, scale=-0.5), "exp")
            def shift_row(k):
                act.wait_ge(p0.sem, p0.at(f"w{k}"))
                if k >= 2:
                    act.wait_ge(p0.sem, p0.at(f"c{k - 2}"))
                a0.done(nc.scalar.activation(row[0:1, k % 2, :], bank(6 + k % 2, P, 2 * P)[0:1, :], ACT.Copy), f"row{k}")

            shift_row(0)
            for k in range(0, KC, 2):
                act.wait_ge(p0.sem, p0.at(f"tr{k}"))
                a0.done(nc.scalar.activation(hT[:, k:k + 2, :], bank3((k // 2) % 4, 2), ACT.Copy), f"e{k}")
            for k in range(KC):
                if k + 1 < KC and k + 1 not in VEC_SHIFT:
                    shift_row(k + 1)
                act.wait_ge(v0.sem, v0.at(f"n{k}"))
                act.wait_ge(a0.sem, a0.at(f"e{k - k % 2}"))
                a0.done(nc.scalar.activation(hT[:, k, :], hT[:, k, :], ACT.Identity,
                                             bias=modc[:, 1, k:k + 1], scale=s1c[:, k:k + 1]), f"h{k}")

            def z_copy(m, dst):
                act.wait_ge(w_used, m + 1)
                nc.scalar.activation(dst, bank(6 + z_bank[0] % 2, 0, T), ACT.Copy).then_inc(z_out, 1)
                z_bank[0] += 1

            def z_copy_first(m, dst):
                act.wait_ge(w_used, m + 1)
                nc.scalar.activation(dst, bank(m, 0, T), ACT.Copy).then_inc(z_out, 1)

            z_bank = [0]
            for n in range(LORA):
                z_copy_first(n, zl[:, n, 1:ZS])
            act.wait_ge(v0.sem, v0.at("zero"))
            for n in range(3):
                z_copy_first(LORA + n, z[:, n, 1:ZS])
            act.wait_ge(v0.sem, v0.at("ml2"))
            a0.done(nc.scalar.activation(tz[0:64, :], ml[0:64, 0, :], ACT.Tanh), "tanh")
            a0.done(nc.scalar.activation(tz[64:P, :], ml[64:P, 0, :], ACT.Copy), "za")
            a0.done(nc.scalar.activation(sgz[:, :, :], ml[:, 1:3, :], ACT.Exp, scale=-1.0), "eg")
            nc.scalar.preload_act_table_set("natural_log_exp_and_others")
            A = nc.scalar.activation
            flat = lambda v: v.rearrange("p a b -> p (a b)")

            def next_a(j, par):
                act.wait_ge(pn.sem, pn.at("wa", j))
                act.wait_ge(vn.sem, vn.at("npp", j))
                an.done(A(ewa[:, 0, :], bank(0, 0, T), ACT.Exp, bias=npp[:, W0:W0 + 1], scale=-1.0), "ew")
                an.done(A(ewa[:, 1, :], bank(0, T), ACT.Exp, bias=npp[:, A0:A0 + 1], scale=-1.0), "ea")
                act.wait_ge(pn.sem, pn.at("g", j))
                an.done(A(gT[par], bank(1, 0, T), ACT.Copy), "gT")
                act.wait_ge(vn.sem, vn.at("zv", j))
                for h in range(2):
                    r = slice(h * 64, h * 64 + 64)
                    an.done(A(vb[r, :, r], zv[r, :].rearrange("p (c t) -> p c t", c=NCH), ACT.Copy), f"vb{h}")

            def next_b(j):
                act.wait_ge(vn.sem, vn.at("cs", j))
                an.done(A(Wt, cs, ACT.Exp, scale=-DECAY), "Wt")
                an.done(A(Wi, cs, ACT.Exp, scale=DECAY), "Wi")
                act.wait_ge(vn.sem, vn.at("cse", j))
                an.done(A(We, cse, ACT.Exp, scale=-DECAY), "We")
                act.wait_ge(pn.sem, pn.at("kks", j))
                an.done(A(rn, bank(1, 0, T), ACT.Ln, bias=cst[:, 2:3]), "lnk")
                act.wait_ge(an.sem, an.at("lnk", j))
                an.done(A(rn, rn, ACT.Exp, scale=-0.5), "rn")

            def act_round(i, par, last):
                tiles = [0]

                def copies(point):
                    while not last and tiles[0] < TILES_AT[point]:
                        t = tiles[0]
                        if t == 3:
                            act.wait_ge(gm.sem, gm.at("cyb", i))
                        z_copy(i * 6 + (LORA + 6 + t), z[:, t, 1:ZS])
                        tiles[0] += 1

                def step(name, out, in_, func, **kw):
                    am.done(A(out, in_, func, **kw), name)

                act.wait_ge(pm.sem, pm.at("lt", i))
                step("lt", flat(LT), bank(2), ACT.Copy)
                act.wait_ge(pm.sem, pm.at("vtr", i))
                step("vtok", flat(vtok), bank(0), ACT.Copy)
                act.wait_ge(pm.sem, pm.at("atr", i))
                step("atok", UA[:, :, 1, :], bank3(1, NCH), ACT.Copy)
                act.wait_ge(pm.sem, pm.at("btr", i))
                step("btok", flat(btok), bank(0), ACT.Copy)
                act.wait_ge(pm.sem, pm.at("ktr", i))
                step("ktok", flat(ktok), bank(1), ACT.Copy)
                for m in range(1, LEVELS):
                    act.wait_ge(pm.sem, pm.at(f"T1_{m}", i))
                    step(f"T1_{m}", flat(T1), bank(2), ACT.Copy)
                    if m == 1:
                        step("u1", UA[:, :, 0, :], bank3(5, NCH), ACT.Copy)
                    copies(f"T1_{m}")
                act.wait_ge(pm.sem, pm.at("qp", i))
                step("qp1", QPb[:, 0:2, :, :].rearrange("p a b c -> p (a b c)"), bank(0), ACT.Copy)
                copies("qp")
                act.wait_ge(pm.sem, pm.at("f", i))
                for c in range(3):
                    w = (c + 1) * CH - 1
                    step(f"f{c}", Fw[:, c, :], bank(4, c * P, c * P + P), ACT.Copy, scale=Wt[:, w:w + 1])
                step("lnc", crs, bank(1, 0, T), ACT.Ln, bias=cst[:, 0:1])
                act.wait_ge(am.sem, am.at("lnc", i))
                step("rsc", crs, crs, ACT.Exp, scale=-0.5)
                copies("f")
                act.wait_ge(pm.sem, pm.at("y", i))
                step("y", y, bank(5, 0, T), ACT.Copy)
                copies("y")
                if not last:
                    next_a(i + 1, 1 - par)
                copies("wa")
                act.wait_ge(pm.sem, pm.at("var", i))
                step("lny", rsy, bank(5, 0, T), ACT.Ln, bias=cst[:, 1:2])
                act.wait_ge(am.sem, am.at("lny", i))
                step("rsy", rsy, rsy, ACT.Exp, scale=-0.5)
                if not last:
                    next_b(i + 1)
                copies("end")

            next_a(0, 0)
            next_b(0)
            for n in range(3, 6):
                z_copy(LORA + n, z[:, n, 1:ZS])
            with act.Fori(0, 3) as it:
                for half in range(2):
                    act_round(it * 2 + half, half, False)
            act_round(6, 0, False)
            act_round(7, 1, True)
            act.wait_ge(p2.sem, p2.at("gate1"))
            a2.done(nc.scalar.activation(gw1, ps[:, 1024:3072], ACT.Copy), "gw1")
            for g in range(4):
                act.wait_ge(w_used, WOUT + 4 * (g + 1))
                for b in range(TB):
                    if g or b:
                        act.wait_ge(m_sq, 2 * g + b)
                    nc.scalar.activation(junk[:, 0:GROUP], bank(OUT_BANKS[g][b]), ACT.Square, accum_out=ss[:, b * 4 + g:b * 4 + g + 1]).then_inc(m_sq, 1)
            act.wait_ge(v2.sem, v2.at("sq1"))
            a2.done(nc.scalar.activation(lns[:, 2:4], ss[:, 8:10], ACT.Ln, bias=cst[:, 0:1], scale=1.0 / D), "ln")
            act.wait_ge(a2.sem, a2.at("ln"))
            a2.done(nc.scalar.activation(rstd[:, 2:4], lns[:, 2:4], ACT.Exp, scale=-0.5), "exp")
            act.wait_ge(m_sq, 8)
            for b in range(TB):
                act.wait_ge(v2.sem, v2.at(f"mx{b}"))
                if b:
                    act.wait_ge(a2.sem, a2.at("sqx0"))
                a2.done(nc.scalar.activation(junk, xs[:, b, :], ACT.Square, accum_out=ss[:, 10 + b:11 + b]), f"sqx{b}")
                act.wait_ge(a2.sem, a2.at(f"sqx{b}"))
                a2.done(nc.scalar.activation(lns[:, 4 + b:5 + b], ss[:, 10 + b:11 + b], ACT.Ln, bias=cst[:, 0:1], scale=1.0 / D), f"ln{b}")
                act.wait_ge(a2.sem, a2.at(f"ln{b}"))
                a2.done(nc.scalar.activation(rstd[:, 4 + b:5 + b], lns[:, 4 + b:5 + b], ACT.Exp, scale=-0.5), f"exp{b}")
            for k in ACT_K:
                act.wait_ge(p2.sem, p2.at(f"tr{k - k % 2}"))
                a2.done(nc.scalar.activation(h2T[:, k, :], bank(k // 2, k % 2 * T, k % 2 * T + T), ACT.Identity,
                                             bias=modc[:, 3, k:k + 1], scale=s2c[:, k:k + 1]), f"h{k}")
            def softmax(b, g):
                act.wait_ge(vr, GATE_AT[4 * b + g])
                gv = gate[:, b, g * 2 * TOPK:(g + 1) * 2 * TOPK]
                nc.scalar.activation(gv, gv, ACT.Exp).then_inc(ar, 1)

            for g in range(4):
                act.wait_ge(w_used, WOUT + 16 + 4 * (g + 1))
                for h in range(2):
                    nc.scalar.activation(qT[:, 4 * g + 2 * h:4 * g + 2 * h + 2, :], bank3(2 * (g % 2) + h, 2), ACT.Copy).then_inc(q_out, 1)
                if g == 0:
                    act.wait_ge(p2.sem, p2.at("rows"))
                    a2.done(nc.scalar.activation(junk, ps[:, 2048:4096], ACT.Copy), "rows")
                for b in range(TB):
                    act.wait_ge(sc_ps, 2 * g + b + 1)
                    nc.scalar.activation(scores[b][:, 4 * g:4 * g + 4, :], bank3(4 + 2 * (g % 2) + b, 4), ACT.Copy).then_inc(sc_out, 1)
                if g:
                    softmax(0, g - 1)
            softmax(0, 3)
            act.wait_ge(p2.sem, p2.at("gate2"))
            a2.done(nc.scalar.activation(gw2, ps[:, 2048:4096], ACT.Copy), "gw2")
            for g in range(2):
                softmax(1, g)
            for b in range(TB):
                act.wait_ge(used, ROWS + (2 * b + 1) * KTOP)
                nc.scalar.activation(wv[:, b, :], actv[:, b, :], ACT.Gelu).then_inc(gelu_done, 1)
                if b == 0:
                    softmax(1, 2)
                    softmax(1, 3)
                act.wait_ge(used, ROWS + (2 * b + 2) * KTOP)
                if b:
                    act.wait_ge(fin_v, 4 * b)
                nc.scalar.activation(junk, ps[:, 2048:4096], ACT.Square, accum_out=ss[:, 12 + b:13 + b]).then_inc(fin_a, 1)
                act.wait_ge(fin_a, 3 * b + 1)
                nc.scalar.activation(lns[:, 12 + b:13 + b], ss[:, 12 + b:13 + b], ACT.Ln, bias=cst[:, 0:1], scale=1.0 / D).then_inc(fin_a, 1)
                act.wait_ge(fin_a, 3 * b + 2)
                nc.scalar.activation(rstd[:, 12 + b:13 + b], lns[:, 12 + b:13 + b], ACT.Exp, scale=-0.5).then_inc(fin_a, 1)

        @block.tensor
        def _(pe):
            mm = nc.tensor.matmul

            def columns(v, out_bank, at):
                for k in range(KC):
                    last = mm(bank(out_bank, at + k, at + k + 1), v[:, k * P:(k + 1) * P], ones[:, 0:1], start=True, stop=True)
                return last

            pe.wait_ge(consts, NCONST)

            def shift_product(k):
                b = 6 + k % 2
                if k >= 2:
                    pe.wait_ge(v0.sem, v0.at(f"n{k - 2}"))
                if k not in VEC_SHIFT:
                    tile, landed = early_tile(2 * k + 1)
                    pe.wait_ge(landed, 16 * ((2 * k + 1) // ADA_SLOTS + 1))
                    pe.wait_ge(v0.sem, v0.at("silu"))
                    for j in range(KC):
                        last = mm(bank(b, P, 2 * P)[0:1, :], silu_c[:, j:j + 1], tile[:, j * P:(j + 1) * P], start=(j == 0), stop=(j == KC - 1))
                    p0.done(last, f"w{k}")

            def early_columns(k):
                b = 6 + k % 2
                if k in VEC_SHIFT:
                    pe.wait_ge(v0.sem, v0.at(f"q{k}"))
                    mm(bank(b, 1, 2), red[:, k % 2, 1, :], ones[:, 0:1], start=True, stop=True)
                else:
                    pe.wait_ge(a0.sem, a0.at(f"row{k}"))
                    mm(bank(b, 1, 2), row[0:1, k % 2, :], ones[0:1, 0:1], start=True, stop=True)
                pe.wait_ge(v0.sem, v0.at(f"r{k}"))
                p0.done(mm(bank(b, 0, 1), red[:, k % 2, 0, :], ones[:, 0:1], start=True, stop=True), f"c{k}")

            def early_projection(k):
                pe.wait_ge(a0.sem, a0.at(f"h{k}"))
                for m in range(LORA + 3):
                    if k % (KC // 2) == 0:
                        pe.wait_ge(land[m], 16 * (k // (KC // 2) + 1))
                    last = mm(bank(m, 0, T), ring[:, m, k * P:(k + 1) * P], hT[:, k, :], start=(k == 0), stop=(k == KC - 1))
                    if k == KC - 1:
                        last.then_inc(w_used, 1)

            shift_product(0)
            early_columns(0)
            pe.wait_ge(v0.sem, v0.at("xn1"))
            for k in range(0, KC, 2):
                if k >= 8:
                    pe.wait_ge(a0.sem, a0.at(f"e{k - 8}"))
                for kk in range(2):
                    for b in range(TB):
                        last = nc.tensor.transpose(bank((k // 2) % 4, kk * T + b * P, kk * T + b * P + P),
                                                   xn[:, b, (k + kk) * P:(k + kk + 1) * P], ident)
                p0.done(last, f"tr{k}")
            for k in range(1, KC):
                shift_product(k)
                if k >= 2:
                    early_projection(k - 2)
                early_columns(k)
            early_projection(KC - 2)
            early_projection(KC - 1)

            def quarter(slot, b, q):
                w = ring[:, slot, :].rearrange("p (a b) -> p a b", a=KC)
                for k in range(4 * q, 4 * q + 4):
                    last = mm(bank(b, 0, T), w[:, k, :], hT[:, k, :], start=(k == 0), stop=(k == KC - 1))
                return last

            def whole(m):
                pe.wait_ge(land[m % WSLOTS], 16 * (m // WSLOTS + 2))
                if m >= WSLOTS + 2:
                    pe.wait_ge(z_out, m - 1)
                for q in range(4):
                    last = quarter(m % WSLOTS, 6 + m % 2, q)
                last.then_inc(w_used, 1)

            pe.sem_inc(pn.sem, pn.lead)

            def next_a(j, first=False):
                pe.wait_ge(lw_in, j * 16 + 16)
                if first:
                    pe.wait_ge(a0.sem, a0.at("za"))
                mm(bank(0, 0, T), lw[:, 0, :], tz, start=True, stop=True)
                pn.done(mm(bank(0, T), lw[:, 1, :], tz, start=True, stop=True), "wa")
                if first:
                    pe.wait_ge(v0.sem, v0.at("sg"))
                mm(bank(1, 0, T), lw[:, 2, :], sgz[:, 0, :], start=True, stop=False)
                pn.done(mm(bank(1, 0, T), lw[:, 3, :], sgz[:, 1, :], start=False, stop=True), "g")

            def next_b(j):
                pe.wait_ge(gn.sem, gn.at("kk2", j))
                pe.wait_ge(an.sem, an.at("gT", j))
                pn.done(mm(bank(1, 0, T), bones, kk2, start=True, stop=True), "kks")

            def turn_half(h):
                for k in range(KC // 2):
                    last = nc.tensor.transpose(bank(2 + k // 4, k % 4 * P, k % 4 * P + P),
                                               acc[:, (h * KC // 2 + k) * P:(h * KC // 2 + k + 1) * P], ident)
                last.then_inc(mod_sum, 1)

            def out_chunk(g, n):
                m = WOUT + 4 * g + n // KT
                if n % KT == 0:
                    pe.wait_ge(land[m % WSLOTS], 16 * (m // WSLOTS + 2))
                w = ring[:, m % WSLOTS, n % KT * GROUP:(n % KT + 1) * GROUP]
                for b in range(TB):
                    last = mm(bank(OUT_BANKS[g][b]), yT[:, OUT_K[n], b * P:(b + 1) * P], w, start=(n == 0), stop=(n == KC - 1))
                if n % KT == KT - 1:
                    last.then_inc(w_used, 1)

            def pe_round(i, par, last_round):
                S = pm
                state = [0]

                def fill(point):
                    while last_round and state[0] < OUT_AT[point]:
                        if state[0] == 0:
                            pe.wait_ge(vm.sem, (PAIRS - 1) * vm.per)
                            pe.wait_ge(z_out, LORA + 6 * PAIRS)
                        out_chunk(0, state[0])
                        state[0] += 1
                    while not last_round and state[0] < FILL_AT[point]:
                        t, q = divmod(state[0], 4)
                        slot, b = (LORA + t) % WSLOTS, 6 + (LORA + t) % 2
                        if q == 0:
                            pe.wait_ge(land[slot], i * 16 + 16 * ((LORA + 6 + t) // WSLOTS + 2))
                            pe.wait_ge(z_out, i * 6 + (LORA + 6 + t - 1))
                        last = quarter(slot, b, q)
                        if q == 3:
                            last.then_inc(w_used, 1)
                        state[0] += 1

                def blocks(b, l, r, name):
                    for c in range(NCH):
                        last = mm(bank(b, c * P, c * P + P), l[:, c, :], r[:, c, :], start=True, stop=True)
                    S.done(last, name)

                def turned(b, t, name):
                    for c in range(NCH):
                        last = nc.tensor.transpose(bank(b, c * P, c * P + P), t[:, c, :], ident)
                    S.done(last, name)

                pe.wait_ge(vn.sem, vn.at("bb1", i))
                if not par:
                    pe.wait_ge(mod_red, i + 2)
                blocks(2, bb, ab, "lt")
                blocks(3, ab, bb, "l")
                pe.wait_ge(gn.sem, gn.at("rt", i))
                blocks(4, kb, ab, "akt")
                for c in range(NCH):
                    mm(bank(5, c * P, c * P + CH), bb[:, c, :], rt[:, c * CH:(c + 1) * CH], start=True, stop=True)
                    last = mm(bank(5, c * P + CH, c * P + P), kb[:, c, :], rt[:, c * CH:(c + 1) * CH], start=True, stop=True)
                S.done(last, "rbk")
                pe.wait_ge(an.sem, an.at("rn", i))
                turned(0, vb, "vtr")
                turned(1, ab, "atr")
                fill("atr")
                pe.wait_ge(am.sem, am.at("vtok", i))
                turned(0, bb, "btr")
                pe.wait_ge(am.sem, am.at("atok", i))
                turned(1, kb, "ktr")
                fill("ktr")
                pe.wait_ge(vm.sem, vm.at("rbk", i))
                blocks(5, AKT, vtok, "u1")
                pe.wait_ge(am.sem, am.at("btok", i))
                pe.wait_ge(vn.sem, vn.at("rk", i))
                S.done(mm(bank(0, 0, T), bones, rk, start=True, stop=True), "bon")
                for m in range(1, LEVELS):
                    pe.wait_ge(gm.sem, gm.at(f"m{m}", i))
                    pe.wait_ge(vm.sem, vm.at("X0" if m == 1 else f"XT{m - 1}", i))
                    blocks(2, LTm[m % 2], X, f"T1_{m}")
                    fill(f"T1_{m}")
                    pe.wait_ge(am.sem, am.at(f"T1_{m}", i))
                    if m < LEVELS - 1:
                        for c in range(NCH):
                            mm(bank(3, c * P, c * P + P), XT[:, c, :], T1[:, c, :], start=True, stop=True)
                    blocks(4, T1, XT, f"X{m}")
                    fill(f"X{m}")
                pe.wait_ge(vm.sem, vm.at("XT5", i))
                pe.wait_ge(am.sem, am.at("ktok", i))
                for c in range(NCH):
                    last = mm(bank(c // 2, (c % 2) * T, (c % 2) * T + T), XT[:, c, :], UA[:, c, :, :].rearrange("p a b -> p (a b)"), start=True, stop=True)
                S.done(last, "qp")
                fill("qp")
                pe.wait_ge(vm.sem, vm.at("qp2", i))
                pe.wait_ge(am.sem, am.at("qp1", i))
                for c in range(1, NCH):
                    last = mm(bank(2, c * CH, c * CH + CH), QPb[:, c, 1, :], RBK[:, c, 0, :], start=True, stop=True)
                S.done(last, "g_")
                for c in (1, 2):
                    last = mm(bank(5, (c - 1) * P, c * P), QPb[:, c, 1, :], btok[:, c, :], start=True, stop=True)
                S.done(last, "et")
                pe.wait_ge(gm.sem, gm.at("csq", i))
                S.done(mm(bank(1, 0, T), bmean, csq, start=True, stop=True), "conv")
                for c in range(3):
                    mm(bank(4, c * P, c * P + P), btok[:, c, :], QPb[:, c, 0, :], start=True, stop=False)
                    last = mm(bank(4, c * P, c * P + P), ktok[:, c, :], vtok[:, c, :], start=False, stop=True)
                S.done(last, "f")
                fill("f")
                pe.wait_ge(am.sem, am.at("f2", i))
                pe.wait_ge(vm.sem, vm.at("et", i))
                S.done(mm(bank(3, 0, P), ET[:, 0, :], Fw[:, 0, :], start=True, stop=True), "s2")
                fill("s2")
                pe.wait_ge(vm.sem, vm.at("s2", i))
                S.done(mm(bank(3, P, 2 * P), ET[:, 1, :], St[:, 0, :], start=True, stop=True), "s3")
                fill("s3")
                pe.wait_ge(vm.sem, vm.at("s3", i))
                for c in range(NCH):
                    o = bank(5, c * CH, c * CH + CH)
                    if c:
                        mm(o, Fw[:, 0, :] if c == 1 else St[:, c - 2, :], Gt[:, c * CH:(c + 1) * CH], start=True, stop=False)
                    mm(o, QPb[:, c, 0, :], RBK[:, c, 0, :], start=(c == 0), stop=False)
                    last = mm(o, vtok[:, c, :], RBK[:, c, 1, :], start=False, stop=True)
                S.done(last, "y")
                if par and not last_round:
                    pe.wait_ge(ada_used, i * 8 + 8)
                    turn_half(0)
                fill("y")
                pe.wait_ge(am.sem, am.at("y", i))
                S.done(mm(bank(4, 0, T), bmean, y, start=True, stop=True), "mean")
                if not last_round:
                    pe.wait_ge(am.sem, am.at("lnc", i))
                    next_a(i + 1)
                fill("wa")
                pe.wait_ge(gm.sem, gm.at("sqy", i))
                S.done(mm(bank(5, 0, T), bmean, y, start=True, stop=True), "var")
                if not last_round:
                    next_b(i + 1)
                if par and not last_round:
                    pe.wait_ge(mod_red, i + 2)
                    turn_half(1)
                fill("end")

            next_a(0, first=True)
            next_b(0)
            for m in range(LORA + 3, LORA + 6):
                whole(m)
            with pe.Fori(0, 3) as it:
                for half in range(2):
                    pe_round(it * 2 + half, half, False)
            pe_round(6, 0, False)
            pe_round(7, 1, True)

            def groups(g, b0):
                for j in range(TILES):
                    m = WOUT + 16 + 4 * g + j
                    pe.wait_ge(land[m % WSLOTS], 16 * (m // WSLOTS + 2))
                    w = ring[:, m % WSLOTS, :].rearrange("p (a b) -> p a b", a=KT)
                    for kk in range(KT):
                        k = j * KT + kk
                        if g == 0:
                            e, n = (a2, max(k, 1)) if k in ACT_K else (v2, max(k, 3))
                            if k == 0:
                                pe.wait_ge(v2.sem, v2.at("h3"))
                            pe.wait_ge(e.sem, e.at(f"h{n}"))
                        for s in range(4):
                            last = mm(bank(b0 + s // 2, (s % 2) * T, (s % 2) * T + T), w[:, kk, s * P:(s + 1) * P], h2T[:, k, :],
                                      start=(k == 0 and s % 2 == 0), stop=(k == KC - 1), skip_group_check=True)
                    last.then_inc(w_used, 1)
                    if g and j == 0:
                        score(g - 1)

            def rows(col, b0):
                for k in range(KC):
                    last = mm(bank(b0 + k // 4, k % 4 * P, k % 4 * P + P), col[:, k:k + 1].broadcast_to([P, P]), ident, start=True, stop=True)
                return last
            pe.wait_ge(vm.sem, PAIRS * vm.per)
            pe.wait_ge(am.sem, PAIRS * am.per)
            for n in range(OUT_AT["end"], KC):
                out_chunk(0, n)
            pe.wait_ge(v2.sem, v2.at("ga1"))
            p2.done(rows(gcol[:, 0, :], 2), "gate1")
            for g in range(1, 4):
                if g == 2:
                    pe.wait_ge(a2.sem, a2.at("gw1"))
                if g == 3:
                    pe.wait_ge(m_out, 4)
                for n in range(KC):
                    out_chunk(g, n)
            pe.wait_ge(ada_used, NADA)
            columns(acc, 4, 0).then_inc(mod_sum, 1)
            pe.wait_ge(m_out, 8)
            pe.wait_ge(v2.sem, v2.at("m5"))
            for b in range(TB):
                pe.wait_ge(v2.sem, v2.at(f"xn{b}"))
                for k in range(KC):
                    last = nc.tensor.transpose(bank(k // 2, k % 2 * T + b * P, k % 2 * T + b * P + P), mixrow[:, b, k * P:(k + 1) * P], ident)
                    if b == TB - 1 and k % 2:
                        p2.done(last, f"tr{k - 1}")

            def score(g):
                pe.wait_ge(q_out, 2 * (g + 1))
                if g == 0:
                    pe.wait_ge(keys_in, 16)
                    pe.wait_ge(a2.sem, a2.at("rows"))
                for b in range(TB):
                    if g >= 2:
                        pe.wait_ge(sc_out, 2 * (g - 2) + b + 1)
                    for c in range(4 * g, 4 * g + 4):
                        last = mm(bank(4 + 2 * (g % 2) + b, (c % 4) * P, (c % 4) * P + P), qT[:, c, b * P:(b + 1) * P], kv[:, c, :], start=True, stop=True)
                    last.then_inc(sc_ps, 1)

            def h_rows(b, at=0):
                for k in range(KC):
                    last = nc.tensor.transpose(ps[:, at + k * P:at + (k + 1) * P], h2T[:, k, b * P:(b + 1) * P], ident)
                return last

            for g in range(4):
                if g >= 2:
                    pe.wait_ge(q_out, 2 * (g - 1))
                groups(g, 2 * (g % 2))
                if g == 0:
                    p2.done(h_rows(0, 2048), "rows")
                if g == 3:
                    pe.wait_ge(q_out, 8)
                    h_rows(0).then_inc(h_ps, 1)
                    score(g)
            pe.wait_ge(sc_out, 2 * 4)
            p2.done(rows(gcol[:, 1, :], 4), "gate2")
            pe.wait_ge(used, ROWS + KTOP)
            h_rows(1).then_inc(h_ps, 1)

        @block.vector
        def _(dve):
            V = nc.vector
            tt, ts, stt = V.tensor_tensor, V.tensor_scalar, V.scalar_tensor_tensor
            dve.wait_ge(a0.sem, a0.at("expc"))
            v0.done(ts(tmp16, tmp16, 1.0, None, ALU.add), "den")
            dve.wait_ge(v0.sem, v0.at("den"))
            v0.done(V.reciprocal(tmp16, tmp16), "rec")
            dve.wait_ge(v0.sem, v0.at("rec"))
            v0.done(tt(silu_c, tmp16, colp[:, C_C:C_C + KC], ALU.mult), "silu")
            dve.wait_ge(v0.sem, v0.at("silu"))

            def ada_tile(dst, slot, k):
                if k == 0:
                    ins = ts(dst, ring[:, slot, :], silu_c[:, 0:1], None, ALU.mult)
                else:
                    ins = stt(dst, ring[:, slot, :], silu_c[:, k:k + 1], dst, ALU.mult, ALU.add)
                ins.then_inc(ada_used, 1)

            def early_sum(q, first, second):
                tile, landed = early_tile(q)
                dve.wait_ge(landed, 16 * (q // ADA_SLOTS + 1))
                t3 = tile.rearrange("p (a b) -> p a b", a=KC)
                v0.done(tt(t3, t3, silu_c.rearrange("p (a b) -> p a b", b=1).broadcast_to([P, KC, P]), ALU.mult), first)
                dve.wait_ge(v0.sem, v0.at(first))
                v0.done(V.tensor_reduce(red[:, q // 2 % 2, q % 2, :], t3.rearrange("p a b -> p b a"), AX.X, ALU.add), second)

            for k in range(KC + 1):
                if k < KC:
                    early_sum(2 * k, f"a{k}", f"r{k}")
                if k in VEC_SHIFT:
                    early_sum(2 * k + 1, f"b{k}", f"q{k}")
                if k == 0:
                    dve.wait_ge(a0.sem, a0.at("exp"))
                    for b in range(TB):
                        v0.done(ts(xn[:, b, :], xn[:, b, :], rstd[:, b:b + 1], None, ALU.mult), f"xn{b}")
                    continue
                n = k - 1
                b = 6 + n % 2
                dve.wait_ge(p0.sem, p0.at(f"c{n}"))
                v0.done(tt(modc[:, 0, n:n + 1], bank(b, 0, 1), colp[:, C_AB + n:C_AB + n + 1], ALU.add), f"m{n}")
                dve.wait_ge(v0.sem, v0.at(f"m{n}"))
                v0.done(stt(s1c[:, n:n + 1], modc[:, 0, n:n + 1], 1.0, colp[:, C_PMW + n:C_PMW + n + 1], ALU.add, ALU.mult), f"s{n}")
                v0.done(tt(modc[:, 1, n:n + 1], bank(b, 1, 2), colp[:, C_AB + KC + n:C_AB + KC + n + 1], ALU.add), f"n{n}")
            v0.done(V.memset(z[:, :, 0:1], 0.0), "zero")
            for n in range(LORA):
                dve.wait_ge(z_out, n + 1)
                if n == 0:
                    V.memset(zl[:, :, 0:1], 0.0).then_inc(zl_zero, 1)
                    dve.wait_ge(zl_zero, 1)
                v0.done(tt(dl[:, n, :], zl[:, n, 0:T], zl[:, n, 1:ZS], ALU.subtract), f"dl{n}")
            for n in range(LORA):
                dve.wait_ge(v0.sem, v0.at(f"dl{n}"))
                v0.done(stt(ml[:, n, :], dl[:, n, :], colp[:, C_ML + n:C_ML + n + 1], zl[:, n, 1:ZS], ALU.mult, ALU.add), f"ml{n}")
            dve.wait_ge(a0.sem, a0.at("eg"))
            v0.done(ts(sgz[:, :, :], sgz[:, :, :], 1.0, None, ALU.add), "eg1")
            dve.wait_ge(v0.sem, v0.at("eg1"))
            v0.done(V.reciprocal(sgz[:, :, :], sgz[:, :, :]), "sg")
            v0.done(V.memset(reset, 1.0), "res1")
            dve.wait_ge(v0.sem, v0.at("res1"))
            v0.done(V.memset(reset.rearrange("p (c t) -> p c t", c=NCH)[:, :, 0:1], 0.0), "reset")
            dve.sem_inc(mod_red, 2)
            dve.wait_ge(zeroed, 5)
            chunked = lambda v: v.rearrange("p (c t) -> p c t", c=NCH)
            flat = lambda v: v.rearrange("p a b -> p (a b)")
            over = lambda v: v.rearrange("p (a b) -> p a b", a=1).broadcast_to([P, NCH, P])

            def next_a(j, par):
                p_ = pp[par]
                vn.done(V.tensor_copy(p_, colp[:, bass.ds(j * PC + C_PP, PC)] if not isinstance(j, int)
                                      else colp[:, C_PP + j * PC:C_PP + (j + 1) * PC]), "pp")
                dve.wait_ge(vn.sem, vn.at("pp", j))
                vn.done(ts(npp, p_, -1.0, None, ALU.mult), "npp")
                for n, (name, src, d, mx, o) in enumerate((("zr", "dr", dr, MIX_R, zr), ("zk", "dk", dk, MIX_K, zk), ("zv", "dv", dv, MIX_V, zv))):
                    dve.wait_ge(gn.sem, gn.at(src, j))
                    vn.done(stt(o, d, p_[:, mx:mx + 1], z[:, n, 1:ZS], ALU.mult, ALU.add), name)
                dve.wait_ge(vn.sem, vn.at("zk", j))
                vn.done(ts(kkr, zk, p_[:, K_K:K_K + 1], None, ALU.mult), "kkr")

            def next_b(j):
                dve.wait_ge(an.sem, an.at("ea", j))
                vn.done(ts(flat(ewa), flat(ewa), 1.0, None, ALU.add), "den")
                dve.wait_ge(vn.sem, vn.at("den", j))
                vn.done(V.reciprocal(flat(ewa), flat(ewa)), "sig")
                dve.wait_ge(vn.sem, vn.at("sig", j))
                vn.done(V.tensor_tensor_scan(cs, reset, ewa[:, 0, :], 0.0, ALU.mult, ALU.add), "cs")
                dve.wait_ge(vn.sem, vn.at("cs", j))
                vn.done(tt(cse, cs, ewa[:, 0, :], ALU.subtract), "cse")

            def next_c(j, par):
                p_ = pp[par]
                dve.wait_ge(an.sem, an.at("rn", j))
                vn.done(tt(kk, kkr, rn, ALU.mult), "kk")
                dve.wait_ge(vn.sem, vn.at("kk", j))
                vn.done(tt(kka, kk, ewa[:, 1, :], ALU.mult), "kka")
                vn.done(ts(t1, ewa[:, 1, :], -1.0, p_[:, K_A:K_A + 1], ALU.add, ALU.mult), "t1")
                dve.wait_ge(vn.sem, vn.at("t1", j))
                vn.done(stt(kf, t1, 1.0, zk, ALU.add, ALU.mult), "kf")
                for h in range(2):
                    r = slice(h * 64, h * 64 + 64)
                    vn.done(stt(ab[r, :, r], chunked(kk)[r], -1.0, chunked(We)[r], ALU.mult, ALU.mult), f"ab{h}")
                for h in range(2):
                    r = slice(h * 64, h * 64 + 64)
                    vn.done(tt(bb[r, :, r], chunked(kka)[r], chunked(Wi)[r], ALU.mult), f"bb{h}")
                dve.wait_ge(vn.sem, vn.at("kf", j))
                vn.done(stt(rk, zr, p_[:, R_K:R_K + 1], kf, ALU.mult, ALU.mult), "rk")

            def reduce_half(h, i):
                dve.wait_ge(mod_sum, i + h)
                V.tensor_reduce(modt[:, h * KC // 2:(h + 1) * KC // 2], ps[:, 1024:2048].rearrange("p (a b) -> p a b", b=P),
                                AX.X, ALU.add).then_inc(mod_red, 1)

            def vec_round(i, par, last):
                S = vm
                p_ = pp[par]
                here = lambda n: S.at(n, i)
                tile = [0]

                def modulation():
                    n = tile[0]
                    k = 8 * par + n
                    dve.wait_ge(land[WSLOTS + n % 2], i * 64 + 16 * (A_BASE + n // 2 + 1))
                    if k:
                        dve.wait_ge(ada_used, i * 8 + n)
                    ada_tile(acc, WSLOTS + n % 2, k)
                    tile[0] += 1

                dve.wait_ge(pm.sem, pm.at("l", i))
                S.done(tt(X[:, :, :], bank3(3, NCH), over(m0T), ALU.mult), "X0a")
                dve.wait_ge(S.sem, here("X0a"))
                S.done(tt(X[:, :, :], X[:, :, :], over(ident), ALU.add), "X0")
                dve.wait_ge(pm.sem, pm.at("akt", i))
                S.done(tt(AKT[:, :, :], bank3(4, NCH), over(strict), ALU.mult), "akt")
                dve.wait_ge(pm.sem, pm.at("rbk", i))
                S.done(tt(RBK.rearrange("p a b c -> p (a b) c"), bank3(5, 2 * NCH),
                          incl.rearrange("p (a b) -> p a b", a=1).broadcast_to([P, 2 * NCH, CH]), ALU.mult), "rbk")
                modulation()
                dve.wait_ge(pm.sem, pm.at("bon", i))
                S.done(tt(bon, bank(0, 0, T), zv, ALU.mult), "bon")
                for m in range(1, LEVELS):
                    dve.wait_ge(pm.sem, pm.at(f"X{m}", i))
                    if m < LEVELS - 1:
                        S.done(tt(flat(X), bank(3), flat(X), ALU.add), f"X{m}")
                    if m == 1:
                        dve.wait_ge(gm.sem, gm.at("XT0", i))
                    S.done(tt(flat(XT), bank(4), flat(XT), ALU.add), f"XT{m}")
                    if m == 1:
                        dve.wait_ge(gm.sem, gm.at("u", i))
                        S.done(ts(cy, u[:, 0:T], p_[:, CW0:CW0 + 1], None, ALU.mult), "c0")
                    if m in (2, 3):
                        dve.wait_ge(S.sem, here(f"c{m - 2}"))
                        S.done(stt(cy, u[:, m - 1:m - 1 + T], p_[:, CW0 + m - 1:CW0 + m], cy, ALU.mult, ALU.add), f"c{m - 1}")
                    modulation()
                dve.wait_ge(pm.sem, pm.at("qp", i))
                S.done(V.tensor_copy(QPb[:, 2:4, :, :].rearrange("p a b c -> p (a b c)"), bank(1)), "qp2")
                dve.wait_ge(pm.sem, pm.at("et", i))
                S.done(tt(ET[:, :, :], bank(5, 0, 2 * P).rearrange("p (a b) -> p a b", a=2),
                          ident.rearrange("p (a b) -> p a b", a=1).broadcast_to([P, 2, P]), ALU.add), "et")
                S.done(tt(Gt[:, CH:], bank(2, CH, T), rt[:, CH:], ALU.add), "g")
                modulation()
                for c, name in ((1, "s2"), (2, "s3")):
                    dve.wait_ge(pm.sem, pm.at(name, i))
                    w = (c + 1) * CH - 1
                    S.done(stt(St[:, c - 1, :], bank(3, (c - 1) * P, c * P), Wt[:, w:w + 1], Fw[:, c, :], ALU.mult, ALU.add), name)
                modulation()
                assert tile[0] == 8
                if not last:
                    next_a(i + 1, 1 - par)
                dve.wait_ge(pm.sem, pm.at("mean", i))
                S.done(tt(yc, y, bank(4, 0, T), ALU.subtract), "yc")
                if par and not last:
                    reduce_half(0, i)
                if not last:
                    next_b(i + 1)
                dve.wait_ge(am.sem, am.at("rsy", i))
                S.done(tt(yc, yc, rsy, ALU.mult), "yn")
                dve.wait_ge(S.sem, here("yn"))
                S.done(ts(yc, yc, p_[:, LN_W:LN_W + 1], p_[:, LN_B:LN_B + 1], ALU.mult, ALU.add), "aff")
                dve.wait_ge(S.sem, here("aff"))
                S.done(tt(yc, yc, bon, ALU.add), "addb")
                dve.wait_ge(S.sem, here("addb"))
                chunk = (lambda n: yT[:, n, :] if isinstance(n, int) else yT[:, bass.ds(n, 1), :].rearrange("p a b -> p (a b)"))
                S.done(tt(chunk(i), yc, gT[par], ALU.mult), "yg")
                S.done(stt(chunk(i + PAIRS), cy, p_[:, CN:CN + 1], crs, ALU.mult, ALU.mult), "cout")
                if par and not last:
                    reduce_half(1, i)
                    dve.wait_ge(mod_red, i + 3)
                    V.tensor_copy(mod_row(i), modt).then_inc(mod_out, 1)
                if not last:
                    next_c(i + 1, 1 - par)

            next_a(0, 0)
            next_b(0)
            next_c(0, 0)
            with dve.Fori(0, 3) as it:
                mod_row = lambda i: modc[:, bass.ds(it + 2, 1), :].rearrange("p a b -> p (a b)")
                for half in range(2):
                    vec_round(it * 2 + half, half, False)
            vec_round(6, 0, False)
            vec_round(7, 1, True)
            dve.wait_ge(mod_out, 3)
            v2.done(tt(flat(modc[:, 2:5, :]), flat(modc[:, 2:5, :]), colp[:, C_AB + 2 * KC:C_AB + 5 * KC], ALU.add), "s2a")
            dve.wait_ge(v2.sem, v2.at("s2a"))
            v2.done(stt(s2c, modc[:, 4, :], 1.0, colp[:, C_PFW:C_PFW + KC], ALU.add, ALU.mult), "s2")
            v2.done(tt(gcol[:, 0, :], modc[:, 2, :], colp[:, C_PG1:C_PG1 + KC], ALU.mult), "ga1")
            dve.wait_ge(a2.sem, a2.at("gw1"))
            for g in range(4):
                c = slice(g * GROUP, (g + 1) * GROUP)
                for b in range(TB):
                    dve.wait_ge(m_sq, 2 * g + b + 1)
                    tt(mixrow[:, b, c], bank(OUT_BANKS[g][b]), gw1[:, c], ALU.mult).then_inc(m_out, 1)
            for b in range(TB):
                v2.done(V.tensor_reduce(ss[:, 8 + b:9 + b], ss[:, 4 * b:4 * b + 4], AX.X, ALU.add), f"sq{b}")
            dve.wait_ge(a2.sem, a2.at("exp"))
            dve.wait_ge(x_in, 32)
            dve.wait_ge(m_out, 8)
            for b in range(TB):
                v2.done(stt(xs[:, b, :], mixrow[:, b, :], rstd[:, 2 + b:3 + b], xs[:, b, :], ALU.mult, ALU.add), f"mx{b}")
            dve.wait_ge(mod_sum, 7)
            v2.done(tt(modc[:, 5, :], bank(4, 0, KC), colp[:, C_AB + 5 * KC:C_AB + 6 * KC], ALU.add), "m5")
            dve.wait_ge(v2.sem, v2.at("m5"))
            v2.done(tt(gcol[:, 1, :], modc[:, 5, :], colp[:, C_PG2:C_PG2 + KC], ALU.mult), "ga2")
            for b in range(TB):
                dve.wait_ge(a2.sem, a2.at(f"exp{b}"))
                v2.done(ts(mixrow[:, b, :], xs[:, b, :], rstd[:, 4 + b:5 + b], None, ALU.mult), f"xn{b}")
            for k in VEC_K:
                dve.wait_ge(p2.sem, p2.at(f"tr{k - k % 2}"))
                v2.done(ts(h2T[:, k, :], bank(k // 2, k % 2 * T, k % 2 * T + T), s2c[:, k:k + 1], modc[:, 3, k:k + 1], ALU.mult, ALU.add), f"h{k}")
            nr = [0]

            def r(ins):
                nr[0] += 1
                return ins.then_inc(vr, 1)

            def settle():
                dve.wait_ge(vr, nr[0])

            for n in range(TOPK):
                r(V.memset(iota16[:, n:n + 1], float(n)))
            NEG = -3.0e38

            def top16(src, vals, where, rep):
                r(V.max(vals[:, 0:8], src))
                settle()
                r(V.max_index(where[:, 0:8], vals[:, 0:8], src))
                r(V.match_replace(rep, vals[:, 0:8], src, NEG))
                settle()
                r(V.max(vals[:, 8:16], rep))
                settle()
                r(V.max_index(where[:, 8:16], vals[:, 8:16], rep))

            def route(b, g):
                dve.wait_ge(sc_out, 2 * g + b + 1)
                for c in range(4):
                    top16(scores[b][:, 4 * g + c, :], v16[:, c, :], u32(iu[:, c, :]), repl[:, c * NKEYS:(c + 1) * NKEYS])
                settle()
                r(V.tensor_copy(i16[:, :, :], u32(iu[:, :, :])))
                wide = lambda v: v.rearrange("p (a b) -> p a b", b=1).broadcast_to([P, TOPK, TOPK])
                deep = lambda v: v.rearrange("p (a b) -> p a b", a=1).broadcast_to([P, TOPK, TOPK])
                for h in range(2):
                    r(tt(cand[:, h, :].rearrange("p (a b) -> p a b", a=TOPK), wide(v16[:, 2 * h, :]), deep(v16[:, 2 * h + 1, :]), ALU.add))
                settle()
                for h in range(2):
                    top16(cand[:, h, :], topv[:, h, :], u32(pos[:, h, :]), repl[:, h * 256:(h + 1) * 256])
                settle()
                r(ts(u32(hi_u[:, :, :]), u32(pos[:, :, :]), 4, None, ALU.logical_shift_right))
                r(ts(u32(lo_u[:, :, :]), u32(pos[:, :, :]), 15, None, ALU.bitwise_and))
                settle()
                r(V.tensor_copy(hi_f[:, :, :], u32(hi_u[:, :, :])))
                r(V.tensor_copy(lo_f[:, :, :], u32(lo_u[:, :, :])))
                settle()
                gb = gate[:, b, g * 2 * TOPK:(g + 1) * 2 * TOPK].rearrange("p (h k) -> p h k", h=2)
                r(tt(gb, topv[:, :, :], topv[:, :, 0:1].broadcast_to([P, 2, TOPK]), ALU.subtract))
                gates.append(nr[0])
                for half, sel, dst in ((0, hi_f, ei), (1, lo_f, ej)):
                    for h in range(2):
                        r(tt(eq[:, h * TOPK:(h + 1) * TOPK, :], wide(sel[:, h, :]), deep(iota16), ALU.is_equal))
                    settle()
                    for h in range(2):
                        e = eq[:, h * TOPK:(h + 1) * TOPK, :]
                        r(tt(e, e, deep(i16[:, 2 * h + half, :]), ALU.mult))
                    settle()
                    r(V.tensor_reduce(dst.rearrange("p a b -> p (a b)"), eq[:, :, :], AX.X, ALU.add))
                    settle()
                r(stt(ei[:, :, :], ei[:, :, :], float(NKEYS), ej[:, :, :], ALU.mult, ALU.add))
                settle()
                for again in range(2):
                    at = (2 * b + again) * KTOP + g * 2 * TOPK
                    r(V.tensor_copy(i32(idx[:, at:at + 2 * TOPK]), ei.rearrange("p a b -> p (a b)")))
                picked.append(nr[0])

            gates, picked = [], []
            r(V.memset(i32(idx[:, 4 * KTOP:4 * KTOP + 2]), 0))
            def gate_sums(b):
                dve.wait_ge(ar, 4 * (b + 1))
                gb = gate[:, b, :].rearrange("p (h k) -> p h k", h=HEADS)
                r(V.tensor_reduce(gsum, gb, AX.X, ALU.add))
                settle()
                r(V.reciprocal(grec, gsum))
                settle()
                r(tt(gb, gb, grec.rearrange("p (a b) -> p a b", b=1).broadcast_to([P, HEADS, TOPK]), ALU.mult))
                settle()

            def each_row(ph, lo, hi, work):
                def body(base, count, t):
                    for j in range(count):
                        n = ph * KTOP + base + j
                        s, count_of = row_place(n)
                        dve.wait_ge(gland[s], t * (16 * LOOP // ROWS) + 16 * count_of)
                        work(row_slot[s], base + j, t)

                loops = (hi - lo) // LOOP
                if loops:
                    with dve.Fori(0, loops) as t:
                        body(lo, LOOP, t)
                body(lo + loops * LOOP, hi - lo - loops * LOOP, 0)

            def column(v, k, t):
                return v[:, k:k + 1] if isinstance(t, int) else v[:, bass.ds(t * LOOP + k, 1)]

            def dots(b, lo, hi, h=ps[:, 0:D]):
                def work(row, k, t):
                    stt(row, row, 1.0, h, ALU.mult, ALU.mult, accum_out=column(actv[:, b, :], k, t)).then_inc(used, 1)
                each_row(2 * b, lo, hi, work)

            def sums(b, lo, hi):
                def work(row, k, t):
                    dve.wait_ge(used, t * LOOP + (ROWS + (2 * b + 1) * KTOP + k))
                    stt(ps[:, 2048:4096], row, column(wv[:, b, :], k, t), ps[:, 2048:4096], ALU.mult, ALU.add).then_inc(used, 1)
                each_row(2 * b + 1, lo, hi, work)

            for b in range(TB):
                if b == 0:
                    route(0, 0)
                    dve.wait_ge(a2.sem, a2.at("rows"))
                    dots(0, 0, 4, h=junk)
                    route(0, 1)
                    dots(0, 4, 10, h=junk)
                    route(0, 2)
                    dots(0, 10, 10 + LOOP, h=junk)
                    route(0, 3)
                dve.wait_ge(h_ps, b + 1)
                if b == 0:
                    dots(0, 10 + LOOP, 10 + 2 * LOOP)
                    route(1, 0)
                    dots(0, 10 + 2 * LOOP, 10 + 4 * LOOP)
                    route(1, 1)
                    dots(0, 10 + 4 * LOOP, KTOP)
                else:
                    dots(1, 0, KTOP)
                gate_sums(b)
                dve.wait_ge(gelu_done, b + 1)
                tt(wv[:, b, :], wv[:, b, :], gate[:, b, :], ALU.mult).then_inc(wv_done, 1)
                if b == 0:
                    dve.wait_ge(a2.sem, a2.at("gw2"))
                V.memset(ps[:, 2048:4096], 0.0).then_inc(wv_done, 1)
                dve.wait_ge(wv_done, 2 * b + 2)
                if b == 0:
                    sums(0, 0, LOOP)
                    route(1, 2)
                    sums(0, LOOP, 3 * LOOP)
                    route(1, 3)
                    sums(0, 3 * LOOP, KTOP)
                    assert tuple(gates) == GATE_AT and tuple(picked) == IDX_AT, (gates, picked)
                else:
                    sums(1, 0, KTOP)
                dve.wait_ge(fin_a, 3 * b + 3)
                for h in range(2):
                    c = slice(h * D // 2, (h + 1) * D // 2)
                    stt(ff[:, c], ps[:, 2048 + h * D // 2:2048 + (h + 1) * D // 2], rstd[:, 12 + b:13 + b], gw2[:, c], ALU.mult, ALU.mult).then_inc(fin_v, 1)
                    dve.wait_ge(fin_v, 4 * b + 2 * h + 1)
                    tt(xs[:, b, c], xs[:, b, c], ff[:, c], ALU.add).then_inc(fin_v, 1)


NCONST = 40
WOUT = LORA + 6 * PAIRS
FILL_AT = dict(atr=1, ktr=2, T1_1=3, X1=4, T1_2=5, X2=6, T1_3=7, X3=8, T1_4=9, X4=10, T1_5=11, X5=12,
               qp=13, f=14, s2=15, s3=16, y=17, wa=19, end=24)
OUT_AT = dict(atr=0, ktr=0, T1_1=1, X1=2, T1_2=3, X2=4, T1_3=5, X3=6, T1_4=7, X4=8, T1_5=9, X5=10,
              qp=10, f=11, s2=12, s3=12, y=12, wa=13, end=14)
TILES_AT = {"T1_1": 0, "T1_2": 1, "T1_3": 1, "T1_4": 2, "T1_5": 2, "qp": 3, "f": 3, "y": 4, "wa": 4, "end": 6}
LAST = WOUT + 32
ROWS = 12
FREE = 6
LOOP = 2 * ROWS
GATE_AT = (55, 106, 157, 208, 259, 310, 364, 415)
IDX_AT = (68, 119, 170, 221, 272, 323, 377, 428)


def kernel(x, c, ada_w, ada_b, pre_mix_w, post_mix_w, w_in, rwkv_mix, w0, w_up, a0, a_up, g_up, k_k, k_a, r_k,
           ln_x_w, ln_x_b, conv_w, conv_norm_w, w_out, pre_ffn_w, post_ffn_w, w_q, sub_keys_1, sub_keys_2,
           expert_u, expert_v):
    import concourse.bacc as bacc
    from concourse.bass_utils import run_bass_kernel_spmd as run

    f = lambda a: np.asarray(a)
    as_cols = lambda v: v.reshape(-1, P).T
    RW = 1024
    lora0 = 3 * RW
    wi = f(w_in)[0]
    ab = f(ada_b)[0].reshape(VECS, D)
    mix = f(rwkv_mix)[0]
    lmix = np.zeros(384, np.float32)
    lmix[:288] = mix[lora0:lora0 + 288]
    per = [mix[0:RW], mix[RW:2 * RW], mix[2 * RW:3 * RW], f(w0)[0], f(a0)[0], f(k_k)[0], f(k_a)[0], f(r_k)[0].reshape(-1),
           f(ln_x_w)[0], f(ln_x_b)[0], f(conv_w)[0, 0], f(conv_w)[0, 1], f(conv_w)[0, 2], f(conv_norm_w)[0],
           np.zeros(RW, np.float32), np.zeros(RW, np.float32)]
    pp = np.stack([as_cols(v) for v in per], 2).reshape(P, PAIRS * PC)
    cols = np.concatenate([as_cols(f(pre_mix_w)[0]), as_cols(f(pre_ffn_w)[0]), as_cols(f(post_mix_w)[0]), as_cols(f(post_ffn_w)[0]),
                           *(as_cols(ab[v]) for v in VEC_ORDER), as_cols(f(c)[0]), as_cols(lmix), np.zeros((P, 1), np.float32), pp], 1)
    ada = f(ada_w)[0].reshape(KC, P, VECS, D).transpose(2, 0, 1, 3)[list(VEC_ORDER)]
    ada = np.concatenate([ada[:2].reshape(2, KC, P, KC, P).transpose(3, 0, 2, 1, 4).reshape(2 * KC, P, D),
                          ada[2:].reshape((VECS - 2) * KC, P, D)])

    def tiles(w, width, order=tuple(range(KC))):
        n = w.shape[1] // width
        return w.reshape(KC, P, n, width)[list(order)].reshape(TILES, KT, P, n, width).transpose(3, 0, 2, 1, 4).reshape(n * TILES, P, KT * width)

    lw = np.zeros((D, 384), np.float32)
    lw[:, :288] = wi[:, lora0:lora0 + 288]
    six = np.concatenate([wi[:, :lora0], wi[:, lora0 + 288:]], 1).reshape(D, 6, PAIRS, P).transpose(0, 2, 1, 3).reshape(D, 6 * PAIRS * P)
    w_main = np.concatenate([lw, six], 1).reshape(KC, P, WOUT, P).transpose(2, 1, 0, 3).reshape(WOUT, P, KC * P)
    up = np.zeros((4, P, RW), np.float32)
    up[0, 0:64] = f(w_up)[0]
    up[1, 64:P] = f(a_up)[0]
    up[2] = f(g_up)[0, 0:P]
    up[3, 0:32] = f(g_up)[0, P:]
    lora_up = up.reshape(4, P, PAIRS, P).transpose(2, 1, 0, 3).reshape(PAIRS, P, 4 * P)
    keys = np.stack([f(sub_keys_1)[0], f(sub_keys_2)[0]], 1).reshape(KC, NKEYS, P).transpose(2, 0, 1).reshape(P, KC * NKEYS)
    arrays = {
        "x": f(x)[0], "cols": cols, "ada": ada, "w_in": w_main,
        "w_tail": np.concatenate([tiles(f(w_out)[0], GROUP, OUT_K), tiles(f(w_q)[0], GROUP)]),
        "lora_up": lora_up, "keys": keys, "expert_u": f(expert_u)[0], "expert_v": f(expert_v)[0],
    }
    nc = bacc.Bacc("TRN2", target_bir_lowering=False, num_devices=1)
    ins, aps = {}, []
    for name, a in arrays.items():
        ins["in_" + name] = np.ascontiguousarray(a)
        aps.append(nc.dram_tensor("in_" + name, a.shape, F32, kind="ExternalInput").ap())
    out = nc.dram_tensor("out_0", (T, D), F32, kind="ExternalOutput").ap()
    build_layer(nc, *aps, out)
    r = run(nc, [ins], core_ids=[0])
    return r.results[0]["out_0"].reshape(1, T, D)
```
